# Optimizing a Trainium2 kernel written in Bass

```python
import math
import jax, jax.numpy as jnp
from jax import lax
import numpy as np

D_MODEL = 1024
BATCH = 1
SEQ = 512
DEPTH = 2

ATTN_HEADS = 16
ATTN_KV_HEADS = 4
ATTN_GROUP = ATTN_HEADS // ATTN_KV_HEADS
ATTN_HEAD_DIM = 64
ATTN_Q_DIM = ATTN_HEADS * ATTN_HEAD_DIM
ATTN_KV_DIM = ATTN_KV_HEADS * ATTN_HEAD_DIM
ATTN_IN_DIM = ATTN_Q_DIM + 2 * ATTN_KV_DIM
WINDOW = 128
ATTN_BLOCK = 128
ROPE_DIM = ATTN_HEAD_DIM // 4
ROPE_THETA = 500000.0

GDN_QK_HEADS = 8
GDN_V_HEADS = 16
GDN_HEAD_K = 128
GDN_HEAD_V = 128
GDN_CONV = 4
GDN_CHUNK = 64
GDN_KEY_DIM = GDN_QK_HEADS * GDN_HEAD_K
GDN_VAL_DIM = GDN_V_HEADS * GDN_HEAD_V
GDN_QKV_DIM = 2 * GDN_KEY_DIM + GDN_VAL_DIM
GDN_IN_DIM = GDN_QKV_DIM + GDN_VAL_DIM + 2 * GDN_V_HEADS

D_FF = 3 * D_MODEL
FFN_CONV = 3

N_ATTN_LAYERS = (DEPTH + 1) // 2
N_GDN_LAYERS = DEPTH // 2
EPS = 1e-6


def rms_norm(x, gain):
    xf = x.astype(jnp.float32)
    y = xf * lax.rsqrt(jnp.mean(xf * xf, axis=-1, keepdims=True) + EPS)
    return (y * gain.astype(jnp.float32)).astype(x.dtype)

def l2_norm(x):
    return x * lax.rsqrt(jnp.sum(x * x, axis=-1, keepdims=True) + EPS)

def causal_dwconv(x, w):
    k = w.shape[0]
    return lax.conv_general_dilated(
        x, w[:, None, :].astype(x.dtype), window_strides=(1,), padding=[(k - 1, 0)],
        dimension_numbers=("NWC", "WIO", "NWC"), feature_group_count=x.shape[-1])

def rope_tables(positions):
    inv_freq = ROPE_THETA ** (-jnp.arange(0, ROPE_DIM, 2, dtype=jnp.float32) / ROPE_DIM)
    ang = positions.astype(jnp.float32)[..., None] * inv_freq
    return jnp.cos(ang)[:, :, None, :], jnp.sin(ang)[:, :, None, :]

def partial_rope(x, cos, sin):
    cos = cos.astype(x.dtype)
    sin = sin.astype(x.dtype)
    half = ROPE_DIM // 2
    x1, x2, xp = x[..., :half], x[..., half:ROPE_DIM], x[..., ROPE_DIM:]
    return jnp.concatenate([x1 * cos - x2 * sin, x2 * cos + x1 * sin, xp], axis=-1)

def swa_sink_attention(u, w_in, q_gain, k_gain, sinks, w_out, cos, sin):
    B, S, _ = u.shape
    nb = S // ATTN_BLOCK
    blk, hkv, g, hd = ATTN_BLOCK, ATTN_KV_HEADS, ATTN_GROUP, ATTN_HEAD_DIM
    qkv = u @ w_in
    q = qkv[..., :ATTN_Q_DIM].reshape(B, S, ATTN_HEADS, hd)
    k = qkv[..., ATTN_Q_DIM:ATTN_Q_DIM + ATTN_KV_DIM].reshape(B, S, hkv, hd)
    v = qkv[..., ATTN_Q_DIM + ATTN_KV_DIM:].reshape(B, S, hkv, hd)
    q = partial_rope(rms_norm(q, q_gain), cos, sin)
    k = partial_rope(rms_norm(k, k_gain), cos, sin)
    qb = q.reshape(B, nb, blk, hkv, g, hd)

    def band(t):
        prev = jnp.pad(t, ((0, 0), (blk, 0), (0, 0), (0, 0)))[:, :S]
        return jnp.concatenate([prev.reshape(B, nb, blk, hkv, hd),
                                t.reshape(B, nb, blk, hkv, hd)], axis=2)

    kb, vb = band(k), band(v)
    scores = jnp.einsum("bnqhgd,bnkhd->bnhgqk", qb, kb,
                        preferred_element_type=jnp.float32) * (hd ** -0.5)
    dist = jnp.arange(blk)[:, None] + blk - jnp.arange(2 * blk)[None, :]
    in_window = (dist >= 0) & (dist < WINDOW)
    key_pos = jnp.arange(nb)[:, None] * blk - blk + jnp.arange(2 * blk)[None, :]
    mask = in_window[None] & (key_pos >= 0)[:, None, :]
    scores = jnp.where(mask[None, :, None, None], scores, jnp.finfo(jnp.float32).min)
    sink = jnp.broadcast_to(sinks.astype(jnp.float32).reshape(1, 1, hkv, g, 1, 1),
                            scores.shape[:-1] + (1,))
    probs = jax.nn.softmax(jnp.concatenate([scores, sink], axis=-1), axis=-1)[..., :-1]
    out = jnp.einsum("bnhgqk,bnkhd->bnqhgd", probs.astype(vb.dtype), vb)
    return out.reshape(B, S, ATTN_Q_DIM) @ w_out

def chunk_gated_delta_rule(q, k, v, g, beta):
    out_dtype = v.dtype
    B, S, H, DK = q.shape
    DV = v.shape[-1]
    C = GDN_CHUNK
    nc = S // C
    f32 = jnp.float32

    def chunks(t):
        t = t.astype(f32).reshape((B, nc, C, H) + t.shape[3:])
        return jnp.moveaxis(t, 3, 1)

    q, k, v, g, beta = chunks(q), chunks(k), chunks(v), chunks(g), chunks(beta)
    gc = jnp.cumsum(g, axis=-1)
    incl = jnp.tril(jnp.ones((C, C), dtype=bool))
    strict = jnp.tril(jnp.ones((C, C), dtype=bool), k=-1)
    decay = jnp.exp(jnp.where(incl, gc[..., :, None] - gc[..., None, :], -jnp.inf))
    kk = jnp.einsum("bhncd,bhnsd->bhncs", k, k)
    m = jnp.where(strict, beta[..., :, None] * kk * decay, 0.0)
    a = m + jnp.eye(C, dtype=f32)
    rhs = jnp.concatenate([v * beta[..., None], k * (beta * jnp.exp(gc))[..., None]], axis=-1)
    sol = lax.linalg.triangular_solve(a, rhs, left_side=True, lower=True, unit_diagonal=True)
    u, w = sol[..., :DV], sol[..., DV:]
    qk = jnp.where(incl, jnp.einsum("bhncd,bhnsd->bhncs", q, k) * decay, 0.0)
    q_dec = q * jnp.exp(gc)[..., None]
    k_dec = k * jnp.exp(gc[..., -1:] - gc)[..., None]
    g_last = jnp.exp(gc[..., -1])

    def step(state, inp):
        u_c, w_c, qk_c, qd_c, kd_c, gl_c = inp
        v_new = u_c - jnp.einsum("bhcd,bhde->bhce", w_c, state)
        o = jnp.einsum("bhcd,bhde->bhce", qd_c, state) + jnp.einsum("bhcs,bhse->bhce", qk_c, v_new)
        state = state * gl_c[..., None, None] + jnp.einsum("bhcd,bhce->bhde", kd_c, v_new)
        return state, o

    xs = tuple(jnp.moveaxis(t, 2, 0) for t in (u, w, qk, q_dec, k_dec, g_last))
    _, o = lax.scan(step, jnp.zeros((B, H, DK, DV), f32), xs)
    o = jnp.transpose(o, (1, 0, 3, 2, 4)).reshape(B, S, H, DV)
    return o.astype(out_dtype)

def gated_deltanet(u, w_in, conv_w, a_log, dt_bias, norm_gain, w_out):
    B, S, _ = u.shape
    proj = u @ w_in
    qkv = jax.nn.silu(causal_dwconv(proj[..., :GDN_QKV_DIM], conv_w))
    z = proj[..., GDN_QKV_DIM:GDN_QKV_DIM + GDN_VAL_DIM].reshape(B, S, GDN_V_HEADS, GDN_HEAD_V)
    b = proj[..., GDN_QKV_DIM + GDN_VAL_DIM:GDN_QKV_DIM + GDN_VAL_DIM + GDN_V_HEADS]
    a = proj[..., GDN_QKV_DIM + GDN_VAL_DIM + GDN_V_HEADS:]
    rep = GDN_V_HEADS // GDN_QK_HEADS
    q = qkv[..., :GDN_KEY_DIM].reshape(B, S, GDN_QK_HEADS, GDN_HEAD_K).astype(jnp.float32)
    k = qkv[..., GDN_KEY_DIM:2 * GDN_KEY_DIM].reshape(B, S, GDN_QK_HEADS, GDN_HEAD_K).astype(jnp.float32)
    v = qkv[..., 2 * GDN_KEY_DIM:].reshape(B, S, GDN_V_HEADS, GDN_HEAD_V)
    q = jnp.repeat(l2_norm(q) * (GDN_HEAD_K ** -0.5), rep, axis=2)
    k = jnp.repeat(l2_norm(k), rep, axis=2)
    beta = jax.nn.sigmoid(b.astype(jnp.float32))
    g = -jnp.exp(a_log.astype(jnp.float32)) * jax.nn.softplus(
        a.astype(jnp.float32) + dt_bias.astype(jnp.float32))
    o = chunk_gated_delta_rule(q, k, v, g, beta)
    o = rms_norm(o, norm_gain) * jax.nn.silu(z)
    return o.reshape(B, S, GDN_VAL_DIM) @ w_out

def conv_glu_ffn(u, w_up, conv_w, conv_b, w_down):
    gu = u @ w_up
    gate = causal_dwconv(gu[..., :D_FF], conv_w) + conv_b
    return (jax.nn.silu(gate) * gu[..., D_FF:]) @ w_down

def first_inputs(seed: int = 0) -> dict:
    key = jax.random.key(seed)
    ks = jax.random.split(key, 24)
    f32 = jnp.float32

    def nrm(k, shape, scale):
        return jax.random.normal(k, shape, f32) * scale

    x = nrm(ks[0], (BATCH, SEQ, D_MODEL), 1.0)
    start = jax.random.randint(ks[1], (BATCH, 1), 0, 4096, dtype=jnp.int32)
    positions = start + jnp.arange(SEQ, dtype=jnp.int32)[None, :]
    mixer_norm = 1.0 + nrm(ks[2], (DEPTH, D_MODEL), 0.05)
    ffn_norm = 1.0 + nrm(ks[3], (DEPTH, D_MODEL), 0.05)

    attn_w_in = nrm(ks[4], (N_ATTN_LAYERS, D_MODEL, ATTN_IN_DIM), D_MODEL ** -0.5)
    attn_q_gain = 1.0 + nrm(ks[5], (N_ATTN_LAYERS, ATTN_HEAD_DIM), 0.05)
    attn_k_gain = 1.0 + nrm(ks[6], (N_ATTN_LAYERS, ATTN_HEAD_DIM), 0.05)
    attn_sinks = nrm(ks[7], (N_ATTN_LAYERS, ATTN_HEADS), 1.0)
    attn_w_out = nrm(ks[8], (N_ATTN_LAYERS, ATTN_Q_DIM, D_MODEL), ATTN_Q_DIM ** -0.5)

    gdn_w_in = nrm(ks[9], (N_GDN_LAYERS, D_MODEL, GDN_IN_DIM), D_MODEL ** -0.5)
    gdn_conv = nrm(ks[10], (N_GDN_LAYERS, GDN_CONV, GDN_QKV_DIM), GDN_CONV ** -0.5)
    gdn_a_log = jnp.log(jax.random.uniform(ks[11], (N_GDN_LAYERS, GDN_V_HEADS), f32, 1.0, 16.0))
    dt = jnp.exp(jax.random.uniform(ks[12], (N_GDN_LAYERS, GDN_V_HEADS), f32,
                                    math.log(1e-3), math.log(1e-1)))
    gdn_dt_bias = dt + jnp.log(-jnp.expm1(-dt))
    gdn_norm = 1.0 + nrm(ks[13], (N_GDN_LAYERS, GDN_HEAD_V), 0.05)
    gdn_w_out = nrm(ks[14], (N_GDN_LAYERS, GDN_VAL_DIM, D_MODEL), GDN_VAL_DIM ** -0.5)

    ffn_w_up = nrm(ks[15], (DEPTH, D_MODEL, 2 * D_FF), D_MODEL ** -0.5)
    ffn_conv = nrm(ks[16], (DEPTH, FFN_CONV, D_FF), FFN_CONV ** -0.5)
    ffn_conv_b = nrm(ks[17], (DEPTH, D_FF), 0.02)
    ffn_w_down = nrm(ks[18], (DEPTH, D_FF, D_MODEL), D_FF ** -0.5)
    return {"x": x, "positions": positions, "mixer_norm": mixer_norm, "ffn_norm": ffn_norm,
            "attn_w_in": attn_w_in, "attn_q_gain": attn_q_gain, "attn_k_gain": attn_k_gain,
            "attn_sinks": attn_sinks, "attn_w_out": attn_w_out,
            "gdn_w_in": gdn_w_in, "gdn_conv": gdn_conv, "gdn_a_log": gdn_a_log,
            "gdn_dt_bias": gdn_dt_bias, "gdn_norm": gdn_norm, "gdn_w_out": gdn_w_out,
            "ffn_w_up": ffn_w_up, "ffn_conv": ffn_conv, "ffn_conv_b": ffn_conv_b,
            "ffn_w_down": ffn_w_down}

def first_block(x, positions, mixer_norm, ffn_norm, attn_w_in, attn_q_gain, attn_k_gain,
              attn_sinks, attn_w_out, gdn_w_in, gdn_conv, gdn_a_log, gdn_dt_bias, gdn_norm,
              gdn_w_out, ffn_w_up, ffn_conv, ffn_conv_b, ffn_w_down):
    cos, sin = rope_tables(positions)
    h = x
    for i in range(DEPTH):
        j = i // 2
        u = rms_norm(h, mixer_norm[i])
        if i % 2 == 0:
            h = h + swa_sink_attention(u, attn_w_in[j], attn_q_gain[j], attn_k_gain[j],
                                       attn_sinks[j], attn_w_out[j], cos, sin)
        else:
            h = h + gated_deltanet(u, gdn_w_in[j], gdn_conv[j], gdn_a_log[j], gdn_dt_bias[j],
                                   gdn_norm[j], gdn_w_out[j])
        u = rms_norm(h, ffn_norm[i])
        h = h + conv_glu_ffn(u, ffn_w_up[i], ffn_conv[i], ffn_conv_b[i], ffn_w_down[i])
    return h


DEPTH_2 = 1

CHUNK = 64
Q_BLOCK = 128
D_FF_2 = 2816
A_HEADS = 8
A_HEAD_DIM = 64
A_Q_W = A_HEADS * A_HEAD_DIM
IDX_HEADS = 8
IDX_DIM = 64
TOPK_MAX = 256
B_HEADS = 8
QK_NOPE = 64
QK_ROPE = 32
V_DIM = 64
Q_LORA = 384
KV_LORA = 256
B_V_W = B_HEADS * V_DIM
ROPE_THETA_2 = 10000.0
NUM_BUCKETS = 32
MAX_DISTANCE = 128
IN_SIZES = (A_Q_W, A_HEAD_DIM, A_HEAD_DIM, IDX_HEADS * IDX_DIM, IDX_DIM, IDX_HEADS,
            Q_LORA, KV_LORA, QK_ROPE, 2 * D_MODEL)
IN_COLS = sum(IN_SIZES)
N_ADA = 9


def rmsnorm(x, g):
    xf = x.astype(jnp.float32)
    y = xf * lax.rsqrt(jnp.mean(xf * xf, axis=-1, keepdims=True) + EPS)
    return (y * g.astype(jnp.float32)).astype(x.dtype)

def modulate(h, shift, scale):
    return h * (1 + scale[:, None, :]) + shift[:, None, :]

def swiglu(h, w_in, w_down):
    g, u = jnp.split(h @ w_in, 2, axis=-1)
    return (jax.nn.silu(g) * u) @ w_down

def rope_angles(positions):
    half = QK_ROPE // 2
    freqs = ROPE_THETA_2 ** (-2.0 * jnp.arange(half, dtype=jnp.float32) / QK_ROPE)
    ang = positions.astype(jnp.float32)[..., None] * freqs
    return jnp.cos(ang), jnp.sin(ang)

def apply_rope(x, cos, sin):
    cos = cos.astype(x.dtype)
    sin = sin.astype(x.dtype)
    x1, x2 = jnp.split(x, 2, axis=-1)
    return jnp.concatenate([x1 * cos - x2 * sin, x2 * cos + x1 * sin], axis=-1)

def t5_bucket(rel):
    half = NUM_BUCKETS // 2
    max_exact = half // 2
    ret = jnp.where(rel > 0, half, 0)
    n = jnp.abs(rel)
    nf = jnp.maximum(n, 1).astype(jnp.float32)
    large = max_exact + (jnp.log(nf / max_exact) / math.log(MAX_DISTANCE / max_exact)
                         * (half - max_exact)).astype(jnp.int32)
    large = jnp.minimum(large, half - 1)
    return ret + jnp.where(n < max_exact, n, large)

def to_blocks(a, nb):
    return jnp.swapaxes(a.reshape(a.shape[0], nb, Q_BLOCK, *a.shape[2:]), 0, 1)

def from_blocks(o):
    o = jnp.swapaxes(o, 0, 1)
    return o.reshape(o.shape[0], o.shape[1] * o.shape[2], -1)

def block_limit(t0):
    tq = t0 + jnp.arange(Q_BLOCK, dtype=jnp.int32)
    return (tq // CHUNK + 1) * CHUNK

def dsa_attention(q_a, k_a, v_a, q_idx, k_idx, w_idx, positions, rel_bias, topk):
    B, S = q_a.shape[0], q_a.shape[1]
    nb = S // Q_BLOCK
    key_ids = jnp.arange(S, dtype=jnp.int32)
    gather = jax.vmap(lambda a, i: a[i])
    idx_scale = IDX_DIM ** -0.5
    head_w_scale = IDX_HEADS ** -0.5
    attn_scale = A_HEAD_DIM ** -0.5
    k_idx_f = k_idx.astype(jnp.float32)

    def body(args):
        q_b, qi_b, wi_b, qpos_b, t0 = args
        limit = block_limit(t0)
        dots = jnp.einsum('bqhd,bsd->bqhs', qi_b.astype(jnp.float32), k_idx_f) * idx_scale
        score = jnp.einsum('bqh,bqhs->bqs', wi_b.astype(jnp.float32) * head_w_scale,
                           jax.nn.relu(dots))
        admissible = key_ids[None, :] < limit[:, None]
        score = jnp.where(admissible[None], score, -jnp.inf)
        _, sel = lax.top_k(score, topk)
        valid = sel < limit[None, :, None]
        k_sel = gather(k_a, sel)
        v_sel = gather(v_a, sel)
        pos_sel = gather(positions, sel)
        bias = rel_bias[t5_bucket(pos_sel - qpos_b[..., None])]
        s = jnp.einsum('bqhd,bqkd->bqhk', q_b, k_sel).astype(jnp.float32) * attn_scale
        s = s + jnp.moveaxis(bias, -1, 2).astype(jnp.float32)
        s = jnp.where(valid[:, :, None, :], s, -jnp.inf)
        p = jax.nn.softmax(s, axis=-1).astype(v_sel.dtype)
        return jnp.einsum('bqhk,bqkd->bqhd', p, v_sel)

    t0s = jnp.arange(nb, dtype=jnp.int32) * Q_BLOCK
    o = lax.map(body, (to_blocks(q_a, nb), to_blocks(q_idx, nb), to_blocks(w_idx, nb),
                       to_blocks(positions, nb), t0s))
    return from_blocks(o)

def mla_attention(q_nope, q_pe, k_nope, k_pe, v):
    S = q_nope.shape[1]
    nb = S // Q_BLOCK
    key_ids = jnp.arange(S, dtype=jnp.int32)
    scale = (QK_NOPE + QK_ROPE) ** -0.5

    def body(args):
        qn, qp, t0 = args
        limit = block_limit(t0)
        s = (jnp.einsum('bqhd,bshd->bhqs', qn, k_nope)
             + jnp.einsum('bqhr,bsr->bhqs', qp, k_pe)).astype(jnp.float32) * scale
        mask = key_ids[None, :] < limit[:, None]
        s = jnp.where(mask[None, None], s, -jnp.inf)
        p = jax.nn.softmax(s, axis=-1).astype(v.dtype)
        return jnp.einsum('bhqs,bshd->bqhd', p, v)

    t0s = jnp.arange(nb, dtype=jnp.int32) * Q_BLOCK
    o = lax.map(body, (to_blocks(q_nope, nb), to_blocks(q_pe, nb), t0s))
    return from_blocks(o)

def second_inputs(seed: int = 0) -> dict:
    key = jax.random.key(seed)
    ks = jax.random.split(key, 32)
    f32 = jnp.float32

    def nrm(k, shape, fan_in, mult=1.0):
        return jax.random.normal(k, shape, f32) * (mult * fan_in ** -0.5)

    def gain(k, shape):
        return 1.0 + 0.05 * jax.random.normal(k, shape, f32)

    x = jax.random.normal(ks[0], (BATCH, SEQ, D_MODEL), f32)
    c = jax.random.normal(ks[1], (BATCH, D_MODEL), f32)
    start = jax.random.randint(ks[2], (BATCH, 1), 0, 4096, dtype=jnp.int32)
    positions = start + jnp.arange(SEQ, dtype=jnp.int32)[None, :]
    L = DEPTH_2
    return {
        "x": x,
        "c": c,
        "positions": positions,
        "w_ada": nrm(ks[3], (L, D_MODEL, N_ADA * D_MODEL), D_MODEL, 0.5),
        "b_ada": 0.02 * jax.random.normal(ks[4], (L, N_ADA * D_MODEL), f32),
        "g_ffn1": gain(ks[5], (L, D_MODEL)),
        "w_ffn1_in": nrm(ks[6], (L, D_MODEL, 2 * D_FF_2), D_MODEL),
        "w_ffn1_down": nrm(ks[7], (L, D_FF_2, D_MODEL), D_FF_2),
        "g_mix": gain(ks[8], (L, D_MODEL)),
        "w_in": nrm(ks[9], (L, D_MODEL, IN_COLS), D_MODEL),
        "g_cq": gain(ks[10], (L, Q_LORA)),
        "w_uq": nrm(ks[11], (L, Q_LORA, B_HEADS * (QK_NOPE + QK_ROPE)), Q_LORA),
        "g_ckv": gain(ks[12], (L, KV_LORA)),
        "w_uk": nrm(ks[13], (L, KV_LORA, B_HEADS * QK_NOPE), KV_LORA),
        "w_uv": nrm(ks[14], (L, KV_LORA, B_HEADS * V_DIM), KV_LORA),
        "rel_bias": 0.5 * jax.random.normal(ks[15], (NUM_BUCKETS, A_HEADS), f32),
        "w_o_a": nrm(ks[16], (L, A_Q_W, D_MODEL), A_Q_W),
        "w_o_b": nrm(ks[17], (L, B_V_W, D_MODEL), B_V_W),
        "w_out": nrm(ks[18], (L, D_MODEL, D_MODEL), D_MODEL),
        "g_ffn2": gain(ks[19], (L, D_MODEL)),
        "w_ffn2_in": nrm(ks[20], (L, D_MODEL, 2 * D_FF_2), D_MODEL),
        "w_ffn2_down": nrm(ks[21], (L, D_FF_2, D_MODEL), D_FF_2),
        "g_final": gain(ks[22], (D_MODEL,)),
    }

def second_block(x, c, positions, w_ada, b_ada, g_ffn1, w_ffn1_in, w_ffn1_down, g_mix, w_in,
              g_cq, w_uq, g_ckv, w_uk, w_uv, rel_bias, w_o_a, w_o_b, w_out,
              g_ffn2, w_ffn2_in, w_ffn2_down, g_final):
    B, S, _ = x.shape
    topk = min(TOPK_MAX, S // 4)
    offsets = []
    acc = 0
    for n in IN_SIZES[:-1]:
        acc += n
        offsets.append(acc)
    cos, sin = rope_angles(positions)

    for l in range(DEPTH_2):
        mod = jax.nn.silu(c) @ w_ada[l] + b_ada[l]
        sh1, sc1, gt1, sh2, sc2, gt2, sh3, sc3, gt3 = jnp.split(mod, N_ADA, axis=-1)

        h = modulate(rmsnorm(x, g_ffn1[l]), sh1, sc1)
        x = x + 0.5 * gt1[:, None, :] * swiglu(h, w_ffn1_in[l], w_ffn1_down[l])

        h = modulate(rmsnorm(x, g_mix[l]), sh2, sc2)
        proj = h @ w_in[l]
        (q_a, k_a, v_a, q_idx, k_idx, w_idx, c_q, c_kv, k_rope,
         gate_logits) = jnp.split(proj, offsets, axis=-1)

        o_a = dsa_attention(q_a.reshape(B, S, A_HEADS, A_HEAD_DIM), k_a, v_a,
                            q_idx.reshape(B, S, IDX_HEADS, IDX_DIM), k_idx, w_idx,
                            positions, rel_bias, topk)

        q_b = (rmsnorm(c_q, g_cq[l]) @ w_uq[l]).reshape(B, S, B_HEADS, QK_NOPE + QK_ROPE)
        q_nope, q_pe = jnp.split(q_b, [QK_NOPE], axis=-1)
        c_kv_n = rmsnorm(c_kv, g_ckv[l])
        k_nope = (c_kv_n @ w_uk[l]).reshape(B, S, B_HEADS, QK_NOPE)
        v_b = (c_kv_n @ w_uv[l]).reshape(B, S, B_HEADS, V_DIM)
        q_pe = apply_rope(q_pe, cos[:, :, None, :], sin[:, :, None, :])
        k_pe = apply_rope(k_rope, cos, sin)
        o_b = mla_attention(q_nope, q_pe, k_nope, k_pe, v_b)

        g_a, g_b = jnp.split(jax.nn.sigmoid(gate_logits), 2, axis=-1)
        y = g_a * (o_a @ w_o_a[l]) + g_b * (o_b @ w_o_b[l])
        x = x + gt2[:, None, :] * (y @ w_out[l])

        h = modulate(rmsnorm(x, g_ffn2[l]), sh3, sc3)
        x = x + 0.5 * gt3[:, None, :] * swiglu(h, w_ffn2_in[l], w_ffn2_down[l])

    return rmsnorm(x, g_final)


def setup_inputs(seed=0):
    out = dict(first_inputs(seed))
    for name, value in second_inputs(seed + 1).items():
        if name != "x":
            out[name + "_2"] = value
    return out


def reference(
    x, positions, mixer_norm, ffn_norm, attn_w_in, attn_q_gain, attn_k_gain, attn_sinks,
    attn_w_out, gdn_w_in, gdn_conv, gdn_a_log, gdn_dt_bias, gdn_norm, gdn_w_out, ffn_w_up,
    ffn_conv, ffn_conv_b, ffn_w_down, c_2, positions_2, w_ada_2, b_ada_2, g_ffn1_2, w_ffn1_in_2,
    w_ffn1_down_2, g_mix_2, w_in_2, g_cq_2, w_uq_2, g_ckv_2, w_uk_2, w_uv_2, rel_bias_2,
    w_o_a_2, w_o_b_2, w_out_2, g_ffn2_2, w_ffn2_in_2, w_ffn2_down_2, g_final_2,
):
    x = first_block(
        x, positions, mixer_norm, ffn_norm, attn_w_in, attn_q_gain, attn_k_gain, attn_sinks,
        attn_w_out, gdn_w_in, gdn_conv, gdn_a_log, gdn_dt_bias, gdn_norm, gdn_w_out, ffn_w_up,
        ffn_conv, ffn_conv_b, ffn_w_down,
    )
    return second_block(
        x, c_2, positions_2, w_ada_2, b_ada_2, g_ffn1_2, w_ffn1_in_2, w_ffn1_down_2, g_mix_2,
        w_in_2, g_cq_2, w_uq_2, g_ckv_2, w_uk_2, w_uv_2, rel_bias_2, w_o_a_2, w_o_b_2, w_out_2,
        g_ffn2_2, w_ffn2_in_2, w_ffn2_down_2, g_final_2,
    )


_drawn_inputs = setup_inputs


def setup_inputs(seed=0):
    import zlib

    import numpy as np

    out = dict(_drawn_inputs(seed))
    spreads = {}
    factors = {'attn_q_gain': 4.395,
     'attn_k_gain': 4.403,
     'attn_sinks': 4.035,
     'ffn_conv_b': 3.684,
     'b_ada_2': 5.654,
     'g_ffn1_2': 8.0,
     'g_mix_2': 8.0,
     'g_cq_2': 8.0,
     'w_uq_2': 4.696,
     'g_ckv_2': 8.0,
     'w_uk_2': 5.301,
     'rel_bias_2': 7.475,
     'g_ffn2_2': 8.0}
    for name, (base, spread) in spreads.items():
        noise = np.random.default_rng([zlib.crc32(name.encode()), seed]).standard_normal(out[name].shape)
        drawn = base * np.exp(spread * noise) if base else spread * noise
        out[name] = __import__('jax').numpy.asarray(drawn.astype(out[name].dtype))
    for name, factor in factors.items():
        out[name] = (out[name] * factor).astype(out[name].dtype)
    return out
```

```python
import math
from contextlib import ExitStack

import numpy as np

import concourse.bass as bass
from concourse import mybir

F32 = mybir.dt.float32
F32R = mybir.dt.float32r
BF16 = mybir.dt.bfloat16
I32 = mybir.dt.int32
ACT = mybir.ActivationFunctionType
ALU = mybir.AluOpType
AXX = mybir.AxisListType.X

P = 128
T = 512
TB = T // P
D = 1024
KT = D // P
RING = 4
BW = KT * P
EPS = 1e-6
BIG = 1e30

FFN_TILES = 3072 // P
SWI_TILES = 2816 // P
CH = 8
N_ADA = 72

ROPE1_HALF, ROPE1_THETA = 8, 500000.0
ROPE2_HALF, ROPE2_THETA = 16, 10000.0

PARAM_COLS = [
    ("mixer_norm", 16), ("ffn_norm", 16), ("ffn_conv", 2 * 3 * FFN_TILES), ("ffn_conv_b", 2 * FFN_TILES),
    ("g_ffn1", KT), ("g_mix", KT), ("g_ffn2", KT), ("g_final", KT), ("c", KT), ("b_ada", N_ADA),
    ("gdn_conv", 4 * 32), ("gdn_norm", 1), ("q_gain", 1), ("k_gain", 1), ("sinks", 16),
    ("a_log", 16), ("dt_bias", 16), ("g_cq", 3), ("g_ckv", 2), ("rel_at", 8), ("rel_before", 8),
]
PARAM_AT, _at = {}, 0
for _n, _w in PARAM_COLS:
    PARAM_AT[_n] = _at
    _at += _w
PARAM_W = _at

COMMON_AT = {"ident": 0, "ones": 128, "head_ones": 256, "inv_freq": 384, "eps": 386}
COMMON_W = 387
SWA_AT = {"rot": 0, "mask": 128, "mask_first": 384}
GDN_AT = {"cumsum": 0, "chunk0": 128, "chunk1": 256, "decay_mask": 384, "levels": 512}
MIX_AT = {"rot": 0, "limit": 128, "thresholds": 256, "query_of_row": 257}
PHASE_W = 1280
MIX_W = MIX_AT["query_of_row"] + 4 * P

SECTIONS = [
    ("qkv", 12, 1024), ("attn_out", 8, 1024), ("ffn0", 72, 1024), ("gdn_ba", 1, 256), ("gdn", 64, 1024),
    ("ffn1", 72, 1024), ("swi0", 60, 1024), ("swi0_tail", 8, 768), ("mix_v", 1, 576), ("mix_in", 16, 1024),
    ("uq", 3, 768), ("ukv", 2, 1024), ("mix_out", 24, 1024), ("w_out", 8, 1024), ("swi1", 60, 1024),
    ("swi1_tail", 8, 768),
]
FIRST, _b = {}, 0
for _n, _k, _w in SECTIONS:
    FIRST[_n] = _b
    _b += _k
N_BLOCKS = _b
ARENA_W = 15872


def build(nc, dram, out):
    ctx = ExitStack()
    with ctx:
        sems = {}

        def S(name):
            if name not in sems:
                sems[name] = ctx.enter_context(nc.semaphore(name))
            return sems[name]

        def sb(name, shape, dt=F32):
            return ctx.enter_context(nc.sbuf_tensor(name, shape, dt))

        h = sb("residual", [P, KT, T])
        u_hi, u_lo = sb("u_hi", [P, KT, T], F32R), sb("u_lo", [P, KT, T], F32R)
        a_hi, a_lo = sb("a_hi", [P, CH, T], F32R), sb("a_lo", [P, CH, T], F32R)
        w_raw = sb("w_raw", [P, RING, BW])
        w_hi, w_lo = sb("w_hi", [P, RING, BW], F32R), sb("w_lo", [P, RING, BW], F32R)
        params = sb("params", [P, PARAM_W])
        common = sb("common", [P, COMMON_W])
        phase_const = sb("phase_const", [P, PHASE_W])
        mod = sb("mod", [P, N_ADA])
        gains = sb("gains", [P, 3 * KT])
        silu_c = sb("silu_c", [P, KT])
        arena = sb("arena", [P, ARENA_W])
        onehot = sb("onehot", [P, 2, T], F32R)
        table_hi, table_lo = sb("table_hi", [P, 4, P], F32R), sb("table_lo", [P, 4, P], F32R)
        ps = ctx.enter_context(nc.psum_tensor("ps", [P, 8, T], F32))

        def par(name, i=0, n=1):
            return params[:, PARAM_AT[name] + i:PARAM_AT[name] + i + n]

        def pcol(name, i):
            return params[:, bass.ds(PARAM_AT[name] + i, 1)]

        ident = common[:, 0:128]
        ones = common[:, 128:256]
        head_ones = common[:, 256:384]

        def view(at, *dims):
            n = int(np.prod(dims))
            assert at + n <= ARENA_W, (at, dims)
            v = arena[:, at:at + n]
            names = " ".join(f"d{k}" for k in range(len(dims)))
            return v if len(dims) == 1 else v.rearrange(
                f"p ({names}) -> p {names}", **{f"d{k}": n_ for k, n_ in enumerate(dims)})

        def num(base, i, more=0):
            return base + more if isinstance(i, int) and i == 0 else i * 4 + (base + more)

        def load_block(sp, base, i, src, width):
            s = base % RING
            if base >= RING:
                sp.wait_ge(S("lo_ready"), num(base, i, 1 - RING))
            sp.dma_start(w_raw[:, s, 0:width], src).then_inc(S(f"raw_landed{s}"), 16)

        def split_hi(act, base, i=0):
            s = base % RING
            lap = base // RING + 1
            act.wait_ge(S(f"raw_landed{s}"), 16 * lap if isinstance(i, int) else (i + lap) * 16)
            if base >= RING:
                act.wait_ge(S("block_done"), num(base, i, 1 - RING))
            nc.scalar.activation(w_hi[:, s, :], w_raw[:, s, :], ACT.Copy).then_inc(S("hi_ready"), 1)

        def split_lo(pool, base, i=0):
            s = base % RING
            pool.wait_ge(S("hi_ready"), num(base, i, 1))
            nc.gpsimd.tensor_tensor(w_lo[:, s, :], w_raw[:, s, :], w_hi[:, s, :].bitcast(F32),
                                    ALU.subtract).then_inc(S("lo_ready"), 1)

        def product(dst, l_hi, l_lo, r_hi, r_lo, first, last):
            nc.tensor.matmul(dst, l_hi, r_hi, start=first, stop=False)
            nc.tensor.matmul(dst, l_hi, r_lo, start=False, stop=False)
            return nc.tensor.matmul(dst, l_lo, r_hi, start=False, stop=last)

        def out_tile(dst, slot, x_hi, x_lo, kts, w_at=0, x_at=0):
            for k in range(kts):
                c = (w_at + k) * P
                last = product(dst, w_hi[:, slot, c:c + P], w_lo[:, slot, c:c + P],
                               x_hi[:, x_at + k, :], x_lo[:, x_at + k, :], k == 0, k == kts - 1)
            return last

        def block_matmul(pe, base, i, x_hi, x_lo, kts=KT):
            pe.wait_ge(S("lo_ready"), num(base, i, 1))
            pe.wait_ge(S("bank_free"), num(base, i, 1))
            out_tile(ps[:, base % 4, :], base % RING, x_hi, x_lo, kts).then_inc(S("block_done"), 1)

        def lookahead(act, base, i=0):
            if base + 2 < N_BLOCKS:
                split_hi(act, base + 2, i)

        SQ, RSTD, NT = view(0, 2, T), view(1024, T), view(1536, 2, T)

        def norm_act(act, n, block, shift=None):
            act.wait_ge(S("bank_free"), block + 4)
            if n == 0:
                act.wait_ge(S("x_landed"), 16)
            for k in range(KT):
                if k >= 2:
                    act.wait_ge(S("sq_used"), 8 * n + k - 1)
                nc.scalar.activation(SQ[:, k % 2, :], h[:, k, :], ACT.Square).then_inc(S("sq_ready"), 1)
            act.wait_ge(S("sq_used"), 8 * n + 8)
            nc.scalar.activation(RSTD, ps[:, 4, :], ACT.Ln, bias=eps_col, scale=1.0 / D).then_inc(S("rstd_ready"), 1)
            act.wait_ge(S("rstd_ready"), 2 * n + 1)
            nc.scalar.activation(RSTD, RSTD, ACT.Exp, scale=-0.5).then_inc(S("rstd_ready"), 1)
            if n == 7:
                return
            for k in range(KT):
                act.wait_ge(S("normed"), 8 * n + k + 1)
                if shift is None:
                    nc.scalar.activation(u_hi[:, k, :], NT[:, k % 2, :], ACT.Copy).then_inc(S("u_hi_ready"), 1)
                else:
                    nc.scalar.activation(u_hi[:, k, :], NT[:, k % 2, :], ACT.Identity,
                                         bias=shift(k)).then_inc(S("u_hi_ready"), 1)

        def norm_pe(pe, n):
            if n:
                pe.wait_ge(S("rstd_ready"), 2 * n)
            for k in range(KT):
                pe.wait_ge(S("sq_ready"), 8 * n + k + 1)
                nc.tensor.matmul(ps[:, 4, :], ones, SQ[:, k % 2, :], start=k == 0, stop=k == KT - 1)\
                    .then_inc(S("sq_used"), 1)

        def norm_dve(dve, n, gain, shift=None):
            dve.wait_ge(S("rstd_ready"), 2 * n + 2)

            def normed(k):
                if k >= 2:
                    dve.wait_ge(S("u_lo_ready"), 8 * n + k - 1)
                nc.vector.scalar_tensor_tensor(out=NT[:, k % 2, :], in0=h[:, k, :], scalar=gain(k), in1=RSTD,
                                               op0=ALU.mult, op1=ALU.mult).then_inc(S("normed"), 1)

            def low(k):
                dve.wait_ge(S("u_hi_ready"), 8 * n + k + 1)
                hi = u_hi[:, k, :].bitcast(F32)
                if shift is None:
                    nc.vector.tensor_tensor(u_lo[:, k, :], NT[:, k % 2, :], hi, ALU.subtract)\
                        .then_inc(S("u_lo_ready"), 1)
                else:
                    nc.vector.scalar_tensor_tensor(out=u_lo[:, k, :], in0=NT[:, k % 2, :], scalar=shift(k),
                                                   in1=hi, op0=ALU.add, op1=ALU.subtract)\
                        .then_inc(S("u_lo_ready"), 1)

            normed(0)
            for k in range(1, KT):
                normed(k)
                low(k - 1)
            low(KT - 1)

        def u_is_ready(pe, n):
            pe.wait_ge(S("u_lo_ready"), 8 * n + 8)

        ADA_RING = view(13312, 2, BW)
        ADA = ps[:, 5, 0:N_ADA]

        def ada_load(sp, body):
            for q in range(2):
                sp.wait_ge(S("ada_free"), body * 2 + (q + 1))
                src = dram["ada"][bass.ds(body * 2 + q, 1)].rearrange("a p n -> (a p) n")
                sp.dma_start(ADA_RING[:, q, :], src).then_inc(S(f"ada_landed{q}"), 16)

        def ada_matmul(pe, body):
            for q in range(2):
                pe.wait_ge(S(f"ada_landed{q}"), body * 16 + 16)
                for k in range(KT):
                    last = nc.tensor.matmul(ps[:, 5, bass.ds(body * 2 + q, 1)], ADA_RING[:, q, k * P:(k + 1) * P],
                                            silu_c[:, k:k + 1], start=k == 0, stop=k == KT - 1)
                last.then_inc(S("ada_free"), 1)

        CV, AV = view(5632, 2, T), view(6656, 2, T)

        def ffn_chunks(kind):
            n = {"ffn0": 0, "ffn1": 1, "swi0": 2, "swi1": 3}[kind]
            tiles = FFN_TILES if n < 2 else SWI_TILES
            pair0 = [0, 24, 48, 70][n]
            b = FIRST[kind]
            done = 0
            while done < tiles:
                m = min(CH, tiles - done)
                ada = (n * 3 + done // CH) * 6 if n < 2 else None
                yield b, pair0 + done, done, m, ada
                b += 2 * m + 8
                done += m

        def ffn_sp(sp, kind):
            first = FIRST[kind]
            for b, _, _, m, ada in ffn_chunks(kind):
                if b == FIRST["ffn1"]:
                    sp.wait_ge(S("bank_free"), b + 4)
                with sp.Fori(0, m // 2) as i:
                    for j in range(4):
                        load_block(sp, b + j, i, dram[kind][bass.ds(i * 4 + (b - first + j), 1)]
                                   .rearrange("a p n -> (a p) n"), BW)
                    if ada is not None:
                        ada_load(sp, i + ada)
                b += 2 * m
                src, at, width = (dram[kind], b - first, BW) if m == CH else (dram[kind + "_tail"], 0, m * P)
                with sp.Fori(0, 2) as i:
                    for j in range(4):
                        load_block(sp, b + j, i, src[bass.ds(i * 4 + (at + j), 1)]
                                   .rearrange("a p n -> (a p) n"), width)
                    if ada is not None:
                        ada_load(sp, i + (ada + 4))

        def ffn_pe(pe, kind):
            for b, pair, _, m, ada in ffn_chunks(kind):
                with pe.Fori(0, m // 2) as i:
                    for j in range(4):
                        block_matmul(pe, b + j, i, u_hi, u_lo)
                    if ada is not None:
                        ada_matmul(pe, i + ada)
                pe.wait_ge(S("a_lo_ready"), pair + m)
                b += 2 * m
                with pe.Fori(0, 2) as i:
                    for j in range(4):
                        block_matmul(pe, b + j, i, a_hi, a_lo, m)
                    if ada is not None:
                        ada_matmul(pe, i + (ada + 4))

        def ffn_act(act, kind, layer):
            conv = kind.startswith("ffn")
            for b, pair, tile, m, _ in ffn_chunks(kind):
                with act.Fori(0, m // 2) as i:
                    for q in range(2):
                        bg, bu = b + 2 * q, b + 2 * q + 1
                        lookahead(act, bg, i)
                        act.wait_ge(S("block_done"), num(bg, i, 1))
                        n = i * 2 + (pair + q)
                        if conv:
                            col = i * 2 + (tile + q)
                            base = layer * 3 * FFN_TILES
                            nc.scalar.activation(CV[:, q, :], ps[:, bg % 4, :], ACT.Identity,
                                                 scale=pcol("ffn_conv", col + (base + 2 * FFN_TILES)),
                                                 bias=pcol("ffn_conv_b", col + layer * FFN_TILES))\
                                .then_inc(S("cv_main"), 1)
                            lookahead(act, bu, i)
                            act.wait_ge(S("bank_free"), num(bg, i, 5))
                            nc.scalar.activation(CV[:, q, :], CV[:, q, :], ACT.Silu).then_inc(S("silu_ready"), 1)
                        else:
                            nc.scalar.activation(CV[:, q, :], ps[:, bg % 4, :], ACT.Silu)\
                                .then_inc(S("silu_ready"), 1)
                            lookahead(act, bu, i)
                        act.wait_ge(S("bank_free"), num(bu, i, 5))
                        t = i * 2 + q
                        nc.scalar.activation(a_hi[:, bass.ds(t, 1), :], AV[:, q, None, :], ACT.Copy)\
                            .then_inc(S("a_hi_ready"), 1)
                b += 2 * m
                tail = b + 8 == N_BLOCKS
                with act.Fori(0, 1 if tail else 2) as i:
                    for j in range(4):
                        lookahead(act, b + j, i)
                if tail:
                    for j in range(4, 8):
                        lookahead(act, b + j)

        def ffn_dve(dve, kind, layer, gate=None):
            conv = kind.startswith("ffn")
            for b, pair, tile, m, _ in ffn_chunks(kind):
                with dve.Fori(0, m // 2) as i:
                    for q in range(2):
                        bg, bu = b + 2 * q, b + 2 * q + 1
                        n = i * 2 + (pair + q)
                        if conv:
                            nconv = n
                            col = i * 2 + (tile + q)
                            base = layer * 3 * FFN_TILES
                            dve.wait_ge(S("cv_main"), nconv + 1)
                            nc.vector.scalar_tensor_tensor(
                                out=CV[:, q, 1:T], in0=ps[:, bg % 4, 0:T - 1],
                                scalar=pcol("ffn_conv", col + (base + FFN_TILES)), in1=CV[:, q, 1:T],
                                op0=ALU.mult, op1=ALU.add).then_inc(S("cv_tap"), 1)
                            dve.wait_ge(S("cv_tap"), nconv + 1)
                            nc.vector.scalar_tensor_tensor(
                                out=CV[:, q, 2:T], in0=ps[:, bg % 4, 0:T - 2],
                                scalar=pcol("ffn_conv", col + base), in1=CV[:, q, 2:T],
                                op0=ALU.mult, op1=ALU.add).then_inc(S("bank_free"), 1)
                        dve.wait_ge(S("silu_ready"), n + 1)
                        dve.wait_ge(S("block_done"), num(bu, i, 1))
                        nc.vector.tensor_tensor(AV[:, q, :], CV[:, q, :], ps[:, bu % 4, :], ALU.mult)\
                            .then_inc(S("bank_free"), 1 if conv else 2)
                        dve.wait_ge(S("a_hi_ready"), n + 1)
                        nc.vector.tensor_tensor(a_lo[:, bass.ds(i * 2 + q, 1), :], AV[:, q, None, :],
                                                a_hi[:, bass.ds(i * 2 + q, 1), :].bitcast(F32), ALU.subtract)\
                            .then_inc(S("a_lo_ready"), 1)
                b += 2 * m
                with dve.Fori(0, 2) as i:
                    for j in range(4):
                        residual_dve(dve, b + j, i, i * 4 + j, None if gate is None else gate(i * 4 + j))

        def residual_dve(dve, base, i, tile, gate=None):
            dve.wait_ge(S("block_done"), num(base, i, 1))
            dve.wait_ge(S("bank_free"), num(base, i, 4))
            at = h[:, bass.ds(tile, 1), :]
            src = ps[:, base % 4:base % 4 + 1, :]
            if gate is None:
                nc.vector.tensor_tensor(at, at, src, ALU.add).then_inc(S("bank_free"), 1)
            else:
                nc.vector.scalar_tensor_tensor(out=at, in0=src, scalar=gate, in1=at, op0=ALU.mult,
                                               op1=ALU.add).then_inc(S("bank_free"), 1)

        def mod_col(v, k, at=mod):
            return at[:, bass.ds(k + v * KT, 1)]

        eps_col = common[:, 386:387]
        chain_count = [0]

        def link(dve, ins):
            chain_count[0] += 1
            ins.then_inc(S("dve_chain"), 1)
            dve.wait_ge(S("dve_chain"), chain_count[0])

        TWO_PI_PARTS = (6.28125, 1.935005187988281e-3, 2.0 * math.pi - 6.28125 - 1.935005187988281e-3)
        ROUND = 1.5 * 2.0 ** 23

        def rope_dve(dve, which, at_cos, at_sin, scratch):
            pos, ang, turns = view(scratch, T), view(scratch + T, T), view(scratch + 2 * T, T)
            dve.wait_ge(S(f"positions{which}"), 16)
            link(dve, nc.vector.tensor_copy(pos, pos.bitcast(I32)))
            freq = common[:, COMMON_AT["inv_freq"] + which:COMMON_AT["inv_freq"] + which + 1]
            link(dve, nc.vector.tensor_scalar(ang, pos, freq, None, ALU.mult))
            for dst, quarter in ((at_cos, 0.25), (at_sin, 0.0)):
                link(dve, nc.vector.tensor_scalar(turns, ang, 1.0 / (2.0 * math.pi), quarter, ALU.mult, ALU.add))
                link(dve, nc.vector.tensor_scalar(turns, turns, ROUND, None, ALU.add))
                link(dve, nc.vector.tensor_scalar(turns, turns, -ROUND, None, ALU.add))
                src = ang
                for part in TWO_PI_PARTS:
                    link(dve, nc.vector.scalar_tensor_tensor(out=dst, in0=turns, scalar=-part, in1=src,
                                                             op0=ALU.mult, op1=ALU.add))
                    src = dst
                link(dve, nc.vector.tensor_scalar(dst, dst, 2.0 * math.pi * quarter, 3.1415925, ALU.add, ALU.min))
                nc.vector.tensor_scalar(dst, dst, -3.1415925, None, ALU.max).then_inc(S("angle_ready"), 1)
                dve.wait_ge(S("angle_ready"), 2 * which + (1 if quarter else 2))

        def rope_act(act, which, at_cos, at_sin):
            for k, dst in enumerate((at_cos, at_sin)):
                act.wait_ge(S("angle_ready"), 2 * which + k + 1)
                nc.scalar.activation(dst, dst, ACT.Sin).then_inc(S("rope_table"), 1)

        HSQ, HR, QN = view(0, 2, T), view(1024, 2, T), view(2048, 2, T)
        ROT1, ROT2 = view(3072, T), view(3584, T)
        COS1, SIN1 = view(4096, T), view(4608, T)
        Q1 = view(5120, 8, T)
        K1 = view(9216, 2, P + T)
        V1 = view(10496, TB + 1, 256)
        ROPE1_SCRATCH = 11776
        SC1 = view(0, 2, 4 * 256)
        PT1 = view(2048, 2, 2, 512)
        ST1 = view(4096, 2, 32)
        ROTM = phase_const[:, 0:128]

        def swa_sp(sp):
            b = FIRST["qkv"]
            for j in range(4):
                load_block(sp, b + j, 0, dram["qkv"][j], BW)
            with sp.Fori(0, 2) as i:
                for j in range(4):
                    load_block(sp, b + 4 + j, i, dram["qkv"][bass.ds(i * 4 + (4 + j), 1)]
                               .rearrange("a p n -> (a p) n"), BW)
            with sp.Fori(0, 2) as i:
                for j in range(4):
                    load_block(sp, b + 12 + j, i, dram["attn_out"][bass.ds(i * 4 + j, 1)]
                               .rearrange("a p n -> (a p) n"), BW)

        def swa_pe(pe):
            b = FIRST["qkv"]

            def head_sum(j):
                pe.wait_ge(S("head_sq"), j + 1)
                if j >= 2:
                    pe.wait_ge(S("head_rstd"), 2 * j - 3)
                nc.tensor.matmul(ps[:, 4 + j % 2, :], head_ones, HSQ[:, j % 2, :], start=True, stop=True)\
                    .then_inc(S("head_sum"), 1)

            def rotate(j):
                pe.wait_ge(S("bank_free"), b + 5 + j)
                if j >= 2:
                    pe.wait_ge(S("roped"), j - 1)
                nc.tensor.matmul(ps[:, 6 + j % 2, :], ROTM, QN[:, j % 2, :], start=True, stop=True)\
                    .then_inc(S("rotated"), 1)

            pe.wait_ge(S("rstd_ready"), 2)
            pe.wait_ge(S("swa_const"), 16)
            for j in range(10):
                block_matmul(pe, b + j, 0, u_hi, u_lo)
                if j >= 1:
                    head_sum(j - 1)
                if j >= 2:
                    rotate(j - 2)
            pe.wait_ge(S("lo_ready"), b + 12)
            pe.wait_ge(S("bank_free"), b + 12)
            for t in range(TB):
                dst = ps[:, 2 + t // 2, (t % 2) * 256:(t % 2) * 256 + 256]
                for k in range(KT):
                    s, c = (b + 10 + k // 4) % RING, (k % 4) * 256
                    last = product(dst, u_hi[:, k, t * P:(t + 1) * P], u_lo[:, k, t * P:(t + 1) * P],
                                   w_hi[:, s, c:c + 256], w_lo[:, s, c:c + 256], k == 0, k == KT - 1)
                if t == 0:
                    head_sum(9)
                    rotate(8)
            last.then_inc(S("block_done"), 2)
            rotate(9)

            def scores(it):
                n, kv = divmod(it, 4)
                if it >= 2:
                    pe.wait_ge(S("masked"), it - 1)
                o = 64 * (kv % 2)
                for g in range(4):
                    dst = ps[:, 2 * (it % 2) + g // 2, (g % 2) * 256:(g % 2) * 256 + 256]
                    last = nc.tensor.matmul(dst, Q1[o:o + 64, kv // 2 * 4 + g, n * P:(n + 1) * P],
                                            K1[o:o + 64, kv // 2, n * P:n * P + 256], start=True, stop=True)
                last.then_inc(S("scored"), 1)

            pe.wait_ge(S("roped"), 10)
            pe.wait_ge(S("bank_free"), b + 16)
            scores(0)
            for it in range(16):
                n, kv = divmod(it, 4)
                if it + 1 < 16:
                    scores(it + 1)
                pe.wait_ge(S("probs"), it + 1)
                if it >= 1:
                    pe.wait_ge(S("pt_act"), it)
                    pe.wait_ge(S("pt_dve"), it)
                for kb in range(2):
                    for g in range(4):
                        last = nc.tensor.transpose(ps[:, 4 + kb, g * P:(g + 1) * P],
                                                   SC1[:, it % 2, g * 256 + kb * P:g * 256 + (kb + 1) * P], ident)
                last.then_inc(S("probs_turned"), 1)
                pe.wait_ge(S("pt_act"), it + 1)
                pe.wait_ge(S("pt_dve"), it + 1)
                if it >= 2:
                    pe.wait_ge(S("o_lo"), it - 1)
                for half in range(2):
                    for kb in range(2):
                        last = nc.tensor.matmul(ps[64 * half:64 * half + 64, 6 + it % 2, 0:256],
                                                V1[:, n + kb, kv * 64:(kv + 1) * 64],
                                                PT1[:, it % 2, kb, half * 256:half * 256 + 256],
                                                start=kb == 0, stop=kb == 1)
                last.then_inc(S("pv_done"), 1)
            pe.wait_ge(S("o_lo"), 16)
            with pe.Fori(0, 2) as i:
                for j in range(4):
                    block_matmul(pe, b + 12 + j, i, a_hi, a_lo)

        def swa_act(act):
            b = FIRST["qkv"]

            def rstd(j):
                act.wait_ge(S("head_sum"), j + 1)
                if j >= 2:
                    act.wait_ge(S("bank_free"), b + 3 + j)
                nc.scalar.activation(HR[:, j % 2, :], ps[:, 4 + j % 2, :], ACT.Ln, bias=eps_col, scale=1.0 / 64)\
                    .then_inc(S("head_rstd"), 1)
                act.wait_ge(S("head_rstd"), 2 * j + 1)
                nc.scalar.activation(HR[:, j % 2, :], HR[:, j % 2, :], ACT.Exp, scale=-0.5)\
                    .then_inc(S("head_rstd"), 1)

            for j in range(12):
                lookahead(act, b + j)
                if j < 10:
                    act.wait_ge(S("block_done"), b + j + 1)
                    if j >= 2:
                        act.wait_ge(S("head_sum"), j - 1)
                    nc.scalar.activation(HSQ[:, j % 2, :], ps[:, (b + j) % 4, :], ACT.Square)\
                        .then_inc(S("head_sq"), 1)
                if 1 <= j <= 10:
                    rstd(j - 1)

            def exps(it):
                act.wait_ge(S("neg_max"), it + 1)
                st = ST1[:, it % 2, :]
                for g in range(4):
                    row = SC1[:, it % 2, g * 256:(g + 1) * 256]
                    nc.scalar.activation(row, row, ACT.Exp, bias=st[:, 4 + g:5 + g], accum_out=st[:, 12 + g:13 + g])\
                        .then_inc(S("exped"), 1)
                nc.scalar.activation(st[:, 8:12], st[:, 8:12], ACT.Exp).then_inc(S("exped"), 1)

            exps(0)
            for it in range(16):
                n, kv = divmod(it, 4)
                if it + 1 < 16:
                    exps(it + 1)
                act.wait_ge(S("probs_turned"), it + 1)
                if it >= 2:
                    act.wait_ge(S("pv_done"), it - 1)
                nc.scalar.activation(PT1[:, it % 2, 0, :], ps[:, 4, :], ACT.Copy).then_inc(S("pt_act"), 1)
                act.wait_ge(S("pv_done"), it + 1)
                nc.scalar.activation(a_hi[:, 2 * kv:2 * kv + 2, n * P:(n + 1) * P],
                                     ps[:, 6 + it % 2, 0:256].rearrange("p (g q) -> p g q", g=2), ACT.Copy)\
                    .then_inc(S("o_hi"), 1)
            with act.Fori(0, 2) as i:
                for j in range(4):
                    lookahead(act, b + 12 + j, i)

        def swa_dve(dve):
            b = FIRST["qkv"]
            nc.vector.memset(K1[:, :, 0:P], 0.0).then_inc(S("dve_chain"), 1)
            nc.vector.memset(V1[:, 0, :], 0.0).then_inc(S("dve_chain"), 1)
            chain_count[0] += 2

            def normed(j):
                dve.wait_ge(S("head_rstd"), 2 * j + 2)
                nc.vector.scalar_tensor_tensor(out=QN[:, j % 2, :], in0=ps[:, (b + j) % 4, :],
                                               scalar=par("q_gain" if j < 8 else "k_gain"),
                                               in1=HR[:, j % 2, :], op0=ALU.mult, op1=ALU.mult)\
                    .then_inc(S("bank_free"), 1)

            def roped(j):
                dve.wait_ge(S("bank_free"), b + 5 + j)
                link(dve, nc.vector.tensor_tensor(ROT1, QN[:, j % 2, :], COS1, ALU.mult))
                dve.wait_ge(S("rotated"), j + 1)
                link(dve, nc.vector.tensor_tensor(ROT2, ps[:, 6 + j % 2, :], SIN1, ALU.mult))
                dst = Q1[:, j, :] if j < 8 else K1[:, j - 8, P:P + T]
                nc.vector.tensor_tensor(dst, ROT1, ROT2, ALU.add).then_inc(S("roped"), 1)
                dve.wait_ge(S("roped"), j + 1)

            dve.wait_ge(S("rope_table"), 2)
            normed(0)
            for j in range(10):
                if j + 1 < 10:
                    normed(j + 1)
                roped(j)
            dve.wait_ge(S("block_done"), b + 12)
            for z in range(2):
                nc.vector.tensor_copy(V1[:, 1 + 2 * z:3 + 2 * z, :],
                                      ps[:, 2 + z, :].rearrange("p (t d) -> p t d", t=2))\
                    .then_inc(S("bank_free"), 1)

            def mask(it):
                n, kv = divmod(it, 4)
                st = ST1[:, it % 2, :]
                dve.wait_ge(S("scored"), it + 1)
                if it >= 2:
                    dve.wait_ge(S("probs_turned"), it - 1)
                at = SWA_AT["mask_first" if n == 0 else "mask"]
                m = phase_const[:, None, at:at + 256].to_broadcast([P, 4, 256])
                nc.vector.scalar_tensor_tensor(
                    out=SC1[:, it % 2, :].rearrange("p (g k) -> p g k", g=4),
                    in0=ps[:, 2 * (it % 2):2 * (it % 2) + 2, :].rearrange("p a (g k) -> p (a g) k", g=2),
                    scalar=0.125, in1=m, op0=ALU.mult, op1=ALU.add).then_inc(S("masked"), 1)
                dve.wait_ge(S("masked"), it + 1)
                link(dve, nc.vector.reduce_max(st[:, 0:4], SC1[:, it % 2, :].rearrange("p (g k) -> p g k", g=4), AXX))
                link(dve, nc.vector.tensor_tensor(st[:, 0:4], st[:, 0:4], par("sinks", 4 * kv, 4), ALU.max))
                link(dve, nc.vector.tensor_scalar(st[:, 4:8], st[:, 0:4], -1.0, None, ALU.mult))
                nc.vector.tensor_tensor(st[:, 8:12], par("sinks", 4 * kv, 4), st[:, 4:8], ALU.add)\
                    .then_inc(S("neg_max"), 1)

            mask(0)
            for it in range(16):
                n, kv = divmod(it, 4)
                st = ST1[:, it % 2, :]
                if it + 1 < 16:
                    mask(it + 1)
                dve.wait_ge(S("exped"), 5 * it + 5)
                link(dve, nc.vector.tensor_tensor(st[:, 16:20], st[:, 8:12], st[:, 12:16], ALU.add))
                link(dve, nc.vector.reciprocal(st[:, 20:24], st[:, 16:20]))
                p = SC1[:, it % 2, :].rearrange("p (g k) -> p g k", g=4)
                nc.vector.tensor_tensor(p, p, st[:, 20:24, None].to_broadcast([P, 4, 256]), ALU.mult)\
                    .then_inc(S("probs"), 1)
                dve.wait_ge(S("probs_turned"), it + 1)
                if it >= 2:
                    dve.wait_ge(S("pv_done"), it - 1)
                nc.vector.tensor_copy(PT1[:, it % 2, 1, :], ps[:, 5, :]).then_inc(S("pt_dve"), 1)
                dve.wait_ge(S("o_hi"), it + 1)
                hi = a_hi[:, 2 * kv:2 * kv + 2, n * P:(n + 1) * P]
                nc.vector.tensor_tensor(a_lo[:, 2 * kv:2 * kv + 2, n * P:(n + 1) * P],
                                        ps[:, 6 + it % 2, 0:256].rearrange("p (g q) -> p g q", g=2),
                                        hi.bitcast(F32), ALU.subtract).then_inc(S("o_lo"), 1)
            with dve.Fori(0, 2) as i:
                for j in range(4):
                    residual_dve(dve, b + 12 + j, i, i * 4 + j)

        QG, KG, VG, ZG = view(0, 2, T), view(1024, 2, T), view(2048, 4, T), view(4096, 4, T)
        SM_NAMES = ["beta", "xa", "ax", "e", "w", "w1", "l", "g", "gc", "neg_gc", "kd", "egc", "ekd", "beg",
                    "gl0", "gl1"]
        SM = {n: view(6144 + 64 * k, 64) for k, n in enumerate(SM_NAMES)}
        GCT, BT = view(7168, T), view(7680, T)
        SLOT = view(8192, 15, T)

        def slot(name, x):
            at = {"mt": 0, "wt": 0, "x": 1, "arg": 1, "qd": 1, "xt": 2, "row_beta": 2, "gated": 2, "c": 3,
                  "row_gc": 3, "kdec": 3, "rstd": 3, "dt": 4, "y": 4, "kbe": 4, "sq": 4, "qkt": 5, "vb": 6}[name]
            return SLOT[:, 2 * at + x, :]

        KK, QK = slot("vb", 0), slot("vb", 1)
        STATE, V_NEW = SLOT[:, 14, 0:256], SLOT[:, 14, 256:512]
        GCV, GSQ, GHR = SLOT[:, 0:2, :], SLOT[:, 2:6, :], SLOT[:, 6:10, :]
        EA = SLOT[:, 10, 0:16]

        def sm_t(name):
            return SM[name].rearrange("p (t h) -> p t h", t=TB)

        def by_block(ap):
            return ap.rearrange("p (t c) -> p t c", t=TB)

        def gdn_mask(name, lv=0):
            at = GDN_AT[name] + P * lv
            return phase_const[:, None, at:at + P].to_broadcast([P, TB, P])

        def gdn_sp(sp):
            load_block(sp, FIRST["gdn_ba"], 0, dram["gdn_ba"][0], 256)
            b = FIRST["gdn"]
            with sp.Fori(0, 16) as i:
                for j in range(4):
                    load_block(sp, b + j, i, dram["gdn"][bass.ds(i * 4 + j, 1)].rearrange("a p n -> (a p) n"), BW)

        def gdn_pe(pe):
            b = FIRST["gdn_ba"]
            pe.wait_ge(S("lo_ready"), b + 1)
            pe.wait_ge(S("bank_free"), b + 4)
            for t in range(TB):
                for k in range(KT):
                    c = k * 32
                    last = product(ps[:, b % 4, t * 32:t * 32 + 32], u_hi[:, k, t * P:(t + 1) * P],
                                   u_lo[:, k, t * P:(t + 1) * P], w_hi[:, b % RING, c:c + 32],
                                   w_lo[:, b % RING, c:c + 32], k == 0, k == KT - 1)
            last.then_inc(S("block_done"), 1)
            for quarter in range(4):
                b = FIRST["gdn"] + 16 * quarter
                pe.wait_ge(S("bank_free"), b + 4)
                for j in range(12):
                    block_matmul(pe, b + j, 0, u_hi, u_lo)
                    if j == 8:
                        for i in range(4):
                            pe.wait_ge(S("gdn_sq"), 4 * quarter + i + 1)
                            nc.tensor.matmul(ps[:, 4 + i, :], ones, GSQ[:, i, :], start=True, stop=True)\
                                .then_inc(S("gdn_sum"), 1)
                    if quarter == 0 and j == 10:
                        gdn_pe_decays(pe)
                for kh in range(2):
                    gdn_pe_pair(pe, quarter, kh)
                pe.wait_ge(S("gdn_o_lo"), 4 * quarter + 4)
                for j in range(12, 16):
                    pe.wait_ge(S("lo_ready"), b + j + 1)
                    if j >= 14:
                        pe.wait_ge(S("bank_free"), b + j + 3)
                    else:
                        pe.wait_ge(S("bank_free"), b + 16)
                    for z in range(2):
                        last = out_tile(ps[:, 2 * (j % 2) + z, :], (b + j) % RING, a_hi, a_lo, 4, 4 * z)
                    last.then_inc(S("block_done"), 1)

        def gdn_pe_decays(pe):
            pe.wait_ge(S("log_decay"), 1)
            pe.wait_ge(S("gdn_const"), 16)
            pe.wait_ge(S("gdn_rstd"), 8)
            for k, at in enumerate((phase_const[:, 0:128], head_ones, phase_const[:, 128:256],
                                    phase_const[:, 256:384])):
                last = nc.tensor.matmul(ps[:, 5, 64 * k:64 * k + 64], at, SM["g"], start=True, stop=True)
            last.then_inc(S("log_decay_sums"), 1)
            pe.wait_ge(S("gc_copied"), 1)
            for src, bank in ((SM["gc"], 6), (SM["beta"], 7)):
                for t in range(TB):
                    last = nc.tensor.transpose(ps[0:16, bank, t * P:(t + 1) * P], src[:, t * 16:(t + 1) * 16], ident)
            last.then_inc(S("head_rows"), 1)

        def gdn_pe_pair(pe, quarter, kh):
            pr = 2 * quarter + kh
            hd = [2 * pr, 2 * pr + 1]
            q, k = by_block(QG[:, kh, :]), by_block(KG[:, kh, :])
            pe.wait_ge(S("gdn_unit"), 4 * quarter + 4)
            pe.wait_ge(S("bank_free"), FIRST["gdn"] + 16 * quarter + 16)
            pe.wait_ge(S("head_rows_copied"), 2)
            if kh:
                pe.wait_ge(S("gdn_o_lo"), 2 * pr)
            for t in range(TB):
                last = nc.tensor.matmul(by_block(ps[:, 0, :])[:, t], k[:, t], k[:, t], start=True, stop=True)
            last.then_inc(S("kk"), 1)
            for t in range(TB):
                last = nc.tensor.matmul(by_block(ps[:, 1, :])[:, t], k[:, t], q[:, t], start=True, stop=True)
            last.then_inc(S("qk"), 1)
            for t in range(TB):
                last = nc.tensor.transpose(by_block(ps[:, 7, :])[:, t], k[:, t], ident)
            last.then_inc(S("k_turned"), 1)
            pe.wait_ge(S("kk_copied"), pr + 1)
            pe.wait_ge(S("qk_copied"), pr + 1)
            for x in range(2):
                pe.wait_ge(S("rows"), 2 * hd[x] + 2)
                nc.tensor.matmul(ps[:, 2 * x, :], ones[0:16, :], slot("row_gc", x)[0:16, :], start=True, stop=True)
                nc.tensor.matmul(ps[:, 2 * x + 1, :], ones[0:16, :], slot("row_beta", x)[0:16, :],
                                 start=True, stop=True).then_inc(S("rows_spread"), 1)
            for x in range(2):
                pe.wait_ge(S(f"xt_ready{x}"), 6 * pr + 1)
                for t in range(TB):
                    last = nc.tensor.transpose(by_block(ps[:, 4 + x, :])[:, t], by_block(slot("xt", x))[:, t], ident)
                last.then_inc(S("x1_turned"), 1)
            for lv in range(1, 6):
                for x in range(2):
                    pe.wait_ge(S(f"c_ready{x}"), 6 * pr + lv + 1)
                    if lv == 1:
                        pe.wait_ge(S("x1_ready"), hd[x] + 1)
                    else:
                        pe.wait_ge(S(f"x_ready{x}"), 4 * pr + lv - 1)
                    pe.wait_ge(S(f"xt_ready{x}"), 6 * pr + lv)
                    for t in range(TB):
                        last = nc.tensor.matmul(by_block(ps[:, 2 * x + 1, :])[:, t], by_block(slot("c", x))[:, t],
                                                by_block(slot("x", x))[:, t], start=True, stop=True)
                    last.then_inc(S(f"cx{x}"), 1)
                for x in range(2):
                    pe.wait_ge(S(f"y_ready{x}"), 5 * pr + lv)
                    y, xt = by_block(slot("y", x)), by_block(slot("xt", x))
                    if lv < 5:
                        for t in range(TB):
                            last = nc.tensor.matmul(by_block(ps[:, 4 + x, :])[:, t], xt[:, t], y[:, t],
                                                    start=True, stop=True)
                    for t in range(TB):
                        last = nc.tensor.matmul(by_block(ps[:, 2 * x + 1, :])[:, t], y[:, t], xt[:, t],
                                                start=True, stop=True)
                    last.then_inc(S(f"xcx{x}"), 1)
            for x in range(2):
                for t in range(TB):
                    last = nc.tensor.transpose(by_block(ps[:, 4 + x, :])[:, t], by_block(VG[:, 2 * kh + x, :])[:, t],
                                               ident)
                last.then_inc(S("v_turned"), 1)
            for x in range(2):
                xt = by_block(slot("xt", x))
                pe.wait_ge(S(f"xt_ready{x}"), 6 * pr + 6)
                pe.wait_ge(S("kbe"), hd[x] + 1)
                for t in range(TB):
                    last = nc.tensor.matmul(by_block(ps[:, 2 * x + 1, :])[:, t], by_block(slot("kbe", x))[:, t],
                                            xt[:, t], start=True, stop=True)
                last.then_inc(S("wt"), 1)
                pe.wait_ge(S("vb"), hd[x] + 1)
                pe.wait_ge(S("egc_row"), hd[x] + 1)
                for t in range(TB):
                    last = nc.tensor.matmul(by_block(ps[:, 2 * x, :])[:, t], xt[:, t], by_block(slot("vb", x))[:, t],
                                            start=True, stop=True)
                last.then_inc(S("u"), 1)
            pe.wait_ge(S("wt_copied"), hd[1] + 1)
            pe.wait_ge(S("u_copied"), hd[1] + 1)
            pe.wait_ge(S("qd"), hd[1] + 1)
            for ch in range(8):
                t, half = divmod(ch, 2)
                lo, hi = 64 * half, 64 * half + 64
                pe.wait_ge(S("state"), 17 * pr + 1 + 2 * ch)
                if ch:
                    pe.wait_ge(S("v_new"), 8 * pr + ch)
                for x in range(2):
                    last = nc.tensor.matmul(ps[lo:hi, 0, x * P:(x + 1) * P], slot("wt", x)[:, ch * 64:ch * 64 + 64],
                                            STATE[:, x * P:(x + 1) * P], start=True, stop=True)
                last.then_inc(S("w_state"), 1)
                for x in range(2):
                    nc.tensor.matmul(ps[:, 4 + x, ch * 64:ch * 64 + 64], STATE[:, x * P:(x + 1) * P],
                                     slot("qd", x)[:, ch * 64:ch * 64 + 64], start=True, stop=False)
                pe.wait_ge(S("v_new"), 8 * pr + ch + 1)
                for x in range(2):
                    nc.tensor.matmul(ps[:, 4 + x, ch * 64:ch * 64 + 64], V_NEW[lo:hi, x * P:(x + 1) * P],
                                     slot("qkt", x)[lo:hi, ch * 64:ch * 64 + 64], start=False, stop=True)
                for x in range(2):
                    last = nc.tensor.matmul(ps[:, 1, x * P:(x + 1) * P], slot("kdec", x)[lo:hi, t * P:(t + 1) * P],
                                            V_NEW[lo:hi, x * P:(x + 1) * P], start=True, stop=True)
                last.then_inc(S("kv_new"), 1)
            for x in range(2):
                pe.wait_ge(S("o_sq"), hd[x] + 1)
                nc.tensor.matmul(ps[:, 2 + x, :], ones, slot("sq", x), start=True, stop=True)\
                    .then_inc(S("o_sum"), 1)

        def gdn_act(act):
            b = FIRST["gdn_ba"]
            lookahead(act, b)
            act.dma_start(phase_const[:, 0:PHASE_W], dram["gdn_const"]).then_inc(S("gdn_const"), 16)
            act.wait_ge(S("block_done"), b + 1)
            nc.scalar.activation(sm_t("beta"), ps[:, b % 4, 0:128].rearrange("p (t c) -> p t c", t=TB)[:, :, 0:16],
                                 ACT.Sigmoid).then_inc(S("beta"), 1)
            nc.scalar.activation(EA, par("a_log", 0, 16), ACT.Exp).then_inc(S("exp_a"), 1)
            act.wait_ge(S("softplus_in"), 1)
            nc.scalar.activation(SM["e"], SM["ax"], ACT.Exp, scale=-1.0).then_inc(S("softplus_exp"), 1)
            act.wait_ge(S("softplus_w"), 1)
            nc.scalar.activation(SM["l"], SM["w"], ACT.Ln).then_inc(S("softplus_ln"), 1)
            for quarter in range(4):
                b = FIRST["gdn"] + 16 * quarter
                for j in range(8):
                    lookahead(act, b + j)
                    act.wait_ge(S("block_done"), b + j + 1)
                    if j >= 2:
                        act.wait_ge(S("gdn_silu"), 8 * quarter + j - 1)
                    elif quarter == 0:
                        act.wait_ge(S("log_decay"), 1)
                    nc.scalar.activation(GCV[:, j % 2, :], ps[:, (b + j) % 4, :], ACT.Copy,
                                         scale=par("gdn_conv", 3 * 32 + 8 * quarter + j)).then_inc(S("gdn_main"), 1)
                    act.wait_ge(S("bank_free"), b + 5 + j)
                    dst = (QG[:, j, :] if j < 2 else KG[:, j - 2, :] if j < 4 else VG[:, j - 4, :])
                    nc.scalar.activation(dst, GCV[:, j % 2, :], ACT.Silu).then_inc(S("gdn_silu"), 1)
                lookahead(act, b + 8)
                qk = [QG[:, 0, :], QG[:, 1, :], KG[:, 0, :], KG[:, 1, :]]
                for i in range(4):
                    act.wait_ge(S("gdn_silu"), 8 * quarter + i + 1)
                    nc.scalar.activation(GSQ[:, i, :], qk[i], ACT.Square).then_inc(S("gdn_sq"), 1)
                lookahead(act, b + 9)
                for i in range(4):
                    act.wait_ge(S("gdn_sum"), 4 * quarter + i + 1)
                    nc.scalar.activation(GHR[:, i, :], ps[:, 4 + i, :], ACT.Ln, bias=eps_col)\
                        .then_inc(S("gdn_rstd"), 1)
                for i in range(4):
                    act.wait_ge(S("gdn_rstd"), 8 * quarter + i + 1)
                    nc.scalar.activation(GHR[:, i, :], GHR[:, i, :], ACT.Exp, scale=-0.5).then_inc(S("gdn_rstd"), 1)
                lookahead(act, b + 10)
                for i in range(4):
                    if i == 3:
                        lookahead(act, b + 11)
                    act.wait_ge(S("block_done"), b + 9 + i)
                    nc.scalar.activation(ZG[:, i, :], ps[:, (b + 8 + i) % 4, :], ACT.Sigmoid)\
                        .then_inc(S("z_gate"), 1)
                if quarter == 0:
                    act.wait_ge(S("kd_ready"), 1)
                    nc.scalar.activation(SM["egc"], SM["gc"], ACT.Exp).then_inc(S("decays"), 1)
                    nc.scalar.activation(SM["ekd"], SM["kd"], ACT.Exp).then_inc(S("decays"), 1)
                    nc.scalar.activation(view(6144 + 64 * 14, 128), ps[:, 5, 128:256], ACT.Exp)\
                        .then_inc(S("decays"), 1)
                for kh in range(2):
                    gdn_act_pair(act, quarter, kh)
                for j in range(12, 16):
                    lookahead(act, b + j)

        def gdn_act_pair(act, quarter, kh):
            pr = 2 * quarter + kh
            hd = [2 * pr, 2 * pr + 1]
            act.wait_ge(S("kk"), pr + 1)
            nc.scalar.activation(KK, ps[:, 0, :], ACT.Copy).then_inc(S("kk_copied"), 1)
            for x in range(2):
                act.wait_ge(S("arg"), hd[x] + 1)
                for t in range(TB):
                    last = nc.scalar.activation(by_block(slot("dt", x))[:, t], by_block(slot("arg", x))[:, t], ACT.Exp,
                                                bias=sm_t("neg_gc")[:, t, hd[x]:hd[x] + 1])
                last.then_inc(S("dt"), 1)
            for x in range(2):
                act.wait_ge(S("x1_turned"), hd[x] + 1)
                nc.scalar.activation(slot("x", x), ps[:, 4 + x, :], ACT.Copy).then_inc(S("x1_ready"), 1)
            for lv in range(1, 6):
                for x in range(2):
                    act.wait_ge(S(f"cx{x}"), 5 * pr + lv)
                    if lv > 1:
                        act.wait_ge(S(f"xcx{x}"), 5 * pr + lv - 1)
                    nc.scalar.activation(slot("y", x), ps[:, 2 * x + 1, :], ACT.Copy).then_inc(S(f"y_ready{x}"), 1)
            for x in range(2):
                act.wait_ge(S(f"x_ready{x}"), 4 * pr + 4)
                act.wait_ge(S(f"cx{x}"), 5 * pr + 5)
                nc.scalar.activation(slot("qd", x), ps[:, 2 * x, :], ACT.Exp).then_inc(S("egc_row"), 1)
            for x in range(2):
                act.wait_ge(S("wt"), hd[x] + 1)
                nc.scalar.activation(slot("wt", x), ps[:, 2 * x + 1, :], ACT.Copy).then_inc(S("wt_copied"), 1)
                act.wait_ge(S("u"), hd[x] + 1)
                nc.scalar.activation(VG[:, 2 * kh + x, :], ps[:, 2 * x, :], ACT.Copy).then_inc(S("u_copied"), 1)
            act.wait_ge(S("kv_new"), 8 * pr + 8)
            for x in range(2):
                nc.scalar.activation(slot("sq", x), ps[:, 4 + x, :], ACT.Square).then_inc(S("o_sq"), 1)
            for x in range(2):
                act.wait_ge(S("o_sum"), hd[x] + 1)
                nc.scalar.activation(slot("rstd", x), ps[:, 2 + x, :], ACT.Ln, bias=eps_col, scale=1.0 / P)\
                    .then_inc(S("o_rstd"), 1)
            for x in range(2):
                act.wait_ge(S("o_rstd"), 4 * pr + x + 1)
                nc.scalar.activation(slot("rstd", x), slot("rstd", x), ACT.Exp, scale=-0.5).then_inc(S("o_rstd"), 1)
            for x in range(2):
                act.wait_ge(S("gated"), hd[x] + 1)
                nc.scalar.activation(a_hi[:, 2 * kh + x, :], slot("gated", x), ACT.Copy).then_inc(S("gdn_o_hi"), 1)

        def gdn_dve(dve):
            b = FIRST["gdn_ba"]
            logits = ps[:, b % 4, 0:128].rearrange("p (t c) -> p t c", t=TB)
            dve.wait_ge(S("beta"), 1)
            nc.vector.tensor_tensor(sm_t("xa"), logits[:, :, 16:32],
                                    par("dt_bias", 0, 16)[:, None, :].to_broadcast([P, TB, 16]), ALU.add)\
                .then_inc(S("bank_free"), 1)
            dve.wait_ge(S("bank_free"), b + 5)
            link(dve, nc.vector.tensor_scalar(SM["w"], SM["xa"], -1.0, None, ALU.mult))
            nc.vector.tensor_tensor(SM["ax"], SM["xa"], SM["w"], ALU.max).then_inc(S("softplus_in"), 1)
            dve.wait_ge(S("softplus_exp"), 1)
            nc.vector.tensor_scalar(SM["w"], SM["e"], 1.0, None, ALU.add).then_inc(S("softplus_w"), 1)
            dve.wait_ge(S("softplus_w"), 1)
            link(dve, nc.vector.tensor_scalar(SM["w1"], SM["w"], -1.0, None, ALU.add))
            link(dve, nc.vector.tensor_tensor(SM["w1"], SM["e"], SM["w1"], ALU.subtract))
            link(dve, nc.vector.reciprocal(SM["kd"], SM["w"]))
            link(dve, nc.vector.tensor_tensor(SM["w1"], SM["w1"], SM["kd"], ALU.mult))
            dve.wait_ge(S("softplus_ln"), 1)
            link(dve, nc.vector.tensor_tensor(SM["l"], SM["l"], SM["w1"], ALU.add))
            link(dve, nc.vector.tensor_scalar(SM["xa"], SM["xa"], 0.0, None, ALU.max))
            link(dve, nc.vector.tensor_tensor(SM["l"], SM["l"], SM["xa"], ALU.add))
            dve.wait_ge(S("exp_a"), 1)
            link(dve, nc.vector.tensor_tensor(sm_t("g"), sm_t("l"), EA[:, None, :].to_broadcast([P, TB, 16]),
                                              ALU.mult))
            nc.vector.tensor_scalar(SM["g"], SM["g"], -1.0, None, ALU.mult).then_inc(S("log_decay"), 1)
            for quarter in range(4):
                b = FIRST["gdn"] + 16 * quarter
                for j in range(8):
                    dve.wait_ge(S("gdn_main"), 8 * quarter + j + 1)
                    for tap in (2, 1, 0):
                        s = 3 - tap
                        ins = nc.vector.scalar_tensor_tensor(
                            out=GCV[:, j % 2, s:T], in0=ps[:, (b + j) % 4, 0:T - s],
                            scalar=par("gdn_conv", 32 * tap + 8 * quarter + j), in1=GCV[:, j % 2, s:T],
                            op0=ALU.mult, op1=ALU.add)
                        if tap:
                            link(dve, ins)
                        else:
                            ins.then_inc(S("bank_free"), 1)
                qk = [QG[:, 0, :], QG[:, 1, :], KG[:, 0, :], KG[:, 1, :]]
                for i in range(4):
                    dve.wait_ge(S("gdn_rstd"), 8 * quarter + 5 + i)
                    nc.vector.scalar_tensor_tensor(out=qk[i], in0=qk[i], scalar=P ** -0.5 if i < 2 else 1.0,
                                                   in1=GHR[:, i, :], op0=ALU.mult, op1=ALU.mult)\
                        .then_inc(S("gdn_unit"), 1)
                if quarter == 0:
                    dve.wait_ge(S("log_decay_sums"), 1)
                    nc.vector.tensor_copy(SM["gc"], ps[:, 5, 0:64]).then_inc(S("gc_copied"), 1)
                    dve.wait_ge(S("gc_copied"), 1)
                    link(dve, nc.vector.tensor_scalar(SM["neg_gc"], SM["gc"], -1.0, None, ALU.mult))
                    nc.vector.tensor_tensor(SM["kd"], ps[:, 5, 64:128], SM["gc"], ALU.subtract)\
                        .then_inc(S("kd_ready"), 1)
                    dve.wait_ge(S("head_rows"), 1)
                    nc.vector.tensor_copy(GCT[0:16, :], ps[0:16, 6, :]).then_inc(S("head_rows_copied"), 1)
                    nc.vector.tensor_copy(BT[0:16, :], ps[0:16, 7, :]).then_inc(S("head_rows_copied"), 1)
                    dve.wait_ge(S("head_rows_copied"), 2)
                    dve.wait_ge(S("decays"), 3)
                    link(dve, nc.vector.tensor_tensor(SM["beg"], SM["beta"], SM["egc"], ALU.mult))
                for i in range(4):
                    dve.wait_ge(S("z_gate"), 4 * quarter + i + 1)
                    nc.vector.tensor_tensor(ZG[:, i, :], ZG[:, i, :], ps[:, (b + 8 + i) % 4, :], ALU.mult)\
                        .then_inc(S("bank_free"), 1)
                for kh in range(2):
                    gdn_dve_pair(dve, quarter, kh)
                for j in range(12, 16):
                    dve.wait_ge(S("block_done"), b + j + 1)
                    at = h[:, 2 * (j - 12):2 * (j - 12) + 2, :]
                    src = ps[:, 2 * (j % 2):2 * (j % 2) + 2, :]
                    dve.wait_ge(S("bank_free"), b + j + 4)
                    nc.vector.tensor_tensor(at, at, src, ALU.add).then_inc(S("bank_free"), 1)

        def gdn_dve_pair(dve, quarter, kh):
            pr = 2 * quarter + kh
            hd = [2 * pr, 2 * pr + 1]
            ident_all = common[:, None, 0:128].to_broadcast([P, TB, P])

            def col(name, x):
                return sm_t(name)[:, :, hd[x]:hd[x] + 1].to_broadcast([P, TB, P])

            if pr:
                dve.wait_ge(S("gdn_o_lo"), hd[0])
            dve.wait_ge(S("gdn_unit"), 4 * quarter + 4)
            nc.vector.memset(STATE, 0.0).then_inc(S("state"), 1)
            for x in range(2):
                for src, name in ((GCT, "row_gc"), (BT, "row_beta")):
                    nc.vector.tensor_scalar(slot(name, x)[0:16, :], src[0:16, :], common[0:16, hd[x]:hd[x] + 1],
                                            None, ALU.mult).then_inc(S("rows"), 1)
            dve.wait_ge(S("qk"), pr + 1)
            nc.vector.tensor_copy(QK, ps[:, 1, :]).then_inc(S("qk_copied"), 1)
            for x in range(2):
                dve.wait_ge(S("rows_spread"), hd[x] + 1)
                nc.vector.tensor_tensor(by_block(slot("arg", x)), by_block(ps[:, 2 * x, :]), gdn_mask("decay_mask"),
                                        ALU.add).then_inc(S("arg"), 1)
            dve.wait_ge(S("kk_copied"), pr + 1)
            dve.wait_ge(S("qk_copied"), pr + 1)
            for x in range(2):
                dve.wait_ge(S("dt"), hd[x] + 1)
                link(dve, nc.vector.tensor_tensor(slot("mt", x), KK, slot("dt", x), ALU.mult))
                link(dve, nc.vector.tensor_tensor(slot("mt", x), slot("mt", x), ps[:, 2 * x + 1, :], ALU.mult))
                nc.vector.tensor_tensor(slot("qkt", x), QK, slot("dt", x), ALU.mult).then_inc(S("qkt"), 1)
                nc.vector.tensor_tensor(by_block(slot("c", x)), by_block(slot("mt", x)), gdn_mask("levels", 0),
                                        ALU.mult).then_inc(S(f"c_ready{x}"), 1)
                dve.wait_ge(S(f"c_ready{x}"), 6 * pr + 1)
                nc.vector.tensor_tensor(by_block(slot("xt", x)), ident_all, by_block(slot("c", x)), ALU.subtract)\
                    .then_inc(S(f"xt_ready{x}"), 1)
                dve.wait_ge(S(f"xt_ready{x}"), 6 * pr + 1)
                nc.vector.tensor_tensor(by_block(slot("c", x)), by_block(slot("mt", x)), gdn_mask("levels", 1),
                                        ALU.mult).then_inc(S(f"c_ready{x}"), 1)
            for lv in range(1, 6):
                for x in range(2):
                    if lv < 5:
                        dve.wait_ge(S(f"cx{x}"), 5 * pr + lv)
                        nc.vector.tensor_tensor(by_block(slot("c", x)), by_block(slot("mt", x)),
                                                gdn_mask("levels", lv + 1), ALU.mult)\
                            .then_inc(S(f"c_ready{x}"), 1)
                    dve.wait_ge(S(f"xcx{x}"), 5 * pr + lv)
                    if lv < 5:
                        if lv == 1:
                            dve.wait_ge(S("x1_ready"), hd[x] + 1)
                        else:
                            dve.wait_ge(S(f"x_ready{x}"), 4 * pr + lv - 1)
                        nc.vector.tensor_tensor(slot("x", x), slot("x", x), ps[:, 4 + x, :], ALU.subtract)\
                            .then_inc(S(f"x_ready{x}"), 1)
                    dve.wait_ge(S(f"xt_ready{x}"), 6 * pr + lv)
                    nc.vector.tensor_tensor(slot("xt", x), slot("xt", x), ps[:, 2 * x + 1, :], ALU.subtract)\
                        .then_inc(S(f"xt_ready{x}"), 1)
            dve.wait_ge(S("qkt"), 2 * pr + 2)
            for x in range(2):
                k_tok = by_block(ps[:, 7, :])
                dve.wait_ge(S("k_turned"), pr + 1)
                dve.wait_ge(S(f"xcx{x}"), 5 * pr + 5)
                nc.vector.tensor_tensor(by_block(slot("kbe", x)), k_tok, col("beg", x), ALU.mult)\
                    .then_inc(S("kbe"), 1)
                dve.wait_ge(S("v_turned"), hd[x] + 1)
                nc.vector.tensor_tensor(by_block(slot("vb", x)), by_block(ps[:, 4 + x, :]), col("beta", x), ALU.mult)\
                    .then_inc(S("vb"), 1)
                nc.vector.tensor_tensor(by_block(slot("kdec", x)), k_tok, col("ekd", x), ALU.mult)\
                    .then_inc(S("kdec"), 1)
                dve.wait_ge(S("egc_row"), hd[x] + 1)
                nc.vector.tensor_tensor(slot("qd", x), slot("qd", x), QG[:, kh, :], ALU.mult).then_inc(S("qd"), 1)
            for ch in range(8):
                t, half = divmod(ch, 2)
                lo, hi = 64 * half, 64 * half + 64
                if ch == 0:
                    dve.wait_ge(S("u_copied"), 2 * pr + 2)
                dve.wait_ge(S("w_state"), 8 * pr + ch + 1)
                u = VG[lo:hi, 2 * kh:2 * kh + 2, t * P:(t + 1) * P]
                nc.vector.tensor_tensor(V_NEW[lo:hi, :].rearrange("p (x d) -> p x d", x=2), u,
                                        ps[lo:hi, 0, 0:256].rearrange("p (x d) -> p x d", x=2), ALU.subtract)\
                    .then_inc(S("v_new"), 1)
                dve.wait_ge(S("kv_new"), 8 * pr + ch + 1)
                for x in range(2):
                    dve.wait_ge(S("state"), 17 * pr + 1 + 2 * ch)
                    col_at = t * 16 + hd[x]
                    nc.vector.scalar_tensor_tensor(
                        out=STATE[:, x * P:(x + 1) * P], in0=STATE[:, x * P:(x + 1) * P],
                        scalar=SM[f"gl{half}"][:, col_at:col_at + 1], in1=ps[:, 1, x * P:(x + 1) * P],
                        op0=ALU.mult, op1=ALU.add).then_inc(S("state"), 1)
            for x in range(2):
                dve.wait_ge(S("o_rstd"), 4 * pr + 3 + x)
                link(dve, nc.vector.scalar_tensor_tensor(out=slot("gated", x), in0=ps[:, 4 + x, :],
                                                         scalar=par("gdn_norm"), in1=slot("rstd", x),
                                                         op0=ALU.mult, op1=ALU.mult))
                nc.vector.tensor_tensor(slot("gated", x), slot("gated", x), ZG[:, 2 * kh + x, :], ALU.mult)\
                    .then_inc(S("gated"), 1)
                dve.wait_ge(S("gdn_o_hi"), hd[x] + 1)
                nc.vector.tensor_tensor(a_lo[:, 2 * kh + x, :], slot("gated", x),
                                        a_hi[:, 2 * kh + x, :].bitcast(F32), ALU.subtract)\
                    .then_inc(S("gdn_o_lo"), 1)

        def ada_bias_dve(dve, layer):
            at, n = layer * N_ADA // 2, N_ADA // 2
            dve.wait_ge(S("ada_free"), 2 + at + n)
            link(dve, nc.vector.tensor_tensor(mod[:, at:at + n], ADA[:, at:at + n], par("b_ada", at, n), ALU.add))

        def modulation_dve(dve):
            for v, name in enumerate(("g_ffn1", "g_mix", "g_ffn2")):
                link(dve, nc.vector.scalar_tensor_tensor(
                    out=gains[:, v * KT:(v + 1) * KT], in0=mod[:, (3 * v + 1) * KT:(3 * v + 2) * KT], scalar=1.0,
                    in1=par(name, 0, KT), op0=ALU.add, op1=ALU.mult))
            for v in (2, 8):
                at = mod[:, v * KT:(v + 1) * KT]
                link(dve, nc.vector.tensor_scalar(at, at, 0.5, None, ALU.mult))

        FINAL = view(2560, KT, T)

        def final_dve(dve):
            dve.wait_ge(S("rstd_ready"), 16)
            for k in range(KT):
                nc.vector.scalar_tensor_tensor(out=FINAL[:, k, :], in0=h[:, k, :], scalar=par("g_final", k),
                                               in1=RSTD, op0=ALU.mult, op1=ALU.mult).then_inc(S("final_ready"), 1)

        def mat(at, n, dt):
            return arena[:, at:at + n // 2].bitcast(dt)

        QA = view(0, T, 4)
        KA, VA, WI = view(2048, T), view(2560, TB, 64), view(2816, TB, 8)
        QI, KI = view(2848, 4, T), view(4896, T)
        QNOPE, QP, KN, VB, KP = view(5408, 4, T), view(7456, 2, T), view(8480, 4, T), view(10528, TB, T), view(12576, T)
        COS2, SIN2 = view(13088, T), view(13600, T)
        ROPE2_SCRATCH = 14112
        POS = view(14112, T)
        TURN1, TURN2 = view(14624, T), view(15136, T)
        LAT = view(5408, 5, T)
        LSQ, LRSTD, LNT = view(8480, 2, T), view(9504, 2, T), view(10528, 2, T)
        RELU, TOP = view(13088, 2, T), view(15776, 8)
        ACC = {1: view(14624, 2 * P), 2: view(14624 + 2 * P, 3 * P), 3: view(14624 + 5 * P, 4 * P)}
        PENAL = mat(3360, TB * T, BF16).rearrange("p (n k) -> p n k", n=TB)
        REP, REP_RAW = mat(2848, KT * P, BF16), view(13088, KT * P)
        QCOL, DELTA, TABLE = view(4896, P), view(5024, 8), view(5040, P)
        LIMIT_BF, IDENT_BF = mat(5168, P, BF16), mat(5232, P, BF16)
        PR, PT = view(13088, 2, T), view(14624, 2, T)
        ST = view(15784, 2, 4)
        LIMIT = phase_const[:, MIX_AT["limit"]:MIX_AT["limit"] + P]
        THRESHOLD = phase_const[:, MIX_AT["thresholds"]:MIX_AT["thresholds"] + 1]
        MLA_SCALE = 96 ** -0.5
        TAKEN = -3e38
        UNITS = 64

        def unit(u):
            return u >= 32, u % 32 // 8, u % 8

        def mix_sp(sp):
            load_block(sp, FIRST["mix_v"], 0, dram["mix_v"][0], 576)
            b = FIRST["mix_in"]
            with sp.Fori(0, 4) as i:
                for j in range(4):
                    load_block(sp, b + j, i, dram["mix_in"][bass.ds(i * 4 + j, 1)].rearrange("a p n -> (a p) n"), BW)
            for j in range(3):
                load_block(sp, FIRST["uq"] + j, 0, dram["uq"][j], 768)
            for j in range(2):
                load_block(sp, FIRST["ukv"] + j, 0, dram["ukv"][j], BW)
            b = FIRST["mix_out"]
            with sp.Fori(0, 2) as i:
                for j in range(12):
                    load_block(sp, b + j, i * 3, dram["mix_out"][bass.ds(i * 12 + j, 1)]
                               .rearrange("a p n -> (a p) n"), BW)
            b = FIRST["w_out"]
            with sp.Fori(0, 2) as i:
                for j in range(4):
                    load_block(sp, b + j, i, dram["w_out"][bass.ds(i * 4 + j, 1)].rearrange("a p n -> (a p) n"), BW)

        def mix_pe(pe):
            b = FIRST["mix_v"]
            pe.wait_ge(S("lo_ready"), b + 1)
            pe.wait_ge(S("bank_free"), b + 1)
            for t in range(TB):
                for k in range(KT):
                    c = k * 72
                    last = product(ps[:, b % 4, t * 72:t * 72 + 72], u_hi[:, k, t * P:(t + 1) * P],
                                   u_lo[:, k, t * P:(t + 1) * P], w_hi[:, b % RING, c:c + 72],
                                   w_lo[:, b % RING, c:c + 72], k == 0, k == KT - 1)
            last.then_inc(S("block_done"), 1)
            b = FIRST["mix_in"]
            with pe.Fori(0, 4) as i:
                for j in range(4):
                    block_matmul(pe, b + j, i, u_hi, u_lo)
            for i in range(5):
                pe.wait_ge(S("lat_sq"), i + 1)
                nc.tensor.matmul(ps[:, 4 + (i >= 3), :], ones, LSQ[:, i % 2, :], start=i in (0, 3), stop=i in (2, 4))\
                    .then_inc(S("lat_sum"), 1)
            b = FIRST["uq"]
            pe.wait_ge(S("bank_free"), b + 4)
            for j in range(3):
                pe.wait_ge(S("lat_lo"), 3)
                pe.wait_ge(S("lo_ready"), b + j + 1)
                if j == 2:
                    pe.wait_ge(S("bank_free"), b + 5)
                for z in range(2):
                    last = out_tile(ps[:, 2 * (j % 2) + z, :], (b + j) % RING, a_hi, a_lo, 3, 3 * z)
                last.then_inc(S("block_done"), 1)
            b = FIRST["ukv"]
            pe.wait_ge(S("lat_lo"), 5)
            pe.wait_ge(S("lo_ready"), b + 1)
            for z in range(4):
                last = out_tile(ps[:, 4 + z, :], b % RING, a_hi, a_lo, 2, 2 * z, 3)
            last.then_inc(S("block_done"), 1)
            b += 1
            pe.wait_ge(S("lo_ready"), b + 1)
            pe.wait_ge(S("bank_free"), b + 3)
            for t in range(TB):
                for k in range(2):
                    last = product(ps[:, t, :], a_hi[:, 3 + k, t * P:(t + 1) * P], a_lo[:, 3 + k, t * P:(t + 1) * P],
                                   w_hi[:, b % RING, k * T:(k + 1) * T], w_lo[:, b % RING, k * T:(k + 1) * T],
                                   k == 0, k == 1)
            last.then_inc(S("block_done"), 1)
            pe.wait_ge(S("bank_free"), b + 5)
            pe.wait_ge(S("mix_const"), 16)
            for i, src in enumerate((KP, QP[:, 0, :], QP[:, 1, :])):
                nc.tensor.matmul(ps[:, 4 + i, :], ROTM, src, start=True, stop=True).then_inc(S("turned2"), 1)
            for v in range(24):
                n, hd = v // 8 + 1, v % 8
                o = 64 * (hd % 2)
                if v >= 4:
                    pe.wait_ge(S("idx_relu"), v - 3)
                nc.tensor.matmul(ps[:, v % 4, 0:(n + 1) * P], QI[o:o + 64, hd // 2, n * P:(n + 1) * P],
                                 KI[o:o + 64, 0:(n + 1) * P], start=True, stop=True).then_inc(S("idx_scored"), 1)

            def scores(u):
                latent, n, m = unit(u)
                w = (n + 1) * P
                dst = ps[:, u % 2, 0:w]
                if u >= 2:
                    pe.wait_ge(S("att_exp"), u - 1)
                if latent:
                    o, r = 64 * (m % 2), 32 * (m % 4)
                    nc.tensor.matmul(dst, QNOPE[o:o + 64, m // 2, n * P:(n + 1) * P], KN[o:o + 64, m // 2, 0:w],
                                     start=True, stop=False, skip_group_check=True)
                    nc.tensor.matmul(dst, QP[r:r + 32, m // 4, n * P:(n + 1) * P], KP[r:r + 32, 0:w],
                                     start=False, stop=False, skip_group_check=True)
                    nc.tensor.matmul(ps[:, u % 2, n * P:w], IDENT_BF, LIMIT_BF, start=False, stop=True,
                                     skip_group_check=True).then_inc(S("att_scored"), 1)
                    return
                pe.wait_ge(S("penal"), n + 1)
                nc.tensor.matmul(dst, REP[:, m * P:(m + 1) * P], PENAL[:, n, 0:w], start=True, stop=False,
                                 skip_group_check=True)
                tok = n * P + m * 16
                for z in range(2):
                    nc.tensor.matmul(ps[64 * z:64 * z + 64, u % 2, 0:w],
                                     QA[64 * z:64 * z + 64, tok:tok + 16, :].rearrange("p t h -> p (t h)"),
                                     KA[64 * z:64 * z + 64, 0:w], start=False, stop=False, skip_group_check=True)
                for j in range(4):
                    pe.wait_ge(S("steps"), 4 * u + j + 1)
                    nc.tensor.matmul(dst, table_hi[:, j, :], onehot[:, j % 2, 0:w], start=False, stop=False,
                                     skip_group_check=True)
                    last = nc.tensor.matmul(dst, table_lo[:, j, :], onehot[:, j % 2, 0:w], start=False, stop=j == 3,
                                            skip_group_check=True)
                    if j < 3:
                        last.then_inc(S("steps_used"), 1)
                last.then_inc(S("att_scored"), 1)

            def values(u):
                latent, n, m = unit(u)
                pe.wait_ge(S("att_pt"), u + 1)
                if m == 0 and u >= 16:
                    pe.wait_ge(S("att_lo"), u // 8 - 1)
                bank = 4 + u // 8 % 2
                for kb in range(n + 1):
                    if latent:
                        o, hp = 64 * (m % 2), m // 2
                        last = nc.tensor.matmul(ps[o:o + 64, bank, hp * P:(hp + 1) * P], VB[:, kb, m * 64:m * 64 + 64],
                                                PT[:, u % 2, kb * P:(kb + 1) * P], start=kb == 0, stop=kb == n)
                if not latent:
                    for z in range(2):
                        for kb in range(n + 1):
                            last = nc.tensor.matmul(ps[64 * z:64 * z + 64, bank, m * 64:m * 64 + 64], VA[:, kb, :],
                                                    PT[:, u % 2, kb * P + 64 * z:kb * P + 64 * z + 64],
                                                    start=kb == 0, stop=kb == n)
                last.then_inc(S("att_pv"), 1)

            pe.wait_ge(S("rep_ready"), 1)
            pe.wait_ge(S("tables"), 1)
            pe.wait_ge(S("roped2"), 3)
            pe.wait_ge(S("idx_relu"), 24)
            scores(0)
            for u in range(UNITS):
                if u + 1 < UNITS:
                    scores(u + 1)
                pe.wait_ge(S("att_probs"), u + 1)
                if u >= 2:
                    pe.wait_ge(S("att_pt"), u - 1)
                for kb in range(unit(u)[1] + 1):
                    last = nc.tensor.transpose(ps[:, 2 + u % 2, kb * P:(kb + 1) * P],
                                               PR[:, u % 2, kb * P:(kb + 1) * P], ident)
                last.then_inc(S("att_turned"), 1)
                if u:
                    values(u - 1)
            values(UNITS - 1)
            pe.wait_ge(S("att_lo"), 8)
            b = FIRST["mix_out"]
            with pe.Fori(0, 2) as i:
                for j in range(4):
                    c, bank = b + 3 * j, 4 * (j % 2)
                    pe.wait_ge(S("bank_free"), num(c, i * 3, 1))
                    for z in range(2):
                        pe.wait_ge(S("lo_ready"), num(c + z, i * 3, 1))
                        out_tile(ps[:, bank + z, :], (c + z) % RING, u_hi, u_lo, KT).then_inc(S("block_done"), 1)
                    pe.wait_ge(S("lo_ready"), num(c + 2, i * 3, 1))
                    out_tile(ps[:, bank + 2, :], (c + 2) % RING, a_hi, a_lo, 4)
                    out_tile(ps[:, bank + 3, :], (c + 2) % RING, a_hi, a_lo, 4, 4, 4).then_inc(S("block_done"), 1)
            pe.wait_ge(S("y_lo"), KT)
            b = FIRST["w_out"]
            with pe.Fori(0, 2) as i:
                for j in range(4):
                    block_matmul(pe, b + j, i, a_hi, a_lo)

        GATES, PROD, Y = view(0, 2, 2, T), view(2048, 2, 2, T), view(4096, KT, T)

        def mix_act(act):
            for base in range(FIRST["mix_v"], FIRST["mix_out"]):
                lookahead(act, base)
                if base < FIRST["uq"]:
                    continue
                if base == FIRST["uq"]:
                    for i in range(5):
                        act.wait_ge(S("bank_free"), FIRST["mix_in"] + 10 + i + 5)
                        if i >= 2:
                            act.wait_ge(S("lat_sum"), i - 1)
                        nc.scalar.activation(LSQ[:, i % 2, :], LAT[:, i, :], ACT.Square).then_inc(S("lat_sq"), 1)
                    for i in range(2):
                        act.wait_ge(S("lat_sum"), 3 + 2 * i)
                        nc.scalar.activation(LRSTD[:, i, :], ps[:, 4 + i, :], ACT.Ln, bias=eps_col,
                                             scale=1.0 / (384, 256)[i]).then_inc(S("lat_rstd"), 1)
                    for i in range(2):
                        act.wait_ge(S("lat_rstd"), 1 + i)
                        nc.scalar.activation(LRSTD[:, i, :], LRSTD[:, i, :], ACT.Exp, scale=-0.5)\
                            .then_inc(S("lat_rstd"), 1)
                    for i in range(5):
                        act.wait_ge(S("lat_normed"), i + 1)
                        nc.scalar.activation(a_hi[:, i, :], LNT[:, i % 2, :], ACT.Copy).then_inc(S("lat_hi"), 1)
            for v in range(24):
                act.wait_ge(S("idx_scored"), v + 1)
                if v >= 2:
                    act.wait_ge(S("idx_acc"), v - 1)
                w = (v // 8 + 2) * P
                if v == 0:
                    act.wait_ge(S("roped2"), 3)
                nc.scalar.activation(RELU[:, v % 2, 0:w], ps[:, v % 4, 0:w], ACT.Relu, scale=0.125)\
                    .then_inc(S("idx_relu"), 1)
            act.wait_ge(S("idx_acc"), 24)
            act.dma_start(REP_RAW, dram["rep_const"]).then_inc(S("rep_landed"), 16)
            act.wait_ge(S("rep_landed"), 16)
            nc.scalar.activation(REP, REP_RAW, ACT.Copy).then_inc(S("rep_ready"), 1)

            def exps(u):
                w = (unit(u)[1] + 1) * P
                act.wait_ge(S("att_max"), u + 1)
                if u >= 2:
                    act.wait_ge(S("att_turned"), u - 1)
                nc.scalar.activation(PR[:, u % 2, 0:w], ps[:, u % 2, 0:w], ACT.Exp, bias=ST[:, u % 2, 1:2],
                                     scale=MLA_SCALE if unit(u)[0] else 1.0, accum_out=ST[:, u % 2, 2:3])\
                    .then_inc(S("att_exp"), 1)

            def heads_out(blk):
                act.wait_ge(S("att_pv"), 8 * blk + 8)
                dst, src = out_heads(blk)
                nc.scalar.activation(dst(a_hi), src, ACT.Copy).then_inc(S("att_hi"), 1)

            act.wait_ge(S("rep_ready"), 1)
            exps(0)
            for u in range(UNITS):
                if u + 1 < UNITS:
                    exps(u + 1)
                act.wait_ge(S("att_turned"), u + 1)
                if u >= 2:
                    act.wait_ge(S("att_pv"), u - 1)
                w = (unit(u)[1] + 1) * P
                nc.scalar.activation(PT[:, u % 2, 0:w], ps[:, 2 + u % 2, 0:w], ACT.Copy).then_inc(S("att_pt"), 1)
                if u and u % 8 == 0:
                    heads_out(u // 8 - 1)
            heads_out(7)
            b = FIRST["mix_out"]
            with act.Fori(0, 2) as i:
                for j in range(4):
                    c, bank = b + 3 * j, 4 * (j % 2)
                    for z in range(2):
                        lookahead(act, c + z, i * 3)
                        act.wait_ge(S("block_done"), num(c + z, i * 3, 1))
                        act.wait_ge(S("bank_free"), num(c, i * 3, 1))
                        nc.scalar.activation(GATES[:, j % 2, z, :], ps[:, bank + z, :], ACT.Sigmoid)\
                            .then_inc(S("gate2"), 1)
                    lookahead(act, c + 2, i * 3)
            act.wait_ge(S("bank_free"), FIRST["w_out"] + 4)
            for k in range(KT):
                nc.scalar.activation(a_hi[:, k, :], Y[:, k, :], ACT.Copy).then_inc(S("y_hi"), 1)
            b = FIRST["w_out"]
            with act.Fori(0, 2) as i:
                for j in range(4):
                    lookahead(act, b + j, i)

        def out_heads(blk):
            n, bank = blk % 4, 4 + blk % 2
            at = 4 if blk >= 4 else 0
            order = "p (h t) -> p h t" if blk >= 4 else "p (t h) -> p h t"
            return lambda a: a[:, at:at + 4, n * P:(n + 1) * P], ps[:, bank, :].rearrange(order, h=4)

        def mix_dve(dve):
            b = FIRST["mix_v"]
            dve.wait_ge(S("block_done"), b + 1)
            src = ps[:, b % 4, 0:288].rearrange("p (t c) -> p t c", t=TB)
            link(dve, nc.vector.tensor_copy(VA, src[:, :, 0:64]))
            nc.vector.tensor_scalar(WI, src[:, :, 64:72], 8 ** -0.5, None, ALU.mult).then_inc(S("bank_free"), 1)
            b = FIRST["mix_in"]
            for j in range(16):
                dve.wait_ge(S("block_done"), b + j + 1)
                src = ps[:, (b + j) % 4, :]
                if j < 4:
                    nc.vector.tensor_scalar(QA[:, :, j:j + 1], src[:, :, None], 0.125, None, ALU.mult)\
                        .then_inc(S("bank_free"), 1)
                    continue
                dst = KA if j == 4 else QI[:, j - 5, :] if j < 9 else KI if j == 9 else \
                    LAT[:, j - 10, :] if j < 15 else KP
                nc.vector.tensor_copy(dst, src).then_inc(S("bank_free"), 1)
            for i in range(5):
                dve.wait_ge(S("bank_free"), b + 5 + 15)
                dve.wait_ge(S("lat_rstd"), 3 + (i >= 3))
                if i >= 2:
                    dve.wait_ge(S("lat_hi"), i - 1)
                    dve.wait_ge(S("lat_lo"), i - 1)
                nc.vector.scalar_tensor_tensor(out=LNT[:, i % 2, :], in0=LAT[:, i, :],
                                               scalar=par("g_cq", i) if i < 3 else par("g_ckv", i - 3),
                                               in1=LRSTD[:, int(i >= 3), :], op0=ALU.mult, op1=ALU.mult)\
                    .then_inc(S("lat_normed"), 1)
                dve.wait_ge(S("lat_normed"), i + 1)
                dve.wait_ge(S("lat_hi"), i + 1)
                nc.vector.tensor_tensor(a_lo[:, i, :], LNT[:, i % 2, :], a_hi[:, i, :].bitcast(F32), ALU.subtract)\
                    .then_inc(S("lat_lo"), 1)
            b = FIRST["uq"]
            dve.wait_ge(S("lat_lo"), 5)
            for j in range(3):
                dve.wait_ge(S("block_done"), b + j + 1)
                dst = QNOPE[:, 2 * j:2 * j + 2, :] if j < 2 else QP
                nc.vector.tensor_copy(dst, ps[:, 2 * (j % 2):2 * (j % 2) + 2, :]).then_inc(S("bank_free"), 1)
            b = FIRST["ukv"]
            dve.wait_ge(S("block_done"), b + 1)
            nc.vector.tensor_copy(KN, ps[:, 4:8, :]).then_inc(S("bank_free"), 1)
            dve.wait_ge(S("block_done"), b + 2)
            nc.vector.tensor_copy(VB, ps[:, 0:4, :]).then_inc(S("bank_free"), 1)
            dve.wait_ge(S("bank_free"), b + 6)
            dve.wait_ge(S("rope_table"), 4)
            for i, at in enumerate((KP, QP[:, 0, :], QP[:, 1, :])):
                dve.wait_ge(S("turned2"), i + 1)
                link(dve, nc.vector.tensor_tensor(TURN1, at, COS2, ALU.mult))
                link(dve, nc.vector.tensor_tensor(TURN2, ps[:, 4 + i, :], SIN2, ALU.mult))
                nc.vector.tensor_tensor(at, TURN1, TURN2, ALU.add).then_inc(S("roped2"), 1)
                dve.wait_ge(S("roped2"), i + 1)
            dve.wait_ge(S("mix_const"), 16)
            for n in range(1, 4):
                w = (n + 1) * P
                acc = ACC[n]
                for hd in range(8):
                    v = 8 * (n - 1) + hd
                    dve.wait_ge(S("idx_relu"), v + 1)
                    if hd == 0:
                        nc.vector.tensor_scalar(acc, RELU[:, v % 2, 0:w], WI[:, n, 0:1], None, ALU.mult)\
                            .then_inc(S("idx_acc"), 1)
                    else:
                        nc.vector.scalar_tensor_tensor(out=acc, in0=RELU[:, v % 2, 0:w], scalar=WI[:, n, hd:hd + 1],
                                                       in1=acc, op0=ALU.mult, op1=ALU.add)\
                            .then_inc(S("idx_acc"), 1)
                    dve.wait_ge(S("idx_acc"), v + 1)
            nc.vector.tensor_copy(PENAL[:, 0, 0:P], LIMIT).then_inc(S("penal"), 1)
            for n in range(1, 4):
                w = (n + 1) * P
                acc = ACC[n]
                link(dve, nc.vector.tensor_tensor(acc[:, n * P:w], acc[:, n * P:w], LIMIT, ALU.add))
                for _ in range(P // 8):
                    link(dve, nc.vector.max(out=TOP, in_=acc))
                    link(dve, nc.vector.match_replace(out=acc, in_to_replace=TOP, in_values=acc, imm_value=TAKEN))
                nc.vector.tensor_scalar(PENAL[:, n, 0:w], acc, TAKEN / 1.5, -BIG, ALU.is_gt, ALU.mult)\
                    .then_inc(S("penal"), 1)
                dve.wait_ge(S("penal"), n + 1)
            for q in range(4):
                r = 32 * q
                last = nc.vector.tensor_scalar(QCOL[r:r + 32, :, None],
                                               POS[r:r + 32, :].rearrange("p (c i) -> p c i", i=4)[:, :, q:q + 1],
                                               THRESHOLD[r:r + 32, :], None, ALU.add)
                link(dve, last)
            link(dve, nc.vector.tensor_tensor(DELTA, par("rel_at", 0, 8), par("rel_before", 0, 8), ALU.subtract))
            for j in range(4):
                at = MIX_AT["query_of_row"] + j * P
                for z in range(2):
                    delta = DELTA.rearrange("p (h z) -> p z h", z=2)[:, z:z + 1, :].to_broadcast([P, 16, 4])
                    link(dve, nc.vector.tensor_tensor(
                        TABLE[:, 64 * z:64 * z + 64].rearrange("p (q h) -> p q h", h=4), delta,
                        phase_const[:, at + 64 * z:at + 64 * z + 64].rearrange("p (q h) -> p q h", h=4), ALU.mult))
                link(dve, nc.vector.tensor_copy(table_hi[:, j, :], TABLE))
                link(dve, nc.vector.tensor_tensor(table_lo[:, j, :], TABLE, table_hi[:, j, :].bitcast(F32),
                                                  ALU.subtract))
            link(dve, nc.vector.tensor_copy(LIMIT_BF, LIMIT))
            nc.vector.tensor_copy(IDENT_BF, ident).then_inc(S("tables"), 1)

            def steps(u):
                latent, n, m = unit(u)
                if latent:
                    return
                for j in range(4):
                    k = 4 * u + j
                    if j >= 2:
                        dve.wait_ge(S("steps_used"), 3 * u + j - 1)
                    elif u:
                        dve.wait_ge(S("att_scored"), u)
                    c = n * 32 + m * 4 + j
                    nc.vector.tensor_scalar(onehot[:, j % 2, 0:(n + 1) * P], POS[:, 0:(n + 1) * P], QCOL[:, c:c + 1],
                                            None, ALU.is_ge).then_inc(S("steps"), 1)

            def maxima(u):
                w = (unit(u)[1] + 1) * P
                dve.wait_ge(S("att_scored"), u + 1)
                if u >= 2:
                    dve.wait_ge(S("att_probs"), u - 1)
                st = ST[:, u % 2, :]
                link(dve, nc.vector.reduce_max(st[:, 0:1], ps[:, u % 2, 0:w], AXX))
                nc.vector.tensor_scalar(st[:, 1:2], st[:, 0:1], -MLA_SCALE if unit(u)[0] else -1.0, None, ALU.mult)\
                    .then_inc(S("att_max"), 1)

            dve.wait_ge(S("penal"), 4)
            steps(0)
            maxima(0)
            for u in range(UNITS):
                w = (unit(u)[1] + 1) * P
                if u + 1 < UNITS:
                    steps(u + 1)
                    maxima(u + 1)
                dve.wait_ge(S("att_exp"), u + 1)
                st = ST[:, u % 2, :]
                link(dve, nc.vector.reciprocal(st[:, 3:4], st[:, 2:3]))
                nc.vector.tensor_scalar(PR[:, u % 2, 0:w], PR[:, u % 2, 0:w], st[:, 3:4], None, ALU.mult)\
                    .then_inc(S("att_probs"), 1)
                if u and u % 8 == 0:
                    heads_low(dve, u // 8 - 1)
            heads_low(dve, 7)
            b = FIRST["mix_out"]
            with dve.Fori(0, 2) as i:
                for j in range(4):
                    c, bank = b + 3 * j, 4 * (j % 2)
                    for z in range(2):
                        dve.wait_ge(S("gate2"), i * 8 + (2 * j + z + 1))
                        dve.wait_ge(S("block_done"), num(c + 2, i * 3, 1))
                        nc.vector.tensor_tensor(PROD[:, j % 2, z, :], GATES[:, j % 2, z, :], ps[:, bank + 2 + z, :],
                                                ALU.mult).then_inc(S("gated2"), 1)
                    dve.wait_ge(S("gated2"), i * 8 + (2 * j + 2))
                    nc.vector.tensor_tensor(Y[:, bass.ds(i * 4 + j, 1), :], PROD[:, j % 2, 0:1, :],
                                            PROD[:, j % 2, 1:2, :], ALU.add).then_inc(S("bank_free"), 3)
                    dve.wait_ge(S("bank_free"), num(c, i * 3, 7))
            for k in range(KT):
                dve.wait_ge(S("y_hi"), k + 1)
                nc.vector.tensor_tensor(a_lo[:, k, :], Y[:, k, :], a_hi[:, k, :].bitcast(F32), ALU.subtract)\
                    .then_inc(S("y_lo"), 1)
            b = FIRST["w_out"]
            with dve.Fori(0, 2) as i:
                for j in range(4):
                    residual_dve(dve, b + j, i, i * 4 + j, mod_col(5, i * 4 + j))

        def heads_low(dve, blk):
            dst, src = out_heads(blk)
            dve.wait_ge(S("att_hi"), blk + 1)
            nc.vector.tensor_tensor(dst(a_lo), src, dst(a_hi).bitcast(F32), ALU.subtract).then_inc(S("att_lo"), 1)

        block = ctx.enter_context(nc.Block())

        @block.sync
        def _(sp):
            swa_sp(sp)
            ffn_sp(sp, "ffn0")
            gdn_sp(sp)
            ffn_sp(sp, "ffn1")
            ffn_sp(sp, "swi0")
            mix_sp(sp)
            ffn_sp(sp, "swi1")
            for k in range(KT):
                sp.wait_ge(S("final_ready"), k + 1)
                sp.dma_start(out[:, k, :], FINAL[:, k, :]).then_inc(S("stored"), 16)
            sp.wait_ge(S("stored"), 16 * KT)

        @block.gpsimd
        def _(pool):
            for s in range(RING):
                split_lo(pool, s)
            with pool.Fori(0, N_BLOCKS // RING - 1) as i:
                for s in range(RING):
                    split_lo(pool, RING + s, i)
            for s in range(N_BLOCKS % RING):
                split_lo(pool, N_BLOCKS // RING * RING + s)

        @block.scalar
        def _(act):
            act.dma_start(h[:, :, :], dram["x"]).then_inc(S("x_landed"), 16)
            act.dma_start(common[:, :], dram["common"]).then_inc(S("common_landed"), 16)
            act.dma_start(params[:, :], dram["params"]).then_inc(S("params_landed"), 16)
            act.dma_start(view(ROPE1_SCRATCH, T).bitcast(I32), dram["positions"]).then_inc(S("positions0"), 16)
            act.dma_start(phase_const[:, 0:640], dram["swa_const"]).then_inc(S("swa_const"), 16)
            act.wait_ge(S("common_landed"), 16)
            act.wait_ge(S("params_landed"), 16)
            split_hi(act, 0)
            split_hi(act, 1)
            nc.scalar.activation(silu_c[:, :], par("c", 0, KT), ACT.Silu).then_inc(S("silu_c_ready"), 1)
            rope_act(act, 0, COS1, SIN1)
            norm_act(act, 0, FIRST["qkv"])
            swa_act(act)
            norm_act(act, 1, FIRST["ffn0"])
            ffn_act(act, "ffn0", 0)
            norm_act(act, 2, FIRST["gdn_ba"])
            gdn_act(act)
            norm_act(act, 3, FIRST["ffn1"])
            ffn_act(act, "ffn1", 1)
            norm_act(act, 4, FIRST["swi0"], lambda k: mod_col(0, k))
            act.dma_start(view(ROPE2_SCRATCH, T).bitcast(I32), dram["positions_2"]).then_inc(S("positions1"), 16)
            act.dma_start(phase_const[:, 0:MIX_W], dram["mix_const"]).then_inc(S("mix_const"), 16)
            rope_act(act, 1, COS2, SIN2)
            ffn_act(act, "swi0", 0)
            norm_act(act, 5, FIRST["mix_v"], lambda k: mod_col(3, k))
            mix_act(act)
            norm_act(act, 6, FIRST["swi1"], lambda k: mod_col(6, k))
            ffn_act(act, "swi1", 0)
            norm_act(act, 7, N_BLOCKS)

        @block.vector
        def _(dve):
            for k in range(4):
                nc.vector.memset(gains[:, k:k + 1], 0.0).then_inc(S("bank_free"), 1)
            for k in range(2):
                nc.vector.memset(gains[:, 4 + k:5 + k], 0.0).then_inc(S("ada_free"), 1)
            dve.wait_ge(S("common_landed"), 16)
            dve.wait_ge(S("params_landed"), 16)
            rope_dve(dve, 0, COS1, SIN1, ROPE1_SCRATCH)
            norm_dve(dve, 0, lambda k: par("mixer_norm", k))
            dve.wait_ge(S("swa_const"), 16)
            swa_dve(dve)
            norm_dve(dve, 1, lambda k: par("ffn_norm", k))
            ffn_dve(dve, "ffn0", 0)
            ada_bias_dve(dve, 0)
            norm_dve(dve, 2, lambda k: par("mixer_norm", KT + k))
            gdn_dve(dve)
            norm_dve(dve, 3, lambda k: par("ffn_norm", KT + k))
            ffn_dve(dve, "ffn1", 1)
            ada_bias_dve(dve, 1)
            modulation_dve(dve)
            norm_dve(dve, 4, lambda k: mod_col(0, k, gains), lambda k: mod_col(0, k))
            rope_dve(dve, 1, COS2, SIN2, ROPE2_SCRATCH)
            ffn_dve(dve, "swi0", 0, lambda k: mod_col(2, k))
            norm_dve(dve, 5, lambda k: mod_col(1, k, gains), lambda k: mod_col(3, k))
            mix_dve(dve)
            norm_dve(dve, 6, lambda k: mod_col(2, k, gains), lambda k: mod_col(6, k))
            ffn_dve(dve, "swi1", 0, lambda k: mod_col(8, k))
            final_dve(dve)

        @block.tensor
        def _(pe):
            pe.wait_ge(S("common_landed"), 16)
            norm_pe(pe, 0)
            u_is_ready(pe, 0)
            swa_pe(pe)
            norm_pe(pe, 1)
            u_is_ready(pe, 1)
            pe.wait_ge(S("silu_c_ready"), 1)
            ffn_pe(pe, "ffn0")
            norm_pe(pe, 2)
            u_is_ready(pe, 2)
            gdn_pe(pe)
            norm_pe(pe, 3)
            u_is_ready(pe, 3)
            ffn_pe(pe, "ffn1")
            norm_pe(pe, 4)
            u_is_ready(pe, 4)
            ffn_pe(pe, "swi0")
            norm_pe(pe, 5)
            u_is_ready(pe, 5)
            mix_pe(pe)
            norm_pe(pe, 6)
            u_is_ready(pe, 6)
            ffn_pe(pe, "swi1")
            norm_pe(pe, 7)


def blocks(w):
    k, n = w.shape
    return w.reshape(k // P, P, n // P, P).transpose(2, 1, 0, 3).reshape(n // P, P, k)


def ffn_blocks(up, down, tiles):
    full, tail = [], []
    g, u = blocks(up[:, :tiles * P]), blocks(up[:, tiles * P:])
    for at in range(0, tiles, CH):
        m = min(CH, tiles - at)
        full.append(np.stack([g[at:at + m], u[at:at + m]], 1).reshape(2 * m, P, BW))
        (full if m == CH else tail).append(blocks(down[at * P:(at + m) * P]))
    return np.concatenate(full), (np.concatenate(tail) if tail else None)


def columns(*vectors):
    return np.concatenate([np.ascontiguousarray(v).reshape(-1, P).T for v in vectors], 1)


def rows_for_all(v):
    return np.broadcast_to(np.asarray(v).reshape(1, -1), (P, np.asarray(v).size))


def rotation(half, dim):
    m = np.zeros((P, P), np.float32)
    for at in range(0, P, dim):
        for d in range(half):
            m[at + d + half, at + d] = -1.0
            m[at + d, at + d + half] = 1.0
    return m


def frequencies(half, dim, theta):
    d = np.arange(P) % dim
    f = theta ** (-(d % half) / half)
    return np.where(d < 2 * half, f, 0.0).astype(np.float32)[:, None]


def shape_constants():
    r = np.arange(P)
    common = np.concatenate([
        np.eye(P), np.ones((P, P)), np.kron(np.eye(2), np.ones((64, 64))),
        frequencies(ROPE1_HALF, 64, ROPE1_THETA), frequencies(ROPE2_HALF, 32, ROPE2_THETA), np.full((P, 1), EPS),
    ], 1)
    q, k = r[:, None], np.arange(256)[None, :]
    dist = q + P - k
    seen = (dist >= 0) & (dist < P)
    mask = np.where(seen, 0.0, -BIG)
    first = np.where(seen & (k >= P), 0.0, -BIG)
    swa = np.concatenate([rotation(ROPE1_HALF, 64), mask, first], 1)
    same = (r[:, None] // 64) == (r[None, :] // 64)
    before = same & (r[:, None] <= r[None, :])
    levels = []
    for lv in range(6):
        s, c = r[:, None] >> lv, r[None, :] >> lv
        levels.append((s // 2 == c // 2) & (c % 2 == 1) & (s % 2 == 0))
    gdn = np.concatenate([
        before, np.broadcast_to(q < 64, (P, P)), np.broadcast_to(q >= 64, (P, P)),
        np.where(before, 0.0, -BIG)] + levels, 1)
    limit = np.where((q < 64) & (r[None, :] >= 64), -BIG, 0.0)
    large = [max(8, math.ceil(8 * 16.0 ** (m / 8) - 1e-9)) for m in range(8)]
    lows = list(range(1, 8)) + large
    thr = [-1e9] + [-(lows[b] - 1) for b in range(14, -1, -1)] + [lows[b] for b in range(15)] + [1e9]
    thresholds = np.tile(np.array(thr), 4)[:, None]
    of_row = (np.arange(P)[None, :] // 4 % 16)
    query = np.concatenate([of_row == 4 * i + (r[:, None] // 32) for i in range(4)], 1)
    mix = np.concatenate([rotation(ROPE2_HALF, 32), limit, thresholds, query], 1)
    rep = np.concatenate([r[:, None] == 16 * s + of_row for s in range(8)], 1)
    f = np.float32
    return common.astype(f), swa.astype(f), gdn.astype(f), mix.astype(f), rep.astype(f)


def kernel(**inp):
    import concourse.bacc as bacc
    from concourse.bass_utils import run_bass_kernel_spmd as run

    nc, arrays, dram, out = prepare(bacc, inp)
    build(nc, dram, out)
    r = run(nc, [arrays], core_ids=[0])
    got = r.results[0]["out_dram"]
    return np.ascontiguousarray(got.reshape(P, KT, T).transpose(2, 1, 0)).reshape(1, T, D)


def prepare(bacc, inp):
    inp = {k: np.asarray(v) for k, v in inp.items()}
    f = np.float32
    arrays = {}
    arrays["x"] = inp["x"][0].T.reshape(KT, P, T).transpose(1, 0, 2)
    arrays["positions"] = rows_for_all(inp["positions"][0]).astype(np.int32)
    arrays["positions_2"] = rows_for_all(inp["positions_2"][0]).astype(np.int32)
    common, swa, gdn, mix, rep = shape_constants()
    arrays["common"], arrays["swa_const"], arrays["gdn_const"], arrays["mix_const"] = common, swa, gdn, mix
    arrays["rep_const"] = rep

    w = inp["attn_w_in"][0]
    q = w[:, :1024].reshape(D, 2, 2, 4, 64).transpose(0, 1, 3, 2, 4).reshape(D, 1024)
    v = w[:, 1280:].reshape(2, 4, P, 256).transpose(0, 2, 1, 3).reshape(2, P, BW)
    arrays["qkv"] = np.concatenate([blocks(q), blocks(w[:, 1024:1280]), v])
    w = inp["attn_w_out"][0].reshape(4, 2, 2, 64, D).transpose(0, 2, 1, 3, 4).reshape(D, D)
    arrays["attn_out"] = blocks(w)
    for n in range(2):
        arrays[f"ffn{n}"], _ = ffn_blocks(inp["ffn_w_up"][n], inp["ffn_w_down"][n], FFN_TILES)
        k = n + 1
        arrays[f"swi{n}"], arrays[f"swi{n}_tail"] = ffn_blocks(
            inp[f"w_ffn{k}_in_2"][0], inp[f"w_ffn{k}_down_2"][0], SWI_TILES)
    arrays["ada"] = blocks(inp["w_ada_2"][0])

    gdn_layout(inp, arrays)
    mix_layout(inp, arrays)

    taps = inp["gdn_conv"][0]
    order = gdn_order()[:, :8].reshape(-1)
    conv = [taps[j].reshape(-1, P)[order] for j in range(4)]
    seg = [15 - s if s < 16 else s + 1 for s in range(31)]
    rel = inp["rel_bias_2"]
    rel_at = np.concatenate([rel[seg], np.zeros((1, 8), f)])
    rel_before = np.concatenate([np.zeros((1, 8), f), rel[seg[:-1]], np.zeros((1, 8), f)])
    packed = {
        "mixer_norm": columns(*inp["mixer_norm"]), "ffn_norm": columns(*inp["ffn_norm"]),
        "ffn_conv": columns(*inp["ffn_conv"].reshape(6, -1)), "ffn_conv_b": columns(*inp["ffn_conv_b"]),
        "g_ffn1": columns(inp["g_ffn1_2"]), "g_mix": columns(inp["g_mix_2"]), "g_ffn2": columns(inp["g_ffn2_2"]),
        "g_final": columns(inp["g_final_2"]), "c": columns(inp["c_2"]), "b_ada": columns(inp["b_ada_2"]),
        "gdn_conv": columns(*conv), "gdn_norm": columns(inp["gdn_norm"]),
        "q_gain": columns(np.tile(inp["attn_q_gain"][0], 2)), "k_gain": columns(np.tile(inp["attn_k_gain"][0], 2)),
        "sinks": rows_for_all(inp["attn_sinks"][0]), "a_log": rows_for_all(inp["gdn_a_log"][0]),
        "dt_bias": rows_for_all(inp["gdn_dt_bias"][0]), "g_cq": columns(inp["g_cq_2"]),
        "g_ckv": columns(inp["g_ckv_2"]), "rel_at": np.tile(rel_at, (4, 1)), "rel_before": np.tile(rel_before, (4, 1)),
    }
    arrays["params"] = np.concatenate([packed[n] for n, _ in PARAM_COLS], 1)

    nc = bacc.Bacc("TRN2", target_bir_lowering=False, num_devices=1)
    dram = {}
    maps = {}
    for name, a in arrays.items():
        a = np.ascontiguousarray(a)
        maps[f"{name}_dram"] = a
        dram[name] = nc.dram_tensor(f"{name}_dram", a.shape, mybir.dt.from_np(a.dtype), kind="ExternalInput").ap()
    out = nc.dram_tensor("out_dram", (P, KT, T), F32, kind="ExternalOutput").ap()
    return nc, maps, dram, out


def gdn_order():
    return np.array([[2 * r, 2 * r + 1, 8 + 2 * r, 9 + 2 * r] + [16 + 4 * r + x for x in range(4)]
                     + [32 + 4 * r + x for x in range(4)] for r in range(4)])


def gdn_layout(inp, arrays):
    w = inp["gdn_w_in"][0]
    main, out = blocks(w[:, :6144]), inp["gdn_w_out"][0]
    quarters = []
    for r in range(4):
        quarters.append(main[gdn_order()[r]])
        quarters.append(blocks(out[r * 512:(r + 1) * 512]).reshape(4, 2, P, 512).transpose(0, 2, 1, 3)
                        .reshape(4, P, BW))
    arrays["gdn"] = np.concatenate(quarters)
    arrays["gdn_ba"] = w[:, 6144:].reshape(KT, P, 32).transpose(1, 0, 2).reshape(1, P, 256)


def mix_layout(inp, arrays):
    w = inp["w_in_2"][0]
    cuts = np.cumsum([0, 512, 64, 64, 512, 64, 8, 384, 256, 32, 1024, 1024])
    qa, ka, va, qi, ki, wi, cq, ckv, kr, ga, gb = [w[:, a:b] for a, b in zip(cuts[:-1], cuts[1:])]
    vw = np.concatenate([va, wi], 1)
    arrays["mix_v"] = vw.reshape(KT, P, 72).transpose(1, 0, 2).reshape(1, P, 576)
    arrays["mix_in"] = blocks(np.concatenate([qa, ka, ka, qi, ki, ki, cq, ckv, kr, kr, kr, kr], 1))
    uq = inp["w_uq_2"][0].reshape(384, 8, 96)
    uq = np.concatenate([uq[:, :, :64].reshape(384, 512), uq[:, :, 64:].reshape(384, 256)], 1)
    arrays["uq"] = blocks(uq).reshape(3, 2, P, 384).transpose(0, 2, 1, 3).reshape(3, P, 768)
    uk = blocks(inp["w_uk_2"][0]).reshape(1, 4, P, 256).transpose(0, 2, 1, 3).reshape(1, P, BW)
    uv = inp["w_uv_2"][0].reshape(2, P, 512).transpose(1, 0, 2).reshape(1, P, BW)
    arrays["ukv"] = np.concatenate([uk, uv])
    oa, ob = blocks(inp["w_o_a_2"][0]), blocks(inp["w_o_b_2"][0])
    arrays["mix_out"] = np.stack([blocks(ga), blocks(gb), np.concatenate([oa, ob], 2)], 1).reshape(24, P, BW)
    arrays["w_out"] = blocks(inp["w_out_2"][0])
```

```python
import math
from contextlib import ExitStack

import numpy as np

import concourse.bass as bass
from concourse import mybir

F32 = mybir.dt.float32
F32R = mybir.dt.float32r
BF16 = mybir.dt.bfloat16
I32 = mybir.dt.int32
ACT = mybir.ActivationFunctionType
ALU = mybir.AluOpType
AXX = mybir.AxisListType.X

P = 128
T = 512
TB = T // P
D = 1024
KT = D // P
RING = 4
BW = KT * P
EPS = 1e-6
BIG = 1e30

FFN_TILES = 3072 // P
SWI_TILES = 2816 // P
CH = 8
N_ADA = 72

ROPE1_HALF, ROPE1_THETA = 8, 500000.0
ROPE2_HALF, ROPE2_THETA = 16, 10000.0

PARAM_COLS = [
    ("mixer_norm", 16), ("ffn_norm", 16), ("ffn_conv", 2 * 3 * FFN_TILES), ("ffn_conv_b", 2 * FFN_TILES),
    ("g_ffn1", KT), ("g_mix", KT), ("g_ffn2", KT), ("g_final", KT), ("b_ada", N_ADA),
    ("gdn_conv", 4 * 32), ("gdn_norm", 1), ("q_gain", 1), ("k_gain", 1), ("sinks", 16),
    ("a_log", 16), ("dt_bias", 16), ("g_cq", 3), ("g_ckv", 2), ("rel_at", 8), ("rel_before", 8),
]
PARAM_AT, _at = {}, 0
for _n, _w in PARAM_COLS:
    PARAM_AT[_n] = _at
    _at += _w
PARAM_W = _at

COMMON_AT = {"ident": 0, "ones": 128, "head_ones": 256, "inv_freq": 384, "eps": 386, "thresholds": 387}
COMMON_W = 388
SWA_AT = {"rot": 0, "mask": 128, "mask_first": 384}
GDN_AT = {"cumsum": 0, "chunk0": 128, "chunk1": 256, "decay_mask": 384, "levels": 512}
MIX_AT = {"rot": 0, "limit": 128, "query_of_row": 256}
PHASE_W = 1280
MIX_W = MIX_AT["query_of_row"] + 4 * P

SECTIONS = [
    ("qkv", 12, 1024), ("attn_out", 8, 1024), ("ffn0", 72, 1024), ("gdn_ba", 1, 256), ("gdn", 64, 1024),
    ("ffn1", 72, 1024), ("swi0", 60, 1024), ("swi0_tail", 8, 768), ("mix_v", 1, 576), ("mix_in", 16, 1024),
    ("uq", 3, 768), ("ukv", 2, 1024), ("mix_out", 24, 1024), ("w_out", 8, 1024), ("swi1", 60, 1024),
    ("swi1_tail", 8, 768),
]
FIRST, _b = {}, 0
for _n, _k, _w in SECTIONS:
    FIRST[_n] = _b
    _b += _k
N_BLOCKS = _b
ARENA_W = 15872


def build(nc, dram, out):
    ctx = ExitStack()
    with ctx:
        sems = {}

        def S(name):
            if name not in sems:
                sems[name] = ctx.enter_context(nc.semaphore(name))
            return sems[name]

        def sb(name, shape, dt=F32):
            return ctx.enter_context(nc.sbuf_tensor(name, shape, dt))

        h = sb("residual", [P, KT, T])
        u_hi, u_lo = sb("u_hi", [P, KT, T], F32R), sb("u_lo", [P, KT, T], F32R)
        a_hi, a_lo = sb("a_hi", [P, CH, T], F32R), sb("a_lo", [P, CH, T], F32R)
        w_raw = sb("w_raw", [P, RING, BW])
        w_hi, w_lo = sb("w_hi", [P, RING, BW], F32R), sb("w_lo", [P, RING, BW], F32R)
        params = sb("params", [P, PARAM_W])
        common = sb("common", [P, COMMON_W])
        phase_const = sb("phase_const", [P, PHASE_W])
        mod = sb("mod", [P, N_ADA])
        gains = sb("gains", [P, 3 * KT])
        arena = sb("arena", [P, ARENA_W])
        onehot = sb("onehot", [P, 2, T], F32R)
        table_hi, table_lo = sb("table_hi", [P, 4, P], F32R), sb("table_lo", [P, 4, P], F32R)
        ps = ctx.enter_context(nc.psum_tensor("ps", [P, 8, T], F32))

        def par(name, i=0, n=1):
            return params[:, PARAM_AT[name] + i:PARAM_AT[name] + i + n]

        def pcol(name, i):
            return params[:, bass.ds(PARAM_AT[name] + i, 1)]

        ident = common[:, 0:128]
        ones = common[:, 128:256]
        head_ones = common[:, 256:384]

        def view(at, *dims):
            n = int(np.prod(dims))
            assert at + n <= ARENA_W, (at, dims)
            v = arena[:, at:at + n]
            names = " ".join(f"d{k}" for k in range(len(dims)))
            return v if len(dims) == 1 else v.rearrange(
                f"p ({names}) -> p {names}", **{f"d{k}": n_ for k, n_ in enumerate(dims)})

        def num(base, i, more=0):
            return base + more if isinstance(i, int) and i == 0 else i * 4 + (base + more)

        def load_block(sp, base, i, src, width):
            s = base % RING
            if base >= RING:
                sp.wait_ge(S("lo_ready"), num(base, i, 1 - RING))
            sp.dma_start(w_raw[:, s, 0:width], src).then_inc(S(f"raw_landed{s}"), 16)

        def split_hi(act, base, i=0):
            s = base % RING
            lap = base // RING + 1
            act.wait_ge(S(f"raw_landed{s}"), 16 * lap if isinstance(i, int) else (i + lap) * 16)
            if base >= RING:
                act.wait_ge(S("block_done"), num(base, i, 1 - RING))
            nc.scalar.activation(w_hi[:, s, :], w_raw[:, s, :], ACT.Copy).then_inc(S("hi_ready"), 1)

        def split_lo(pool, base, i=0):
            s = base % RING
            pool.wait_ge(S("hi_ready"), num(base, i, 1))
            nc.gpsimd.tensor_tensor(w_lo[:, s, :], w_raw[:, s, :], w_hi[:, s, :].bitcast(F32),
                                    ALU.subtract).then_inc(S("lo_ready"), 1)

        def product(dst, l_hi, l_lo, r_hi, r_lo, first, last):
            nc.tensor.matmul(dst, l_hi, r_hi, start=first, stop=False)
            nc.tensor.matmul(dst, l_hi, r_lo, start=False, stop=False)
            return nc.tensor.matmul(dst, l_lo, r_hi, start=False, stop=last)

        def out_tile(dst, slot, x_hi, x_lo, kts, w_at=0, x_at=0, ready=None):
            for k in range(kts):
                if ready is not None:
                    ready(k)
                c = (w_at + k) * P
                last = product(dst, w_hi[:, slot, c:c + P], w_lo[:, slot, c:c + P],
                               x_hi[:, x_at + k, :], x_lo[:, x_at + k, :], k == 0, k == kts - 1)
            return last

        def block_matmul(pe, base, i, x_hi, x_lo, kts=KT, ready=None):
            pe.wait_ge(S("lo_ready"), num(base, i, 1))
            pe.wait_ge(S("bank_free"), num(base, i, 1))
            out_tile(ps[:, base % 4, :], base % RING, x_hi, x_lo, kts, ready=ready).then_inc(S("block_done"), 1)

        def lookahead(act, base, i=0):
            if base + 3 < N_BLOCKS:
                split_hi(act, base + 3, i)

        def load_ln_exp(act):
            nc.scalar.preload_act_table_set("natural_log_exp_and_others")

        SQ, RSTD, NT = view(0, T), view(1024, T), view(1536, 2, T)

        def squares_begin(dve, n):
            if n:
                dve.wait_ge(S("normed"), 8 * n)
            nc.vector.memset(RSTD, 0.0).then_inc(S("sq_sum"), 1)

        def square_dve(dve, n, i, j):
            at = i * 8 + (17 * n + 2 * j + 1)
            dve.wait_ge(S("sq_sum"), at)
            tile = h[:, bass.ds(i * 4 + j, 1), :]
            nc.vector.tensor_tensor(SQ[:, None, :], tile, tile, ALU.mult).then_inc(S("sq_sum"), 1)
            dve.wait_ge(S("sq_sum"), at + 1)
            nc.vector.tensor_tensor(RSTD, RSTD, SQ, ALU.add).then_inc(S("sq_sum"), 1)

        def norm_act(act, n, shift=None):
            load_ln_exp(act)
            act.wait_ge(S("sq_used"), n + 1)
            nc.scalar.activation(RSTD, ps[:, 4, :], ACT.Ln, bias=eps_col, scale=1.0 / D).then_inc(S("rstd_ready"), 1)
            act.wait_ge(S("rstd_ready"), 2 * n + 1)
            nc.scalar.activation(RSTD, RSTD, ACT.Exp, scale=-0.5).then_inc(S("rstd_ready"), 1)
            if n == 7:
                return
            for k in range(KT):
                act.wait_ge(S("normed"), 8 * n + k + 1)
                if shift is None:
                    nc.scalar.activation(u_hi[:, k, :], NT[:, k % 2, :], ACT.Copy).then_inc(S("u_hi_ready"), 1)
                else:
                    nc.scalar.activation(u_hi[:, k, :], NT[:, k % 2, :], ACT.Identity,
                                         bias=shift(k)).then_inc(S("u_hi_ready"), 1)

        def norm_pe(pe, n):
            if n:
                pe.wait_ge(S("rstd_ready"), 2 * n)
            pe.wait_ge(S("sq_sum"), 17 * n + 17)
            nc.tensor.matmul(ps[:, 4, :], ones, RSTD, start=True, stop=True).then_inc(S("sq_used"), 1)

        def norm_dve(dve, n, gain, shift=None):
            dve.wait_ge(S("rstd_ready"), 2 * n + 2)

            def normed(k):
                if k >= 2:
                    dve.wait_ge(S("u_lo_ready"), 8 * n + k - 1)
                nc.vector.scalar_tensor_tensor(out=NT[:, k % 2, :], in0=h[:, k, :], scalar=gain(k), in1=RSTD,
                                               op0=ALU.mult, op1=ALU.mult).then_inc(S("normed"), 1)

            def low(k):
                dve.wait_ge(S("u_hi_ready"), 8 * n + k + 1)
                hi = u_hi[:, k, :].bitcast(F32)
                if shift is None:
                    nc.vector.tensor_tensor(u_lo[:, k, :], NT[:, k % 2, :], hi, ALU.subtract)\
                        .then_inc(S("u_lo_ready"), 1)
                else:
                    nc.vector.scalar_tensor_tensor(out=u_lo[:, k, :], in0=NT[:, k % 2, :], scalar=shift(k),
                                                   in1=hi, op0=ALU.add, op1=ALU.subtract)\
                        .then_inc(S("u_lo_ready"), 1)

            normed(0)
            for k in range(1, KT):
                normed(k)
                low(k - 1)
            low(KT - 1)

        def u_tile(n):
            return lambda k: nc.tensor.wait_ge(S("u_lo_ready"), 8 * n + k + 1)

        ADA_RING = view(13312, 2, BW)
        ADA_SUM = view(13304, 2)
        SILU_ROW = view(7680, D)

        def ada_load(sp, body):
            for q in range(2):
                sp.wait_ge(S("ada_free"), body * 2 + (q + 1))
                src = dram["ada"][bass.ds(body * 2 + q, 1)].rearrange("a p n -> (a p) n")
                sp.dma_start(ADA_RING[:, q, :], src).then_inc(S(f"ada_landed{q}"), 16)

        def silu_row_load(act, layer):
            act.dma_start(SILU_ROW, dram["c_row"]).then_inc(S("c_landed"), 16)

        def silu_row_act(act, layer):
            act.wait_ge(S("c_landed"), 16 * layer + 16)
            nc.scalar.activation(SILU_ROW, SILU_ROW, ACT.Silu).then_inc(S("silu_row"), 1)

        def ada_dve(dve, body):
            for q in range(2):
                dve.wait_ge(S(f"ada_landed{q}"), body * 16 + 16)
                dve.wait_ge(S("ada_kept"), body * 2 + (q + 1))
                nc.vector.tensor_tensor_reduce(ADA_RING[:, q, :], ADA_RING[:, q, :], SILU_ROW, 1.0, 0.0, ALU.mult,
                                               ALU.add, ADA_SUM[:, q:q + 1]).then_inc(S("ada_free"), 1)
                dve.wait_ge(S("ada_free"), body * 2 + (q + 3))
                nc.vector.tensor_scalar(mod[:, bass.ds(body * 2 + q, 1)], ADA_SUM[:, q:q + 1], 1.0, None, ALU.mult)\
                    .then_inc(S("ada_kept"), 1)

        CV, AV = view(5632, 2, T), view(6656, 2, T)

        def ffn_chunks(kind):
            n = {"ffn0": 0, "ffn1": 1, "swi0": 2, "swi1": 3}[kind]
            tiles = FFN_TILES if n < 2 else SWI_TILES
            pair0 = [0, 24, 48, 70][n]
            b = FIRST[kind]
            done = 0
            while done < tiles:
                m = min(CH, tiles - done)
                ada = (n * 3 + done // CH) * 6 if n < 2 else None
                yield b, pair0 + done, done, m, ada
                b += 2 * m + 8
                done += m

        def done_after(kind, tiles):
            return tiles == (FFN_TILES if kind.startswith("ffn") else SWI_TILES)

        def ffn_sp(sp, kind):
            first = FIRST[kind]
            for b, _, _, m, ada in ffn_chunks(kind):
                with sp.Fori(0, m // 2) as i:
                    for j in range(4):
                        load_block(sp, b + j, i, dram[kind][bass.ds(i * 4 + (b - first + j), 1)]
                                   .rearrange("a p n -> (a p) n"), BW)
                    if ada is not None:
                        sp.wait_ge(S("c_landed"), 16 * (1 + (kind == "ffn1")))
                        ada_load(sp, i + ada)
                b += 2 * m
                src, at, width = (dram[kind], b - first, BW) if m == CH else (dram[kind + "_tail"], 0, m * P)
                with sp.Fori(0, 2) as i:
                    for j in range(4):
                        load_block(sp, b + j, i, src[bass.ds(i * 4 + (at + j), 1)]
                                   .rearrange("a p n -> (a p) n"), width)
                    if ada is not None:
                        ada_load(sp, i + (ada + 4))

        def ffn_pe(pe, kind, norm):
            for b, pair, _, m, _ in ffn_chunks(kind):
                with pe.Fori(0, m // 2) as i:
                    for j in range(4):
                        first = j == 0 and b == FIRST[kind]
                        block_matmul(pe, b + j, i, u_hi, u_lo, ready=u_tile(norm) if first else None)
                b += 2 * m
                with pe.Fori(0, 2) as i:
                    for j in range(4):
                        block_matmul(pe, b + j, i, a_hi, a_lo, m,
                                     ready=(lambda k: pe.wait_ge(S("a_lo_ready"), pair + k + 1)) if j == 0 else None)

        def ffn_act(act, kind, layer):
            conv = kind.startswith("ffn")
            for b, pair, tile, m, _ in ffn_chunks(kind):
                with act.Fori(0, m // 2) as i:
                    for q in range(2):
                        bg, bu = b + 2 * q, b + 2 * q + 1
                        lookahead(act, bg, i)
                        act.wait_ge(S("block_done"), num(bg, i, 1))
                        n = i * 2 + (pair + q)
                        if conv:
                            col = i * 2 + (tile + q)
                            base = layer * 3 * FFN_TILES
                            nc.scalar.activation(CV[:, q, :], ps[:, bg % 4, :], ACT.Identity,
                                                 scale=pcol("ffn_conv", col + (base + 2 * FFN_TILES)),
                                                 bias=pcol("ffn_conv_b", col + layer * FFN_TILES))\
                                .then_inc(S("cv_main"), 1)
                            lookahead(act, bu, i)
                            act.wait_ge(S("bank_free"), num(bg, i, 5))
                            nc.scalar.activation(CV[:, q, :], CV[:, q, :], ACT.Silu).then_inc(S("silu_ready"), 1)
                        else:
                            nc.scalar.activation(CV[:, q, :], ps[:, bg % 4, :], ACT.Silu)\
                                .then_inc(S("silu_ready"), 1)
                            lookahead(act, bu, i)
                        act.wait_ge(S("bank_free"), num(bu, i, 5))
                        t = i * 2 + q
                        nc.scalar.activation(a_hi[:, bass.ds(t, 1), :], AV[:, q, None, :], ACT.Copy)\
                            .then_inc(S("a_hi_ready"), 1)
                b += 2 * m
                tail = b + 8 == N_BLOCKS
                with act.Fori(0, 1 if tail else 2) as i:
                    for j in range(4):
                        lookahead(act, b + j, i)
                if tail:
                    for j in range(4, 8):
                        lookahead(act, b + j)

        def ffn_dve(dve, kind, layer, norm, gate=None):
            conv = kind.startswith("ffn")
            if conv:
                dve.wait_ge(S("silu_row"), layer + 1)
            for b, pair, tile, m, ada in ffn_chunks(kind):
                with dve.Fori(0, m // 2) as i:
                    for q in range(2):
                        bg, bu = b + 2 * q, b + 2 * q + 1
                        n = i * 2 + (pair + q)
                        if conv:
                            nconv = n
                            col = i * 2 + (tile + q)
                            base = layer * 3 * FFN_TILES
                            dve.wait_ge(S("cv_main"), nconv + 1)
                            nc.vector.scalar_tensor_tensor(
                                out=CV[:, q, 1:T], in0=ps[:, bg % 4, 0:T - 1],
                                scalar=pcol("ffn_conv", col + (base + FFN_TILES)), in1=CV[:, q, 1:T],
                                op0=ALU.mult, op1=ALU.add).then_inc(S("cv_tap"), 1)
                            dve.wait_ge(S("cv_tap"), nconv + 1)
                            nc.vector.scalar_tensor_tensor(
                                out=CV[:, q, 2:T], in0=ps[:, bg % 4, 0:T - 2],
                                scalar=pcol("ffn_conv", col + base), in1=CV[:, q, 2:T],
                                op0=ALU.mult, op1=ALU.add).then_inc(S("bank_free"), 1)
                        dve.wait_ge(S("silu_ready"), n + 1)
                        dve.wait_ge(S("block_done"), num(bu, i, 1))
                        nc.vector.tensor_tensor(AV[:, q, :], CV[:, q, :], ps[:, bu % 4, :], ALU.mult)\
                            .then_inc(S("bank_free"), 1 if conv else 2)
                        dve.wait_ge(S("a_hi_ready"), n + 1)
                        nc.vector.tensor_tensor(a_lo[:, bass.ds(i * 2 + q, 1), :], AV[:, q, None, :],
                                                a_hi[:, bass.ds(i * 2 + q, 1), :].bitcast(F32), ALU.subtract)\
                            .then_inc(S("a_lo_ready"), 1)
                    if ada is not None:
                        ada_dve(dve, i + ada)
                b += 2 * m
                last = done_after(kind, tile + m)
                if last:
                    squares_begin(dve, norm)
                with dve.Fori(0, 2) as i:
                    for j in range(4):
                        residual_dve(dve, b + j, i, i * 4 + j, None if gate is None else gate(i * 4 + j))
                        if last:
                            dve.wait_ge(S("bank_free"), num(b + j, i, 5))
                            square_dve(dve, norm, i, j)
                        if ada is not None and j == 1:
                            ada_dve(dve, i + (ada + 4))

        def residual_dve(dve, base, i, tile, gate=None):
            dve.wait_ge(S("block_done"), num(base, i, 1))
            dve.wait_ge(S("bank_free"), num(base, i, 4))
            at = h[:, bass.ds(tile, 1), :]
            src = ps[:, base % 4:base % 4 + 1, :]
            if gate is None:
                nc.vector.tensor_tensor(at, at, src, ALU.add).then_inc(S("bank_free"), 1)
            else:
                nc.vector.scalar_tensor_tensor(out=at, in0=src, scalar=gate, in1=at, op0=ALU.mult,
                                               op1=ALU.add).then_inc(S("bank_free"), 1)

        def mod_col(v, k, at=mod):
            return at[:, bass.ds(k + v * KT, 1)]

        eps_col = common[:, 386:387]
        chain_count = [0]

        def link(dve, ins):
            chain_count[0] += 1
            ins.then_inc(S("dve_chain"), 1)
            dve.wait_ge(S("dve_chain"), chain_count[0])

        TWO_PI_PARTS = (6.28125, 1.935005187988281e-3, 2.0 * math.pi - 6.28125 - 1.935005187988281e-3)
        ROUND = 1.5 * 2.0 ** 23

        def rope_dve(dve, which, at_cos, at_sin, scratch):
            pos, ang, turns = view(scratch, T), view(scratch + T, T), view(scratch + 2 * T, T)
            dve.wait_ge(S(f"positions{which}"), 16)
            link(dve, nc.vector.tensor_copy(pos, pos.bitcast(I32)))
            freq = common[:, COMMON_AT["inv_freq"] + which:COMMON_AT["inv_freq"] + which + 1]
            link(dve, nc.vector.tensor_scalar(ang, pos, freq, None, ALU.mult))
            for dst, quarter in ((at_cos, 0.25), (at_sin, 0.0)):
                link(dve, nc.vector.tensor_scalar(turns, ang, 1.0 / (2.0 * math.pi), quarter, ALU.mult, ALU.add))
                link(dve, nc.vector.tensor_scalar(turns, turns, ROUND, None, ALU.add))
                link(dve, nc.vector.tensor_scalar(turns, turns, -ROUND, None, ALU.add))
                src = ang
                for part in TWO_PI_PARTS:
                    link(dve, nc.vector.scalar_tensor_tensor(out=dst, in0=turns, scalar=-part, in1=src,
                                                             op0=ALU.mult, op1=ALU.add))
                    src = dst
                link(dve, nc.vector.tensor_scalar(dst, dst, 2.0 * math.pi * quarter, 3.1415925, ALU.add, ALU.min))
                nc.vector.tensor_scalar(dst, dst, -3.1415925, None, ALU.max).then_inc(S("angle_ready"), 1)
                dve.wait_ge(S("angle_ready"), 2 * which + (1 if quarter else 2))

        def rope_act(act, which, at_cos, at_sin):
            for k, dst in enumerate((at_cos, at_sin)):
                act.wait_ge(S("angle_ready"), 2 * which + k + 1)
                nc.scalar.activation(dst, dst, ACT.Sin).then_inc(S("rope_table"), 1)

        HSQ, HR, QN = view(0, 2, T), view(1024, 2, T), view(2048, 2, T)
        ROT1, ROT2 = view(3072, T), view(3584, T)
        COS1, SIN1 = view(4096, T), view(4608, T)
        Q1 = view(5120, 8, T)
        K1 = view(9216, 2, P + T)
        V1 = view(10496, TB + 1, 256)
        ROPE1_SCRATCH = 11776
        SC1 = view(0, 2, 4 * 256)
        PT1 = view(2048, 2, 2, 512)
        ST1 = view(4096, 2, 32)
        ROTM = phase_const[:, 0:128]

        def swa_sp(sp):
            b = FIRST["qkv"]
            for j in range(4):
                load_block(sp, b + j, 0, dram["qkv"][j], BW)
            with sp.Fori(0, 2) as i:
                for j in range(4):
                    load_block(sp, b + 4 + j, i, dram["qkv"][bass.ds(i * 4 + (4 + j), 1)]
                               .rearrange("a p n -> (a p) n"), BW)
            with sp.Fori(0, 2) as i:
                for j in range(4):
                    load_block(sp, b + 12 + j, i, dram["attn_out"][bass.ds(i * 4 + j, 1)]
                               .rearrange("a p n -> (a p) n"), BW)

        def swa_pe(pe):
            b = FIRST["qkv"]

            def head_sum(j):
                pe.wait_ge(S("head_sq"), j + 1)
                if j >= 2:
                    pe.wait_ge(S("head_rstd"), 2 * j - 3)
                nc.tensor.matmul(ps[:, 4 + j % 2, :], head_ones, HSQ[:, j % 2, :], start=True, stop=True)\
                    .then_inc(S("head_sum"), 1)

            def rotate(j):
                pe.wait_ge(S("bank_free"), b + 5 + j)
                if j >= 2:
                    pe.wait_ge(S("roped"), j - 1)
                nc.tensor.matmul(ps[:, 6 + j % 2, :], ROTM, QN[:, j % 2, :], start=True, stop=True)\
                    .then_inc(S("rotated"), 1)

            pe.wait_ge(S("rstd_ready"), 2)
            pe.wait_ge(S("swa_const"), 16)
            for j in range(10):
                block_matmul(pe, b + j, 0, u_hi, u_lo, ready=u_tile(0) if j == 0 else None)
                if j >= 1:
                    head_sum(j - 1)
                if j >= 2:
                    rotate(j - 2)
            pe.wait_ge(S("lo_ready"), b + 12)
            pe.wait_ge(S("bank_free"), b + 12)
            for t in range(TB):
                dst = ps[:, 2 + t // 2, (t % 2) * 256:(t % 2) * 256 + 256]
                for k in range(KT):
                    s, c = (b + 10 + k // 4) % RING, (k % 4) * 256
                    last = product(dst, u_hi[:, k, t * P:(t + 1) * P], u_lo[:, k, t * P:(t + 1) * P],
                                   w_hi[:, s, c:c + 256], w_lo[:, s, c:c + 256], k == 0, k == KT - 1)
                if t == 0:
                    head_sum(9)
                    rotate(8)
            last.then_inc(S("block_done"), 2)
            rotate(9)

            def scores(it):
                n, kv = divmod(it, 4)
                if it >= 2:
                    pe.wait_ge(S("masked"), it - 1)
                o = 64 * (kv % 2)
                for g in range(4):
                    dst = ps[:, 2 * (it % 2) + g // 2, (g % 2) * 256:(g % 2) * 256 + 256]
                    last = nc.tensor.matmul(dst, Q1[o:o + 64, kv // 2 * 4 + g, n * P:(n + 1) * P],
                                            K1[o:o + 64, kv // 2, n * P:n * P + 256], start=True, stop=True)
                last.then_inc(S("scored"), 1)

            def values(it):
                n, kv = divmod(it, 4)
                pe.wait_ge(S("pt_copied"), it + 1)
                if it >= 2:
                    pe.wait_ge(S("o_lo"), it - 1)
                for half in range(2):
                    for kb in range(2):
                        last = nc.tensor.matmul(ps[64 * half:64 * half + 64, 6 + it % 2, 0:256],
                                                V1[:, n + kb, kv * 64:(kv + 1) * 64],
                                                PT1[:, it % 2, kb, half * 256:half * 256 + 256],
                                                start=kb == 0, stop=kb == 1)
                last.then_inc(S("pv_done"), 1)

            pe.wait_ge(S("roped"), 10)
            pe.wait_ge(S("bank_free"), b + 16)
            scores(0)
            for it in range(16):
                n, kv = divmod(it, 4)
                if it + 1 < 16:
                    scores(it + 1)
                pe.wait_ge(S("probs"), it + 1)
                if it >= 1:
                    pe.wait_ge(S("pt_copied"), it)
                for kb in range(2):
                    for g in range(4):
                        last = nc.tensor.transpose(ps[:, 4 + kb, g * P:(g + 1) * P],
                                                   SC1[:, it % 2, g * 256 + kb * P:g * 256 + (kb + 1) * P], ident)
                last.then_inc(S("probs_turned"), 1)
                if it:
                    values(it - 1)
            values(15)
            pe.wait_ge(S("o_lo"), 16)
            with pe.Fori(0, 2) as i:
                for j in range(4):
                    block_matmul(pe, b + 12 + j, i, a_hi, a_lo)

        def swa_act(act):
            b = FIRST["qkv"]

            def rstd(j):
                act.wait_ge(S("head_sum"), j + 1)
                if j >= 2:
                    act.wait_ge(S("bank_free"), b + 3 + j)
                nc.scalar.activation(HR[:, j % 2, :], ps[:, 4 + j % 2, :], ACT.Ln, bias=eps_col, scale=1.0 / 64)\
                    .then_inc(S("head_rstd"), 1)
                act.wait_ge(S("head_rstd"), 2 * j + 1)
                nc.scalar.activation(HR[:, j % 2, :], HR[:, j % 2, :], ACT.Exp, scale=-0.5)\
                    .then_inc(S("head_rstd"), 1)

            for j in range(12):
                lookahead(act, b + j)
                if j < 10:
                    act.wait_ge(S("block_done"), b + j + 1)
                    if j >= 2:
                        act.wait_ge(S("head_sum"), j - 1)
                    nc.scalar.activation(HSQ[:, j % 2, :], ps[:, (b + j) % 4, :], ACT.Square)\
                        .then_inc(S("head_sq"), 1)
                if 1 <= j <= 10:
                    rstd(j - 1)

            def exps(it):
                act.wait_ge(S("neg_max"), it + 1)
                st = ST1[:, it % 2, :]
                for g in range(4):
                    row = SC1[:, it % 2, g * 256:(g + 1) * 256]
                    nc.scalar.activation(row, row, ACT.Exp, bias=st[:, 4 + g:5 + g], accum_out=st[:, 12 + g:13 + g])\
                        .then_inc(S("exped"), 1)
                nc.scalar.activation(st[:, 8:12], st[:, 8:12], ACT.Exp).then_inc(S("exped"), 1)

            def heads_out(it):
                n, kv = divmod(it, 4)
                act.wait_ge(S("pv_done"), it + 1)
                nc.scalar.activation(a_hi[:, 2 * kv:2 * kv + 2, n * P:(n + 1) * P],
                                     ps[:, 6 + it % 2, 0:256].rearrange("p (g q) -> p g q", g=2), ACT.Copy)\
                    .then_inc(S("o_hi"), 1)

            exps(0)
            for it in range(16):
                if it >= 2:
                    heads_out(it - 2)
                act.wait_ge(S("probs_turned"), it + 1)
                if it >= 2:
                    act.wait_ge(S("pv_done"), it - 1)
                nc.scalar.activation(PT1[:, it % 2, :, :], ps[:, 4:6, :], ACT.Copy).then_inc(S("pt_copied"), 1)
                if it + 1 < 16:
                    exps(it + 1)
            heads_out(14)
            heads_out(15)
            with act.Fori(0, 2) as i:
                for j in range(4):
                    lookahead(act, b + 12 + j, i)

        def swa_dve(dve):
            b = FIRST["qkv"]
            nc.vector.memset(K1[:, :, 0:P], 0.0).then_inc(S("dve_chain"), 1)
            nc.vector.memset(V1[:, 0, :], 0.0).then_inc(S("dve_chain"), 1)
            chain_count[0] += 2

            def normed(j):
                dve.wait_ge(S("head_rstd"), 2 * j + 2)
                nc.vector.scalar_tensor_tensor(out=QN[:, j % 2, :], in0=ps[:, (b + j) % 4, :],
                                               scalar=par("q_gain" if j < 8 else "k_gain"),
                                               in1=HR[:, j % 2, :], op0=ALU.mult, op1=ALU.mult)\
                    .then_inc(S("bank_free"), 1)

            def roped(j):
                dve.wait_ge(S("bank_free"), b + 5 + j)
                link(dve, nc.vector.tensor_tensor(ROT1, QN[:, j % 2, :], COS1, ALU.mult))
                dve.wait_ge(S("rotated"), j + 1)
                link(dve, nc.vector.tensor_tensor(ROT2, ps[:, 6 + j % 2, :], SIN1, ALU.mult))
                dst = Q1[:, j, :] if j < 8 else K1[:, j - 8, P:P + T]
                nc.vector.tensor_tensor(dst, ROT1, ROT2, ALU.add).then_inc(S("roped"), 1)
                dve.wait_ge(S("roped"), j + 1)

            dve.wait_ge(S("rope_table"), 2)
            normed(0)
            for j in range(10):
                if j + 1 < 10:
                    normed(j + 1)
                roped(j)
            dve.wait_ge(S("block_done"), b + 12)
            for z in range(2):
                nc.vector.tensor_copy(V1[:, 1 + 2 * z:3 + 2 * z, :],
                                      ps[:, 2 + z, :].rearrange("p (t d) -> p t d", t=2))\
                    .then_inc(S("bank_free"), 1)

            def mask(it):
                n, kv = divmod(it, 4)
                st = ST1[:, it % 2, :]
                dve.wait_ge(S("scored"), it + 1)
                if it >= 2:
                    dve.wait_ge(S("probs_turned"), it - 1)
                at = SWA_AT["mask_first" if n == 0 else "mask"]
                m = phase_const[:, None, at:at + 256].to_broadcast([P, 4, 256])
                nc.vector.scalar_tensor_tensor(
                    out=SC1[:, it % 2, :].rearrange("p (g k) -> p g k", g=4),
                    in0=ps[:, 2 * (it % 2):2 * (it % 2) + 2, :].rearrange("p a (g k) -> p (a g) k", g=2),
                    scalar=0.125, in1=m, op0=ALU.mult, op1=ALU.add).then_inc(S("masked"), 1)
                dve.wait_ge(S("masked"), it + 1)
                link(dve, nc.vector.reduce_max(st[:, 0:4], SC1[:, it % 2, :].rearrange("p (g k) -> p g k", g=4), AXX))
                link(dve, nc.vector.tensor_tensor(st[:, 0:4], st[:, 0:4], par("sinks", 4 * kv, 4), ALU.max))
                link(dve, nc.vector.tensor_scalar(st[:, 4:8], st[:, 0:4], -1.0, None, ALU.mult))
                nc.vector.tensor_tensor(st[:, 8:12], par("sinks", 4 * kv, 4), st[:, 4:8], ALU.add)\
                    .then_inc(S("neg_max"), 1)

            def heads_low(it):
                n, kv = divmod(it, 4)
                dve.wait_ge(S("o_hi"), it + 1)
                hi = a_hi[:, 2 * kv:2 * kv + 2, n * P:(n + 1) * P]
                nc.vector.tensor_tensor(a_lo[:, 2 * kv:2 * kv + 2, n * P:(n + 1) * P],
                                        ps[:, 6 + it % 2, 0:256].rearrange("p (g q) -> p g q", g=2),
                                        hi.bitcast(F32), ALU.subtract).then_inc(S("o_lo"), 1)

            mask(0)
            for it in range(16):
                st = ST1[:, it % 2, :]
                dve.wait_ge(S("exped"), 5 * it + 5)
                link(dve, nc.vector.tensor_tensor(st[:, 16:20], st[:, 8:12], st[:, 12:16], ALU.add))
                link(dve, nc.vector.reciprocal(st[:, 20:24], st[:, 16:20]))
                p = SC1[:, it % 2, :].rearrange("p (g k) -> p g k", g=4)
                nc.vector.tensor_tensor(p, p, st[:, 20:24, None].to_broadcast([P, 4, 256]), ALU.mult)\
                    .then_inc(S("probs"), 1)
                if it + 1 < 16:
                    mask(it + 1)
                if it >= 2:
                    heads_low(it - 2)
            heads_low(14)
            heads_low(15)
            squares_begin(dve, 1)
            with dve.Fori(0, 2) as i:
                for j in range(4):
                    residual_dve(dve, b + 12 + j, i, i * 4 + j)
                    dve.wait_ge(S("bank_free"), num(b + 12 + j, i, 5))
                    square_dve(dve, 1, i, j)

        QG, KG, VG, ZG = view(0, 2, T), view(1024, 2, T), view(2048, 4, T), view(4096, 4, T)
        SM_NAMES = ["beta", "xa", "ax", "e", "w", "w1", "l", "g", "gc", "neg_gc", "kd", "egc", "ekd", "beg",
                    "gl0", "gl1"]
        SM = {n: view(6144 + 64 * k, 64) for k, n in enumerate(SM_NAMES)}
        GC_ROWS, BETA_ROWS, PICK = a_hi[0:16, 4:6, :], a_lo[0:16, 4:6, :], a_hi[0:16, 6, 0:16]
        SLOT = view(8192, 15, T)

        def slot(name, x):
            at = {"mt": 0, "wt": 0, "x": 1, "arg": 1, "qd": 1, "xt": 2, "gated": 2, "c": 3, "kdec": 3,
                  "rstd": 3, "dt": 4, "y": 4, "kbe": 4, "sq": 4, "qkt": 5, "vb": 6}[name]
            return SLOT[:, 2 * at + x, :]

        KK, QK = slot("vb", 0), slot("vb", 1)
        STATE, V_NEW = SLOT[:, 14, 0:256], SLOT[:, 14, 256:512]
        GCV, GSQ, GHR = SLOT[:, 0:2, :], SLOT[:, 2:6, :], SLOT[:, 6:10, :]
        EA = SLOT[:, 10, 0:16]

        def sm_t(name):
            return SM[name].rearrange("p (t h) -> p t h", t=TB)

        def by_block(ap):
            return ap.rearrange("p (t c) -> p t c", t=TB)

        def gdn_mask(name, lv=0):
            at = GDN_AT[name] + P * lv
            return phase_const[:, None, at:at + P].to_broadcast([P, TB, P])

        def even(ap, lv):
            return ap.rearrange("p (a two w) -> p a two w", two=2, w=1 << lv)[:, :, 0, :]

        def odd(ap, lv):
            return ap.rearrange("p (a two w) -> p a two w", two=2, w=1 << lv)[:, :, 1, :]

        def runs(ap, lv):
            return ap.rearrange("p (a w) -> p a w", w=1 << lv)

        def level_mask(lv, x):
            return slot("vb" if lv in (2, 4) else "c", x)

        def in_block(r, j):
            b = FIRST["gdn"]
            return b + j if r == 0 else b + 12 + 16 * (r - 1) + (j if j < 4 else j + 4)

        def out_block(r, j):
            return FIRST["gdn"] + 12 + 16 * r + (4 if r < 3 else 0) + j

        def gdn_sp(sp):
            load_block(sp, FIRST["gdn_ba"], 0, dram["gdn_ba"][0], 256)
            b = FIRST["gdn"]
            with sp.Fori(0, 16) as i:
                for j in range(4):
                    load_block(sp, b + j, i, dram["gdn"][bass.ds(i * 4 + j, 1)].rearrange("a p n -> (a p) n"), BW)

        def gdn_pe(pe):
            b = FIRST["gdn_ba"]
            pe.wait_ge(S("lo_ready"), b + 1)
            pe.wait_ge(S("bank_free"), b + 4)
            for t in range(TB):
                for k in range(KT):
                    if t == 0:
                        u_tile(2)(k)
                    c = k * 32
                    last = product(ps[:, b % 4, t * 32:t * 32 + 32], u_hi[:, k, t * P:(t + 1) * P],
                                   u_lo[:, k, t * P:(t + 1) * P], w_hi[:, b % RING, c:c + 32],
                                   w_lo[:, b % RING, c:c + 32], k == 0, k == KT - 1)
            last.then_inc(S("block_done"), 1)
            def project(r, j):
                base = in_block(r, j)
                pe.wait_ge(S("lo_ready"), base + 1)
                if r == 0:
                    pe.wait_ge(S("bank_free"), base + (4 if j == 0 else 1))
                else:
                    pe.wait_ge(S("bank_free"), base + (3 if j == 4 else 2 if j in (5, 6) else 1 if j > 4 else 4 - j))
                out_tile(ps[:, j % 4, :], base % RING, u_hi, u_lo, KT).then_inc(S("block_done"), 1)

            for r in range(4):
                for j in range(0 if r == 0 else 4, 12):
                    project(r, j)
                    if j == 9:
                        for i in range(4):
                            pe.wait_ge(S("gdn_sq"), 4 * r + i + 1)
                            nc.tensor.matmul(ps[:, 4 + i, :], ones, GSQ[:, i, :], start=True, stop=True)\
                                .then_inc(S("gdn_sum"), 1)
                    if r == 0 and j == 10:
                        gdn_pe_decays(pe)
                gdn_pe_open(pe, 2 * r)
                gdn_pe_pair(pe, 2 * r)
                gdn_pe_open(pe, 2 * r + 1)
                gdn_pe_close(pe, 2 * r)
                gdn_pe_pair(pe, 2 * r + 1)
                if r < 3:
                    project(r + 1, 0)
                gdn_pe_close(pe, 2 * r + 1)
                if r < 3:
                    project(r + 1, 1)
                    pe.wait_ge(S("o_rstd"), 8 * r + 6)
                    project(r + 1, 2)
                    project(r + 1, 3)
                pe.wait_ge(S("gdn_o_lo"), 4 * r + 4)
                for j in range(4):
                    base = out_block(r, j)
                    pe.wait_ge(S("lo_ready"), base + 1)
                    pe.wait_ge(S("bank_free"), base + (2 if j == 0 else 3))
                    for z in range(2):
                        last = out_tile(ps[:, 2 * (j % 2) + z, :], base % RING, a_hi, a_lo, 4, 4 * z)
                    last.then_inc(S("block_done"), 1)

        def gdn_pe_decays(pe):
            pe.wait_ge(S("log_decay"), 1)
            pe.wait_ge(S("gdn_const"), 16)
            pe.wait_ge(S("gdn_rstd"), 8)
            for k, at in enumerate((phase_const[:, 0:128], head_ones, phase_const[:, 128:256],
                                    phase_const[:, 256:384])):
                last = nc.tensor.matmul(ps[:, 5, 64 * k:64 * k + 64], at, SM["g"], start=True, stop=True)
            last.then_inc(S("log_decay_sums"), 1)
            pe.wait_ge(S("gc_copied"), 1)
            for src, bank in ((SM["gc"], 6), (SM["beta"], 7)):
                for t in range(TB):
                    last = nc.tensor.transpose(ps[0:16, bank, t * P:(t + 1) * P], src[:, t * 16:(t + 1) * 16], ident)
            last.then_inc(S("head_rows"), 1)

        def gdn_pe_open(pe, pr):
            quarter, kh = divmod(pr, 2)
            q, k = by_block(QG[:, kh, :]), by_block(KG[:, kh, :])
            pe.wait_ge(S("gdn_unit"), 4 * quarter + 4)
            pe.wait_ge(S("bank_free"), in_block(quarter, 11) + 5)
            pe.wait_ge(S("head_rows_copied"), 2)
            for t in range(TB):
                last = nc.tensor.matmul(by_block(ps[:, 0, :])[:, t], k[:, t], k[:, t], start=True, stop=True)
            last.then_inc(S("kk"), 1)
            for t in range(TB):
                last = nc.tensor.matmul(by_block(ps[:, 1, :])[:, t], k[:, t], q[:, t], start=True, stop=True)
            last.then_inc(S("qk"), 1)
            for t in range(TB):
                last = nc.tensor.transpose(by_block(ps[:, 7, :])[:, t], k[:, t], ident)
            last.then_inc(S("k_turned"), 1)

        def gdn_pe_close(pe, pr):
            for x in range(2):
                pe.wait_ge(S("o_sq"), 2 * pr + x + 1)
                nc.tensor.matmul(ps[:, 2 + x, :], ones, slot("sq", x), start=True, stop=True)\
                    .then_inc(S("o_sum"), 1)

        def gdn_pe_pair(pe, pr):
            quarter, kh = divmod(pr, 2)
            hd = [2 * pr, 2 * pr + 1]
            pe.wait_ge(S("kk_copied"), pr + 1)
            pe.wait_ge(S("qk_copied"), pr + 1)
            if kh:
                pe.wait_ge(S("o_rstd"), 4 * pr - 2)
            for x in range(2):
                pick = PICK[:, hd[x]:hd[x] + 1].to_broadcast([16, P])
                for rows, bank in ((GC_ROWS, 2 * x), (BETA_ROWS, 2 * x + 1)):
                    nc.tensor.matmul(ps[:, bank, :], pick, rows[:, 0, :], start=True, stop=False)
                    last = nc.tensor.matmul(ps[:, bank, :], pick, rows[:, 1, :], start=False, stop=True)
                last.then_inc(S("rows_spread"), 1)
            for t in range(TB):
                last = nc.tensor.transpose(by_block(ps[:, 6, :])[:, t], by_block(VG[:, 2 * kh, :])[:, t], ident)
            last.then_inc(S("v_turned"), 1)
            if kh:
                pe.wait_ge(S("gated"), 2 * pr)
            for x in range(2):
                pe.wait_ge(S(f"xt_ready{x}"), 6 * pr + 1)
                for t in range(TB):
                    last = nc.tensor.transpose(by_block(ps[:, 4 + x, :])[:, t], by_block(slot("xt", x))[:, t], ident)
                last.then_inc(S("x1_turned"), 1)
            for lv in range(1, 6):
                for x in range(2):
                    pe.wait_ge(S(f"c_ready{x}"), 6 * pr + lv + 1)
                    if lv == 1:
                        pe.wait_ge(S("x1_ready"), hd[x] + 1)
                    else:
                        pe.wait_ge(S(f"x_ready{x}"), 4 * pr + lv - 1)
                    for t in range(TB):
                        last = nc.tensor.matmul(by_block(ps[:, 2 * x + 1, :])[:, t], by_block(level_mask(lv, x))[:, t],
                                                by_block(slot("x", x))[:, t], start=True, stop=True)
                    last.then_inc(S(f"cx{x}"), 1)
                for x in range(2):
                    pe.wait_ge(S(f"y_ready{x}"), 5 * pr + lv)
                    pe.wait_ge(S(f"xt_ready{x}"), 6 * pr + lv)
                    y, xt, half = by_block(slot("y", x)), by_block(slot("xt", x)), ps[:, 4 + x, :]
                    if lv < 5:
                        for t in range(TB):
                            last = nc.tensor.matmul(runs(half[:, t * 64:t * 64 + 64], lv), xt[:, t], even(y[:, t], lv),
                                                    start=True, stop=True)
                    for t in range(TB):
                        last = nc.tensor.matmul(runs(half[:, 256 + t * 64:320 + t * 64], lv), y[:, t],
                                                odd(xt[:, t], lv), start=True, stop=True)
                    last.then_inc(S(f"xcx{x}"), 1)
            pe.wait_ge(S("xt_ready1"), 6 * pr + 6)
            for t in range(TB):
                last = nc.tensor.transpose(by_block(ps[:, 5, :])[:, t], by_block(VG[:, 2 * kh + 1, :])[:, t], ident)
            last.then_inc(S("v_turned"), 1)
            for x in range(2):
                xt = by_block(slot("xt", x))
                pe.wait_ge(S(f"xt_ready{x}"), 6 * pr + 6)
                pe.wait_ge(S("kbe"), hd[x] + 1)
                for t in range(TB):
                    last = nc.tensor.matmul(by_block(ps[:, 2 * x + 1, :])[:, t], by_block(slot("kbe", x))[:, t],
                                            xt[:, t], start=True, stop=True)
                last.then_inc(S("wt"), 1)
                pe.wait_ge(S("vb"), hd[x] + 1)
                pe.wait_ge(S("egc_row"), hd[x] + 1)
                for t in range(TB):
                    last = nc.tensor.matmul(by_block(ps[:, 2 * x, :])[:, t], xt[:, t], by_block(slot("vb", x))[:, t],
                                            start=True, stop=True)
                last.then_inc(S("u"), 1)
            pe.wait_ge(S("wt_copied"), hd[1] + 1)
            pe.wait_ge(S("u_copied"), hd[1] + 1)
            pe.wait_ge(S("qd"), hd[1] + 1)
            for ch in range(8):
                t, half = divmod(ch, 2)
                lo, hi, at = 64 * half, 64 * half + 64, ch * 64
                for x in range(2):
                    state = STATE[:, x * P:(x + 1) * P]
                    pe.wait_ge(S(f"state{x}"), 8 * pr + 1 + ch)
                    nc.tensor.matmul(ps[lo:hi, 2 * x, 0:P], slot("wt", x)[:, at:at + 64], state,
                                     start=True, stop=True).then_inc(S(f"w_state{x}"), 1)
                    nc.tensor.matmul(ps[:, 4 + x, at:at + 64], state, slot("qd", x)[:, at:at + 64],
                                     start=True, stop=False)
                for x in range(2):
                    v_new = V_NEW[lo:hi, x * P:(x + 1) * P]
                    pe.wait_ge(S(f"v_new{x}"), 8 * pr + ch + 1)
                    if ch < 7:
                        nc.tensor.matmul(ps[:, 2 * x + 1, 0:P], slot("kdec", x)[lo:hi, t * P:(t + 1) * P], v_new,
                                         start=True, stop=True).then_inc(S(f"kv_new{x}"), 1)
                    last = nc.tensor.matmul(ps[:, 4 + x, at:at + 64], v_new, slot("qkt", x)[lo:hi, at:at + 64],
                                            start=False, stop=True)
                    if ch == 7:
                        last.then_inc(S("heads_done"), 1)

        def gdn_act(act):
            b = FIRST["gdn_ba"]
            lookahead(act, b)
            act.dma_start(phase_const[:, 0:PHASE_W], dram["gdn_const"]).then_inc(S("gdn_const"), 16)
            act.wait_ge(S("block_done"), b + 1)
            nc.scalar.activation(sm_t("beta"), ps[:, b % 4, 0:128].rearrange("p (t c) -> p t c", t=TB)[:, :, 0:16],
                                 ACT.Sigmoid).then_inc(S("beta"), 1)
            nc.scalar.activation(EA, par("a_log", 0, 16), ACT.Exp).then_inc(S("exp_a"), 1)
            act.wait_ge(S("softplus_in"), 1)
            nc.scalar.activation(SM["e"], SM["ax"], ACT.Exp, scale=-1.0).then_inc(S("softplus_exp"), 1)
            act.wait_ge(S("softplus_w"), 1)
            nc.scalar.activation(SM["l"], SM["w"], ACT.Ln).then_inc(S("softplus_ln"), 1)
            def convolve(r, j):
                base = in_block(r, j)
                lookahead(act, base)
                act.wait_ge(S("block_done"), base + 1)
                if j >= 2:
                    act.wait_ge(S("gdn_silu"), 8 * r + j - 1)
                elif r == 0:
                    act.wait_ge(S("log_decay"), 1)
                nc.scalar.activation(GCV[:, j % 2, :], ps[:, j % 4, :], ACT.Copy,
                                     scale=par("gdn_conv", 3 * 32 + 8 * r + j)).then_inc(S("gdn_main"), 1)
                act.wait_ge(S("bank_free"), base + 5)
                dst = (QG[:, j, :] if j < 2 else KG[:, j - 2, :] if j < 4 else VG[:, j - 4, :])
                nc.scalar.activation(dst, GCV[:, j % 2, :], ACT.Silu).then_inc(S("gdn_silu"), 1)

            for r in range(4):
                for j in range(0 if r == 0 else 4, 8):
                    convolve(r, j)
                lookahead(act, in_block(r, 8))
                qk = [QG[:, 0, :], QG[:, 1, :], KG[:, 0, :], KG[:, 1, :]]
                for i in range(4):
                    act.wait_ge(S("gdn_silu"), 8 * r + i + 1)
                    nc.scalar.activation(GSQ[:, i, :], qk[i], ACT.Square).then_inc(S("gdn_sq"), 1)
                lookahead(act, in_block(r, 9))
                load_ln_exp(act)
                for i in range(4):
                    act.wait_ge(S("gdn_sum"), 4 * r + i + 1)
                    nc.scalar.activation(GHR[:, i, :], ps[:, 4 + i, :], ACT.Ln, bias=eps_col)\
                        .then_inc(S("gdn_rstd"), 1)
                for i in range(4):
                    act.wait_ge(S("gdn_rstd"), 8 * r + i + 1)
                    nc.scalar.activation(GHR[:, i, :], GHR[:, i, :], ACT.Exp, scale=-0.5).then_inc(S("gdn_rstd"), 1)
                lookahead(act, in_block(r, 10))
                for i in range(4):
                    if i == 3:
                        lookahead(act, in_block(r, 11))
                    act.wait_ge(S("block_done"), in_block(r, 8 + i) + 1)
                    nc.scalar.activation(ZG[:, i, :], ps[:, i, :], ACT.Sigmoid).then_inc(S("z_gate"), 1)
                load_ln_exp(act)
                if r == 0:
                    act.wait_ge(S("kd_ready"), 1)
                    nc.scalar.activation(SM["egc"], SM["gc"], ACT.Exp).then_inc(S("decays"), 1)
                    nc.scalar.activation(SM["ekd"], SM["kd"], ACT.Exp).then_inc(S("decays"), 1)
                    nc.scalar.activation(view(6144 + 64 * 14, 128), ps[:, 5, 128:256], ACT.Exp)\
                        .then_inc(S("decays"), 1)
                gdn_act_open(act, 2 * r)
                gdn_act_pair(act, 2 * r)
                gdn_act_open(act, 2 * r + 1)
                gdn_act_close(act, 2 * r)
                gdn_act_pair(act, 2 * r + 1)
                gdn_act_close(act, 2 * r + 1)
                if r < 3:
                    for j in range(4):
                        convolve(r + 1, j)
                for j in range(4):
                    lookahead(act, out_block(r, j))

        def gdn_act_open(act, pr):
            act.wait_ge(S("kk"), pr + 1)
            nc.scalar.activation(KK, ps[:, 0, :], ACT.Copy).then_inc(S("kk_copied"), 1)

        def gdn_act_close(act, pr):
            quarter, kh = divmod(pr, 2)
            hd = [2 * pr, 2 * pr + 1]
            for x in range(2):
                act.wait_ge(S("o_sum"), hd[x] + 1)
                nc.scalar.activation(slot("rstd", x), ps[:, 2 + x, :], ACT.Ln, bias=eps_col, scale=1.0 / P)\
                    .then_inc(S("o_rstd"), 1)
            for x in range(2):
                act.wait_ge(S("o_rstd"), 4 * pr + x + 1)
                nc.scalar.activation(slot("rstd", x), slot("rstd", x), ACT.Exp, scale=-0.5).then_inc(S("o_rstd"), 1)
            for x in range(2):
                act.wait_ge(S("gated"), hd[x] + 1)
                nc.scalar.activation(a_hi[:, 2 * kh + x, :], slot("gated", x), ACT.Copy).then_inc(S("gdn_o_hi"), 1)

        def gdn_act_pair(act, pr):
            quarter, kh = divmod(pr, 2)
            hd = [2 * pr, 2 * pr + 1]
            for x in range(2):
                act.wait_ge(S("arg"), hd[x] + 1)
                for t in range(TB):
                    last = nc.scalar.activation(by_block(slot("dt", x))[:, t], by_block(slot("arg", x))[:, t], ACT.Exp,
                                                bias=sm_t("neg_gc")[:, t, hd[x]:hd[x] + 1])
                last.then_inc(S("dt"), 1)
            for x in range(2):
                act.wait_ge(S("x1_turned"), hd[x] + 1)
                nc.scalar.activation(slot("x", x), ps[:, 4 + x, :], ACT.Copy).then_inc(S("x1_ready"), 1)
            act.wait_ge(S("qkt"), 2 * pr + 2)
            for lv in range(1, 6):
                for x in range(2):
                    act.wait_ge(S(f"cx{x}"), 5 * pr + lv)
                    if lv > 1:
                        act.wait_ge(S(f"xcx{x}"), 5 * pr + lv - 1)
                    nc.scalar.activation(slot("y", x), ps[:, 2 * x + 1, :], ACT.Copy).then_inc(S(f"y_ready{x}"), 1)
            for x in range(2):
                act.wait_ge(S(f"x_ready{x}"), 4 * pr + 4)
                act.wait_ge(S(f"cx{x}"), 5 * pr + 5)
                nc.scalar.activation(slot("qd", x), ps[:, 2 * x, :], ACT.Exp).then_inc(S("egc_row"), 1)
            for x in range(2):
                act.wait_ge(S("wt"), hd[x] + 1)
                nc.scalar.activation(slot("wt", x), ps[:, 2 * x + 1, :], ACT.Copy).then_inc(S("wt_copied"), 1)
                act.wait_ge(S("u"), hd[x] + 1)
                nc.scalar.activation(VG[:, 2 * kh + x, :], ps[:, 2 * x, :], ACT.Copy).then_inc(S("u_copied"), 1)
            for x in range(2):
                act.wait_ge(S("heads_done"), hd[x] + 1)
                nc.scalar.activation(slot("sq", x), ps[:, 4 + x, :], ACT.Square).then_inc(S("o_sq"), 1)

        def gdn_dve(dve):
            b = FIRST["gdn_ba"]
            logits = ps[:, b % 4, 0:128].rearrange("p (t c) -> p t c", t=TB)
            dve.wait_ge(S("beta"), 1)
            nc.vector.tensor_tensor(sm_t("xa"), logits[:, :, 16:32],
                                    par("dt_bias", 0, 16)[:, None, :].to_broadcast([P, TB, 16]), ALU.add)\
                .then_inc(S("bank_free"), 1)
            dve.wait_ge(S("bank_free"), b + 5)
            link(dve, nc.vector.tensor_scalar(SM["w"], SM["xa"], -1.0, None, ALU.mult))
            nc.vector.tensor_tensor(SM["ax"], SM["xa"], SM["w"], ALU.max).then_inc(S("softplus_in"), 1)
            dve.wait_ge(S("softplus_exp"), 1)
            nc.vector.tensor_scalar(SM["w"], SM["e"], 1.0, None, ALU.add).then_inc(S("softplus_w"), 1)
            dve.wait_ge(S("softplus_w"), 1)
            link(dve, nc.vector.tensor_scalar(SM["w1"], SM["w"], -1.0, None, ALU.add))
            link(dve, nc.vector.tensor_tensor(SM["w1"], SM["e"], SM["w1"], ALU.subtract))
            link(dve, nc.vector.reciprocal(SM["kd"], SM["w"]))
            link(dve, nc.vector.tensor_tensor(SM["w1"], SM["w1"], SM["kd"], ALU.mult))
            dve.wait_ge(S("softplus_ln"), 1)
            link(dve, nc.vector.tensor_tensor(SM["l"], SM["l"], SM["w1"], ALU.add))
            link(dve, nc.vector.tensor_scalar(SM["xa"], SM["xa"], 0.0, None, ALU.max))
            link(dve, nc.vector.tensor_tensor(SM["l"], SM["l"], SM["xa"], ALU.add))
            dve.wait_ge(S("exp_a"), 1)
            link(dve, nc.vector.tensor_tensor(sm_t("g"), sm_t("l"), EA[:, None, :].to_broadcast([P, TB, 16]),
                                              ALU.mult))
            nc.vector.tensor_scalar(SM["g"], SM["g"], -1.0, None, ALU.mult).then_inc(S("log_decay"), 1)
            def convolve(r, j):
                dve.wait_ge(S("gdn_main"), 8 * r + j + 1)
                for tap in (2, 1, 0):
                    s = 3 - tap
                    ins = nc.vector.scalar_tensor_tensor(
                        out=GCV[:, j % 2, s:T], in0=ps[:, j % 4, 0:T - s],
                        scalar=par("gdn_conv", 32 * tap + 8 * r + j), in1=GCV[:, j % 2, s:T],
                        op0=ALU.mult, op1=ALU.add)
                    if tap:
                        link(dve, ins)
                    else:
                        ins.then_inc(S("bank_free"), 1)

            for quarter in range(4):
                for j in range(0 if quarter == 0 else 4, 8):
                    convolve(quarter, j)
                qk = [QG[:, 0, :], QG[:, 1, :], KG[:, 0, :], KG[:, 1, :]]
                for i in range(4):
                    dve.wait_ge(S("gdn_rstd"), 8 * quarter + 5 + i)
                    nc.vector.scalar_tensor_tensor(out=qk[i], in0=qk[i], scalar=P ** -0.5 if i < 2 else 1.0,
                                                   in1=GHR[:, i, :], op0=ALU.mult, op1=ALU.mult)\
                        .then_inc(S("gdn_unit"), 1)
                if quarter == 0:
                    dve.wait_ge(S("log_decay_sums"), 1)
                    nc.vector.tensor_copy(SM["gc"], ps[:, 5, 0:64]).then_inc(S("gc_copied"), 1)
                    dve.wait_ge(S("gc_copied"), 1)
                    link(dve, nc.vector.tensor_scalar(SM["neg_gc"], SM["gc"], -1.0, None, ALU.mult))
                    nc.vector.tensor_tensor(SM["kd"], ps[:, 5, 64:128], SM["gc"], ALU.subtract)\
                        .then_inc(S("kd_ready"), 1)
                    dve.wait_ge(S("head_rows"), 1)
                    link(dve, nc.vector.tensor_copy(PICK, common[0:16, 0:16]))
                    for rows, bank in ((GC_ROWS, 6), (BETA_ROWS, 7)):
                        link(dve, nc.vector.tensor_copy(rows[:, 0, :], ps[0:16, bank, :]))
                        nc.vector.tensor_tensor(rows[:, 1, :], ps[0:16, bank, :], rows[:, 0, :].bitcast(F32),
                                                ALU.subtract).then_inc(S("head_rows_copied"), 1)
                    dve.wait_ge(S("decays"), 3)
                    link(dve, nc.vector.tensor_tensor(SM["beg"], SM["beta"], SM["egc"], ALU.mult))
                for i in range(4):
                    dve.wait_ge(S("z_gate"), 4 * quarter + i + 1)
                    nc.vector.tensor_tensor(ZG[:, i, :], ZG[:, i, :], ps[:, i, :], ALU.mult)\
                        .then_inc(S("bank_free"), 1)
                gdn_dve_open(dve, 2 * quarter)
                gdn_dve_pair(dve, 2 * quarter)
                gdn_dve_open(dve, 2 * quarter + 1)
                gdn_dve_close(dve, 2 * quarter)
                gdn_dve_pair(dve, 2 * quarter + 1)
                gdn_dve_close(dve, 2 * quarter + 1)
                if quarter < 3:
                    for j in range(4):
                        convolve(quarter + 1, j)
                if quarter == 3:
                    squares_begin(dve, 3)
                for j in range(4):
                    base = out_block(quarter, j)
                    dve.wait_ge(S("block_done"), base + 1)
                    at = h[:, 2 * j:2 * j + 2, :]
                    src = ps[:, 2 * (j % 2):2 * (j % 2) + 2, :]
                    dve.wait_ge(S("bank_free"), base + 4)
                    nc.vector.tensor_tensor(at, at, src, ALU.add).then_inc(S("bank_free"), 1)
                    if quarter == 3:
                        dve.wait_ge(S("bank_free"), base + 5)
                        for z in range(2):
                            square_dve(dve, 3, 0, 2 * j + z)

        def gdn_dve_open(dve, pr):
            dve.wait_ge(S("gdn_unit"), 4 * (pr // 2) + 4)
            if pr:
                dve.wait_ge(S("heads_done"), 2 * pr)
            for x in range(2):
                if pr:
                    dve.wait_ge(S(f"state{x}"), 8 * pr)
                nc.vector.memset(STATE[:, x * P:(x + 1) * P], 0.0).then_inc(S(f"state{x}"), 1)
            dve.wait_ge(S("qk"), pr + 1)
            nc.vector.tensor_copy(QK, ps[:, 1, :]).then_inc(S("qk_copied"), 1)

        def gdn_dve_close(dve, pr):
            quarter, kh = divmod(pr, 2)
            hd = [2 * pr, 2 * pr + 1]
            for x in range(2):
                dve.wait_ge(S("o_rstd"), 4 * pr + 3 + x)
                link(dve, nc.vector.scalar_tensor_tensor(out=slot("gated", x), in0=ps[:, 4 + x, :],
                                                         scalar=par("gdn_norm"), in1=slot("rstd", x),
                                                         op0=ALU.mult, op1=ALU.mult))
                nc.vector.tensor_tensor(slot("gated", x), slot("gated", x), ZG[:, 2 * kh + x, :], ALU.mult)\
                    .then_inc(S("gated"), 1)
            for x in range(2):
                dve.wait_ge(S("gated"), hd[x] + 1)
                dve.wait_ge(S("gdn_o_hi"), hd[x] + 1)
                nc.vector.tensor_tensor(a_lo[:, 2 * kh + x, :], slot("gated", x),
                                        a_hi[:, 2 * kh + x, :].bitcast(F32), ALU.subtract)\
                    .then_inc(S("gdn_o_lo"), 1)

        def gdn_dve_pair(dve, pr):
            quarter, kh = divmod(pr, 2)
            hd = [2 * pr, 2 * pr + 1]
            ident_all = common[:, None, 0:128].to_broadcast([P, TB, P])

            def col(name, x):
                return sm_t(name)[:, :, hd[x]:hd[x] + 1].to_broadcast([P, TB, P])

            if pr:
                dve.wait_ge(S("gdn_o_lo"), hd[0])
            for x in range(2):
                dve.wait_ge(S("rows_spread"), hd[x] + 1)
                nc.vector.tensor_tensor(by_block(slot("arg", x)), by_block(ps[:, 2 * x, :]), gdn_mask("decay_mask"),
                                        ALU.add).then_inc(S("arg"), 1)
            dve.wait_ge(S("kk_copied"), pr + 1)
            dve.wait_ge(S("qk_copied"), pr + 1)
            for x in range(2):
                dve.wait_ge(S("dt"), hd[x] + 1)
                link(dve, nc.vector.tensor_tensor(slot("mt", x), KK, slot("dt", x), ALU.mult))
                link(dve, nc.vector.tensor_tensor(slot("mt", x), slot("mt", x), ps[:, 2 * x + 1, :], ALU.mult))
                nc.vector.tensor_tensor(by_block(slot("c", x)), by_block(slot("mt", x)), gdn_mask("levels", 0),
                                        ALU.mult).then_inc(S(f"c_ready{x}"), 1)
                dve.wait_ge(S(f"c_ready{x}"), 6 * pr + 1)
                nc.vector.tensor_tensor(by_block(slot("xt", x)), ident_all, by_block(slot("c", x)), ALU.subtract)\
                    .then_inc(S(f"xt_ready{x}"), 1)
                dve.wait_ge(S(f"xt_ready{x}"), 6 * pr + 1)
                nc.vector.tensor_tensor(by_block(slot("c", x)), by_block(slot("mt", x)), gdn_mask("levels", 1),
                                        ALU.mult).then_inc(S(f"c_ready{x}"), 1)
            for x in range(2):
                nc.vector.tensor_tensor(slot("qkt", x), QK, slot("dt", x), ALU.mult).then_inc(S("qkt"), 1)
            dve.wait_ge(S("qkt"), 2 * pr + 2)
            for lv in range(1, 6):
                for x in range(2):
                    if lv < 5:
                        if lv > 1:
                            dve.wait_ge(S(f"cx{x}"), 5 * pr + lv - 1)
                        nc.vector.tensor_tensor(by_block(level_mask(lv + 1, x)), by_block(slot("mt", x)),
                                                gdn_mask("levels", lv + 1), ALU.mult)\
                            .then_inc(S(f"c_ready{x}"), 1)
                for x in range(2):
                    dve.wait_ge(S(f"xcx{x}"), 5 * pr + lv)
                    if lv < 5:
                        if lv == 1:
                            dve.wait_ge(S("x1_ready"), hd[x] + 1)
                        else:
                            dve.wait_ge(S(f"x_ready{x}"), 4 * pr + lv - 1)
                        at = even(slot("x", x), lv)
                        nc.vector.tensor_tensor(at, at, runs(ps[:, 4 + x, 0:256], lv), ALU.subtract)\
                            .then_inc(S(f"x_ready{x}"), 1)
                    dve.wait_ge(S(f"xt_ready{x}"), 6 * pr + lv)
                    at = odd(slot("xt", x), lv)
                    nc.vector.tensor_tensor(at, at, runs(ps[:, 4 + x, 256:512], lv), ALU.subtract)\
                        .then_inc(S(f"xt_ready{x}"), 1)
            for x in range(2):
                k_tok = by_block(ps[:, 7, :])
                dve.wait_ge(S("k_turned"), pr + 1)
                dve.wait_ge(S(f"xcx{x}"), 5 * pr + 5)
                nc.vector.tensor_tensor(by_block(slot("kbe", x)), k_tok, col("beg", x), ALU.mult)\
                    .then_inc(S("kbe"), 1)
                dve.wait_ge(S("v_turned"), hd[x] + 1)
                nc.vector.tensor_tensor(by_block(slot("vb", x)), by_block(ps[:, 6 - x, :]), col("beta", x), ALU.mult)\
                    .then_inc(S("vb"), 1)
                nc.vector.tensor_tensor(by_block(slot("kdec", x)), k_tok, col("ekd", x), ALU.mult)\
                    .then_inc(S("kdec"), 1)
                dve.wait_ge(S("egc_row"), hd[x] + 1)
                nc.vector.tensor_tensor(slot("qd", x), slot("qd", x), QG[:, kh, :], ALU.mult).then_inc(S("qd"), 1)
            for ch in range(8):
                t, half = divmod(ch, 2)
                lo, hi = 64 * half, 64 * half + 64
                if ch == 0:
                    dve.wait_ge(S("u_copied"), 2 * pr + 2)
                for x in range(2):
                    dve.wait_ge(S(f"w_state{x}"), 8 * pr + ch + 1)
                    nc.vector.tensor_tensor(V_NEW[lo:hi, x * P:(x + 1) * P], VG[lo:hi, 2 * kh + x, t * P:(t + 1) * P],
                                            ps[lo:hi, 2 * x, 0:P], ALU.subtract).then_inc(S(f"v_new{x}"), 1)
                for x in range(2):
                    if ch == 7:
                        continue
                    dve.wait_ge(S(f"kv_new{x}"), 7 * pr + ch + 1)
                    dve.wait_ge(S(f"state{x}"), 8 * pr + 1 + ch)
                    col_at = t * 16 + hd[x]
                    nc.vector.scalar_tensor_tensor(
                        out=STATE[:, x * P:(x + 1) * P], in0=STATE[:, x * P:(x + 1) * P],
                        scalar=SM[f"gl{half}"][:, col_at:col_at + 1], in1=ps[:, 2 * x + 1, 0:P],
                        op0=ALU.mult, op1=ALU.add).then_inc(S(f"state{x}"), 1)

        def ada_bias_dve(dve, layer):
            at, n = layer * N_ADA // 2, N_ADA // 2
            dve.wait_ge(S("ada_kept"), 2 + at + n)
            link(dve, nc.vector.tensor_tensor(mod[:, at:at + n], mod[:, at:at + n], par("b_ada", at, n), ALU.add))

        def modulation_dve(dve):
            for v, name in enumerate(("g_ffn1", "g_mix", "g_ffn2")):
                link(dve, nc.vector.scalar_tensor_tensor(
                    out=gains[:, v * KT:(v + 1) * KT], in0=mod[:, (3 * v + 1) * KT:(3 * v + 2) * KT], scalar=1.0,
                    in1=par(name, 0, KT), op0=ALU.add, op1=ALU.mult))
            for v in (2, 8):
                at = mod[:, v * KT:(v + 1) * KT]
                link(dve, nc.vector.tensor_scalar(at, at, 0.5, None, ALU.mult))

        FINAL = view(2560, KT, T)

        def final_dve(dve):
            dve.wait_ge(S("rstd_ready"), 16)
            for k in range(KT):
                nc.vector.scalar_tensor_tensor(out=FINAL[:, k, :], in0=h[:, k, :], scalar=par("g_final", k),
                                               in1=RSTD, op0=ALU.mult, op1=ALU.mult).then_inc(S("final_ready"), 1)

        def mat(at, n, dt):
            return arena[:, at:at + n // 2].bitcast(dt)

        QA = view(0, T, 4)
        KA, VA, WI = view(2048, T), view(2560, TB, 64), view(2816, TB, 8)
        QI, KI = view(2848, 4, T), view(4896, T)
        QNOPE, QP, KN, VB, KP = view(5408, 4, T), view(7456, 2, T), view(8480, 4, T), view(10528, TB, T), view(12576, T)
        COS2, SIN2 = view(13088, T), view(13600, T)
        ROPE2_SCRATCH = 14112
        POS = view(14112, T)
        TURN1, TURN2 = view(14624, T), view(15136, T)
        LAT = view(5408, 5, T)
        LSQ, LRSTD, LNT = view(8480, 2, T), view(9504, 2, T), view(10528, 2, T)
        RELU, TOP = view(13088, 2, T), view(15776, 8)
        ACC = {1: view(14624, 2 * P), 2: view(14624 + 2 * P, 3 * P), 3: view(14624 + 5 * P, 4 * P)}
        PENAL = mat(3360, TB * T, BF16).rearrange("p (n k) -> p n k", n=TB)
        REP, REP_WORDS = mat(2848, KT * P, BF16), view(2848, KT * P // 2)
        QCOL, DELTA, TABLE = view(4896, P), view(5024, 8), view(5040, P)
        LIMIT_BF, IDENT_BF = mat(5168, P, BF16), mat(5232, P, BF16)
        PR, PT = view(13088, 2, T), (view(4384, T), phase_const[:, MIX_W:MIX_W + T])
        ST = view(15784, 2, 4)
        LIMIT = phase_const[:, MIX_AT["limit"]:MIX_AT["limit"] + P]
        THRESHOLD = common[:, COMMON_AT["thresholds"]:COMMON_AT["thresholds"] + 1]
        MLA_SCALE = 96 ** -0.5
        TAKEN = -3e38
        UNITS = 64

        def unit(u):
            return u < 32, u % 32 // 8, u % 8

        def mix_sp(sp):
            load_block(sp, FIRST["mix_v"], 0, dram["mix_v"][0], 576)
            b = FIRST["mix_in"]
            with sp.Fori(0, 4) as i:
                for j in range(4):
                    load_block(sp, b + j, i, dram["mix_in"][bass.ds(i * 4 + j, 1)].rearrange("a p n -> (a p) n"), BW)
            for j in range(3):
                load_block(sp, FIRST["uq"] + j, 0, dram["uq"][j], 768)
            for j in range(2):
                load_block(sp, FIRST["ukv"] + j, 0, dram["ukv"][j], BW)
            b = FIRST["mix_out"]
            with sp.Fori(0, 2) as i:
                for j in range(12):
                    load_block(sp, b + j, i * 3, dram["mix_out"][bass.ds(i * 12 + j, 1)]
                               .rearrange("a p n -> (a p) n"), BW)
            b = FIRST["w_out"]
            with sp.Fori(0, 2) as i:
                for j in range(4):
                    load_block(sp, b + j, i, dram["w_out"][bass.ds(i * 4 + j, 1)].rearrange("a p n -> (a p) n"), BW)

        def mix_pe(pe):
            b = FIRST["mix_v"]
            pe.wait_ge(S("lo_ready"), b + 1)
            pe.wait_ge(S("bank_free"), b + 1)
            for t in range(TB):
                for k in range(KT):
                    if t == 0:
                        u_tile(5)(k)
                    c = k * 72
                    last = product(ps[:, b % 4, t * 72:t * 72 + 72], u_hi[:, k, t * P:(t + 1) * P],
                                   u_lo[:, k, t * P:(t + 1) * P], w_hi[:, b % RING, c:c + 72],
                                   w_lo[:, b % RING, c:c + 72], k == 0, k == KT - 1)
            last.then_inc(S("block_done"), 1)
            b = FIRST["mix_in"]
            with pe.Fori(0, 4) as i:
                for j in range(4):
                    block_matmul(pe, b + j, i, u_hi, u_lo)
            for i in range(5):
                pe.wait_ge(S("lat_sq"), i + 1)
                nc.tensor.matmul(ps[:, 4 + (i >= 3), :], ones, LSQ[:, i % 2, :], start=i in (0, 3), stop=i in (2, 4))\
                    .then_inc(S("lat_sum"), 1)
            b = FIRST["uq"]
            pe.wait_ge(S("bank_free"), b + 4)
            for j in range(3):
                pe.wait_ge(S("lat_lo"), 3)
                pe.wait_ge(S("lo_ready"), b + j + 1)
                if j == 2:
                    pe.wait_ge(S("bank_free"), b + 5)
                for z in range(2):
                    last = out_tile(ps[:, 2 * (j % 2) + z, :], (b + j) % RING, a_hi, a_lo, 3, 3 * z)
                last.then_inc(S("block_done"), 1)
            b = FIRST["ukv"]
            pe.wait_ge(S("lat_lo"), 5)
            pe.wait_ge(S("lo_ready"), b + 1)
            for z in range(4):
                last = out_tile(ps[:, 4 + z, :], b % RING, a_hi, a_lo, 2, 2 * z, 3)
            last.then_inc(S("block_done"), 1)
            b += 1
            pe.wait_ge(S("lo_ready"), b + 1)
            pe.wait_ge(S("bank_free"), b + 3)
            for t in range(TB):
                for k in range(2):
                    last = product(ps[:, t, :], a_hi[:, 3 + k, t * P:(t + 1) * P], a_lo[:, 3 + k, t * P:(t + 1) * P],
                                   w_hi[:, b % RING, k * T:(k + 1) * T], w_lo[:, b % RING, k * T:(k + 1) * T],
                                   k == 0, k == 1)
            last.then_inc(S("block_done"), 1)
            pe.wait_ge(S("bank_free"), b + 5)
            pe.wait_ge(S("mix_const"), 16)
            for i, src in enumerate((KP, QP[:, 0, :], QP[:, 1, :])):
                nc.tensor.matmul(ps[:, 4 + i, :], ROTM, src, start=True, stop=True).then_inc(S("turned2"), 1)
            for v in range(24):
                n, hd = v // 8 + 1, v % 8
                o = 64 * (hd % 2)
                if v >= 4:
                    pe.wait_ge(S("idx_relu"), v - 3)
                nc.tensor.matmul(ps[:, v % 4, 0:(n + 1) * P], QI[o:o + 64, hd // 2, n * P:(n + 1) * P],
                                 KI[o:o + 64, 0:(n + 1) * P], start=True, stop=True).then_inc(S("idx_scored"), 1)

            def scores(u):
                latent, n, m = unit(u)
                w = (n + 1) * P
                dst = ps[:, u % 2, 0:w]
                if u >= 2:
                    pe.wait_ge(S("att_exp"), u - 1)
                if latent:
                    o, r = 64 * (m % 2), 32 * (m % 4)
                    nc.tensor.matmul(dst, QNOPE[o:o + 64, m // 2, n * P:(n + 1) * P], KN[o:o + 64, m // 2, 0:w],
                                     start=True, stop=False, skip_group_check=True)
                    nc.tensor.matmul(dst, QP[r:r + 32, m // 4, n * P:(n + 1) * P], KP[r:r + 32, 0:w],
                                     start=False, stop=False, skip_group_check=True)
                    nc.tensor.matmul(ps[:, u % 2, n * P:w], IDENT_BF, LIMIT_BF, start=False, stop=True,
                                     skip_group_check=True).then_inc(S("att_scored"), 1)
                    return
                if u == 32:
                    pe.wait_ge(S("rep_landed"), 16)
                    pe.wait_ge(S("tables"), 1)
                pe.wait_ge(S("penal"), n + 1)
                nc.tensor.matmul(dst, REP[:, m * P:(m + 1) * P], PENAL[:, n, 0:w], start=True, stop=False,
                                 skip_group_check=True)
                g, tok = u - 32, n * P + m * 16
                for z in range(2):
                    nc.tensor.matmul(ps[64 * z:64 * z + 64, u % 2, 0:w],
                                     QA[64 * z:64 * z + 64, tok:tok + 16, :].rearrange("p t h -> p (t h)"),
                                     KA[64 * z:64 * z + 64, 0:w], start=False, stop=False, skip_group_check=True)
                for j in range(4):
                    pe.wait_ge(S("steps"), 4 * g + j + 1)
                    nc.tensor.matmul(dst, table_hi[:, j, :], onehot[:, j % 2, 0:w], start=False, stop=False,
                                     skip_group_check=True)
                    last = nc.tensor.matmul(dst, table_lo[:, j, :], onehot[:, j % 2, 0:w], start=False, stop=j == 3,
                                            skip_group_check=True)
                    if j < 3:
                        last.then_inc(S("steps_used"), 1)
                last.then_inc(S("att_scored"), 1)

            def values(u):
                latent, n, m = unit(u)
                pe.wait_ge(S("att_pt"), u + 1)
                if m == 0 and u >= 16:
                    pe.wait_ge(S("att_lo"), u // 8 - 1)
                bank = 4 + u // 8 % 2
                for kb in range(n + 1):
                    if latent:
                        o, hp = 64 * (m % 2), m // 2
                        last = nc.tensor.matmul(ps[o:o + 64, bank, hp * P:(hp + 1) * P], VB[:, kb, m * 64:m * 64 + 64],
                                                PT[u % 2][:, kb * P:(kb + 1) * P], start=kb == 0, stop=kb == n)
                if not latent:
                    for z in range(2):
                        for kb in range(n + 1):
                            last = nc.tensor.matmul(ps[64 * z:64 * z + 64, bank, m * 64:m * 64 + 64], VA[:, kb, :],
                                                    PT[u % 2][:, kb * P + 64 * z:kb * P + 64 * z + 64],
                                                    start=kb == 0, stop=kb == n)
                last.then_inc(S("att_pv"), 1)

            pe.wait_ge(S("masks"), 1)
            pe.wait_ge(S("roped2"), 3)
            pe.wait_ge(S("idx_relu"), 24)
            scores(0)
            for u in range(UNITS):
                if u + 1 < UNITS:
                    scores(u + 1)
                pe.wait_ge(S("att_probs"), u + 1)
                if u >= 2:
                    pe.wait_ge(S("att_pt"), u - 1)
                for kb in range(unit(u)[1] + 1):
                    last = nc.tensor.transpose(ps[:, 2 + u % 2, kb * P:(kb + 1) * P],
                                               PR[:, u % 2, kb * P:(kb + 1) * P], ident)
                last.then_inc(S("att_turned"), 1)
                if u:
                    values(u - 1)
            values(UNITS - 1)
            pe.wait_ge(S("att_exp"), UNITS)
            b = FIRST["mix_out"]
            with pe.Fori(0, 2) as i:
                for j in range(4):
                    c, bank = b + 3 * j, 4 * (j % 2)
                    pe.wait_ge(S("bank_free"), num(c, i * 3, 1))
                    for z in range(2):
                        pe.wait_ge(S("lo_ready"), num(c + z, i * 3, 1))
                        out_tile(ps[:, bank + z, :], (c + z) % RING, u_hi, u_lo, KT).then_inc(S("block_done"), 1)
                    pe.wait_ge(S("lo_ready"), num(c + 2, i * 3, 1))
                    pe.wait_ge(S("att_lo"), 8)
                    out_tile(ps[:, bank + 2, :], (c + 2) % RING, a_hi, a_lo, 4)
                    out_tile(ps[:, bank + 3, :], (c + 2) % RING, a_hi, a_lo, 4, 4, 4).then_inc(S("block_done"), 1)
            b = FIRST["w_out"]
            with pe.Fori(0, 2) as i:
                for j in range(4):
                    block_matmul(pe, b + j, i, a_hi, a_lo,
                                 ready=(lambda k: pe.wait_ge(S("y_lo"), k + 1)) if j == 0 else None)

        GATES, PROD, Y = view(0, 2, 2, T), view(2048, 2, 2, T), view(4096, KT, T)

        def mix_act(act):
            rope_act(act, 1, COS2, SIN2)
            for base in range(FIRST["mix_v"], FIRST["mix_out"]):
                lookahead(act, base)
                if base < FIRST["uq"]:
                    continue
                if base == FIRST["uq"]:
                    for i in range(5):
                        act.wait_ge(S("bank_free"), FIRST["mix_in"] + 10 + i + 5)
                        if i >= 2:
                            act.wait_ge(S("lat_sum"), i - 1)
                        nc.scalar.activation(LSQ[:, i % 2, :], LAT[:, i, :], ACT.Square).then_inc(S("lat_sq"), 1)
                    for i in range(2):
                        act.wait_ge(S("lat_sum"), 3 + 2 * i)
                        nc.scalar.activation(LRSTD[:, i, :], ps[:, 4 + i, :], ACT.Ln, bias=eps_col,
                                             scale=1.0 / (384, 256)[i]).then_inc(S("lat_rstd"), 1)
                    for i in range(2):
                        act.wait_ge(S("lat_rstd"), 1 + i)
                        nc.scalar.activation(LRSTD[:, i, :], LRSTD[:, i, :], ACT.Exp, scale=-0.5)\
                            .then_inc(S("lat_rstd"), 1)
                    for i in range(5):
                        act.wait_ge(S("lat_normed"), i + 1)
                        nc.scalar.activation(a_hi[:, i, :], LNT[:, i % 2, :], ACT.Copy).then_inc(S("lat_hi"), 1)
            for v in range(24):
                act.wait_ge(S("idx_scored"), v + 1)
                if v >= 2:
                    act.wait_ge(S("idx_acc"), v - 1)
                w = (v // 8 + 2) * P
                if v == 0:
                    act.wait_ge(S("roped2"), 3)
                nc.scalar.activation(RELU[:, v % 2, 0:w], ps[:, v % 4, 0:w], ACT.Relu, scale=0.125)\
                    .then_inc(S("idx_relu"), 1)
            act.wait_ge(S("idx_acc"), 24)
            act.dma_start(REP_WORDS, dram["rep_const"]).then_inc(S("rep_landed"), 16)

            def exps(u):
                w = (unit(u)[1] + 1) * P
                act.wait_ge(S("att_max"), u + 1)
                if u >= 2:
                    act.wait_ge(S("att_turned"), u - 1)
                nc.scalar.activation(PR[:, u % 2, 0:w], ps[:, u % 2, 0:w], ACT.Exp, bias=ST[:, u % 2, 1:2],
                                     scale=MLA_SCALE if unit(u)[0] else 1.0, accum_out=ST[:, u % 2, 2:3])\
                    .then_inc(S("att_exp"), 1)

            def heads_out(blk):
                act.wait_ge(S("att_pv"), 8 * blk + 8)
                dst, src = out_heads(blk)
                nc.scalar.activation(dst(a_hi), src, ACT.Copy).then_inc(S("att_hi"), 1)

            exps(0)
            for u in range(UNITS):
                act.wait_ge(S("att_turned"), u + 1)
                if u >= 2:
                    act.wait_ge(S("att_pv"), u - 1)
                w = (unit(u)[1] + 1) * P
                nc.scalar.activation(PT[u % 2][:, 0:w], ps[:, 2 + u % 2, 0:w], ACT.Copy).then_inc(S("att_pt"), 1)
                if u + 1 < UNITS:
                    exps(u + 1)
                if u and u % 8 == 0:
                    heads_out(u // 8 - 1)
            heads_out(7)
            b = FIRST["mix_out"]
            with act.Fori(0, 2) as i:
                for j in range(4):
                    c, bank = b + 3 * j, 4 * (j % 2)
                    for z in range(2):
                        lookahead(act, c + z, i * 3)
                        act.wait_ge(S("block_done"), num(c + z, i * 3, 1))
                        act.wait_ge(S("bank_free"), num(c, i * 3, 1))
                        nc.scalar.activation(GATES[:, j % 2, z, :], ps[:, bank + z, :], ACT.Sigmoid)\
                            .then_inc(S("gate2"), 1)
                    lookahead(act, c + 2, i * 3)
            act.wait_ge(S("bank_free"), FIRST["w_out"] + 4)
            for k in range(KT):
                nc.scalar.activation(a_hi[:, k, :], Y[:, k, :], ACT.Copy).then_inc(S("y_hi"), 1)
            b = FIRST["w_out"]
            with act.Fori(0, 2) as i:
                for j in range(4):
                    lookahead(act, b + j, i)

        def out_heads(blk):
            n, bank = blk % 4, 4 + blk % 2
            at = 4 if blk < 4 else 0
            order = "p (h t) -> p h t" if blk < 4 else "p (t h) -> p h t"
            return lambda a: a[:, at:at + 4, n * P:(n + 1) * P], ps[:, bank, :].rearrange(order, h=4)

        def mix_dve(dve):
            b = FIRST["mix_v"]
            dve.wait_ge(S("block_done"), b + 1)
            src = ps[:, b % 4, 0:288].rearrange("p (t c) -> p t c", t=TB)
            link(dve, nc.vector.tensor_copy(VA, src[:, :, 0:64]))
            nc.vector.tensor_scalar(WI, src[:, :, 64:72], 8 ** -0.5, None, ALU.mult).then_inc(S("bank_free"), 1)
            b = FIRST["mix_in"]
            for j in range(16):
                dve.wait_ge(S("block_done"), b + j + 1)
                src = ps[:, (b + j) % 4, :]
                if j < 4:
                    nc.vector.tensor_scalar(QA[:, :, j:j + 1], src[:, :, None], 0.125, None, ALU.mult)\
                        .then_inc(S("bank_free"), 1)
                    continue
                dst = KA if j == 4 else QI[:, j - 5, :] if j < 9 else KI if j == 9 else \
                    LAT[:, j - 10, :] if j < 15 else KP
                nc.vector.tensor_copy(dst, src).then_inc(S("bank_free"), 1)
            for i in range(5):
                dve.wait_ge(S("bank_free"), b + 5 + 15)
                dve.wait_ge(S("lat_rstd"), 3 + (i >= 3))
                if i >= 2:
                    dve.wait_ge(S("lat_hi"), i - 1)
                    dve.wait_ge(S("lat_lo"), i - 1)
                nc.vector.scalar_tensor_tensor(out=LNT[:, i % 2, :], in0=LAT[:, i, :],
                                               scalar=par("g_cq", i) if i < 3 else par("g_ckv", i - 3),
                                               in1=LRSTD[:, int(i >= 3), :], op0=ALU.mult, op1=ALU.mult)\
                    .then_inc(S("lat_normed"), 1)
                dve.wait_ge(S("lat_normed"), i + 1)
                dve.wait_ge(S("lat_hi"), i + 1)
                nc.vector.tensor_tensor(a_lo[:, i, :], LNT[:, i % 2, :], a_hi[:, i, :].bitcast(F32), ALU.subtract)\
                    .then_inc(S("lat_lo"), 1)
            b = FIRST["uq"]
            dve.wait_ge(S("lat_lo"), 5)
            for j in range(3):
                dve.wait_ge(S("block_done"), b + j + 1)
                dst = QNOPE[:, 2 * j:2 * j + 2, :] if j < 2 else QP
                nc.vector.tensor_copy(dst, ps[:, 2 * (j % 2):2 * (j % 2) + 2, :]).then_inc(S("bank_free"), 1)
            b = FIRST["ukv"]
            dve.wait_ge(S("block_done"), b + 1)
            nc.vector.tensor_copy(KN, ps[:, 4:8, :]).then_inc(S("bank_free"), 1)
            dve.wait_ge(S("block_done"), b + 2)
            nc.vector.tensor_copy(VB, ps[:, 0:4, :]).then_inc(S("bank_free"), 1)
            dve.wait_ge(S("bank_free"), b + 6)
            dve.wait_ge(S("rope_table"), 4)
            for i, at in enumerate((KP, QP[:, 0, :], QP[:, 1, :])):
                dve.wait_ge(S("turned2"), i + 1)
                link(dve, nc.vector.tensor_tensor(TURN1, at, COS2, ALU.mult))
                link(dve, nc.vector.tensor_tensor(TURN2, ps[:, 4 + i, :], SIN2, ALU.mult))
                nc.vector.tensor_tensor(at, TURN1, TURN2, ALU.add).then_inc(S("roped2"), 1)
                dve.wait_ge(S("roped2"), i + 1)
            dve.wait_ge(S("mix_const"), 16)
            for n in range(1, 4):
                w = (n + 1) * P
                acc = ACC[n]
                for hd in range(8):
                    v = 8 * (n - 1) + hd
                    dve.wait_ge(S("idx_relu"), v + 1)
                    if hd == 0:
                        nc.vector.tensor_scalar(acc, RELU[:, v % 2, 0:w], WI[:, n, 0:1], None, ALU.mult)\
                            .then_inc(S("idx_acc"), 1)
                    else:
                        nc.vector.scalar_tensor_tensor(out=acc, in0=RELU[:, v % 2, 0:w], scalar=WI[:, n, hd:hd + 1],
                                                       in1=acc, op0=ALU.mult, op1=ALU.add)\
                            .then_inc(S("idx_acc"), 1)
                    dve.wait_ge(S("idx_acc"), v + 1)
            nc.vector.tensor_copy(PENAL[:, 0, 0:P], LIMIT).then_inc(S("penal"), 1)
            link(dve, nc.vector.tensor_copy(LIMIT_BF, LIMIT))
            nc.vector.tensor_copy(IDENT_BF, ident).then_inc(S("masks"), 1)

            def select(r):
                n = r // 16 + 1
                w, acc = (n + 1) * P, ACC[n]
                if r % 16 == 0:
                    link(dve, nc.vector.tensor_tensor(acc[:, n * P:w], acc[:, n * P:w], LIMIT, ALU.add))
                link(dve, nc.vector.max(out=TOP, in_=acc))
                link(dve, nc.vector.match_replace(out=acc, in_to_replace=TOP, in_values=acc, imm_value=TAKEN))
                if r % 16 == 15:
                    nc.vector.tensor_scalar(PENAL[:, n, 0:w], acc, TAKEN / 1.5, -BIG, ALU.is_gt, ALU.mult)\
                        .then_inc(S("penal"), 1)
                    dve.wait_ge(S("penal"), n + 1)

            for q in range(4):
                r = 32 * q
                last = nc.vector.tensor_scalar(QCOL[r:r + 32, :, None],
                                               POS[r:r + 32, :].rearrange("p (c i) -> p c i", i=4)[:, :, q:q + 1],
                                               THRESHOLD[r:r + 32, :], None, ALU.add)
                link(dve, last)
            link(dve, nc.vector.tensor_tensor(DELTA, par("rel_at", 0, 8), par("rel_before", 0, 8), ALU.subtract))
            for j in range(4):
                at = MIX_AT["query_of_row"] + j * P
                for z in range(2):
                    delta = DELTA.rearrange("p (h z) -> p z h", z=2)[:, z:z + 1, :].to_broadcast([P, 16, 4])
                    link(dve, nc.vector.tensor_tensor(
                        TABLE[:, 64 * z:64 * z + 64].rearrange("p (q h) -> p q h", h=4), delta,
                        phase_const[:, at + 64 * z:at + 64 * z + 64].rearrange("p (q h) -> p q h", h=4), ALU.mult))
                link(dve, nc.vector.tensor_copy(table_hi[:, j, :], TABLE))
                last = nc.vector.tensor_tensor(table_lo[:, j, :], TABLE, table_hi[:, j, :].bitcast(F32),
                                               ALU.subtract)
                if j < 3:
                    link(dve, last)
            last.then_inc(S("tables"), 1)
            dve.wait_ge(S("tables"), 1)

            def steps(u):
                latent, n, m = unit(u)
                if latent:
                    return
                g = u - 32
                for j in range(4):
                    if j >= 2:
                        dve.wait_ge(S("steps_used"), 3 * g + j - 1)
                    elif g:
                        dve.wait_ge(S("att_scored"), u)
                    c = n * 32 + m * 4 + j
                    nc.vector.tensor_scalar(onehot[:, j % 2, 0:(n + 1) * P], POS[:, 0:(n + 1) * P], QCOL[:, c:c + 1],
                                            None, ALU.is_ge).then_inc(S("steps"), 1)

            def maxima(u):
                w = (unit(u)[1] + 1) * P
                dve.wait_ge(S("att_scored"), u + 1)
                if u >= 2:
                    dve.wait_ge(S("att_probs"), u - 1)
                st = ST[:, u % 2, :]
                link(dve, nc.vector.reduce_max(st[:, 0:1], ps[:, u % 2, 0:w], AXX))
                nc.vector.tensor_scalar(st[:, 1:2], st[:, 0:1], -MLA_SCALE if unit(u)[0] else -1.0, None, ALU.mult)\
                    .then_inc(S("att_max"), 1)

            maxima(0)
            for u in range(UNITS):
                w = (unit(u)[1] + 1) * P
                if u + 1 < UNITS:
                    steps(u + 1)
                dve.wait_ge(S("att_exp"), u + 1)
                st = ST[:, u % 2, :]
                link(dve, nc.vector.reciprocal(st[:, 3:4], st[:, 2:3]))
                nc.vector.tensor_scalar(PR[:, u % 2, 0:w], PR[:, u % 2, 0:w], st[:, 3:4], None, ALU.mult)\
                    .then_inc(S("att_probs"), 1)
                if u + 1 < UNITS:
                    maxima(u + 1)
                if u < 32:
                    for r in range(3 * u // 2, 3 * (u + 1) // 2):
                        select(r)
                if u and u % 8 == 0:
                    heads_low(dve, u // 8 - 1)
            heads_low(dve, 7)
            b = FIRST["mix_out"]
            with dve.Fori(0, 2) as i:
                for j in range(4):
                    c, bank = b + 3 * j, 4 * (j % 2)
                    for z in range(2):
                        dve.wait_ge(S("gate2"), i * 8 + (2 * j + z + 1))
                        dve.wait_ge(S("block_done"), num(c + 2, i * 3, 1))
                        nc.vector.tensor_tensor(PROD[:, j % 2, z, :], GATES[:, j % 2, z, :], ps[:, bank + 2 + z, :],
                                                ALU.mult).then_inc(S("gated2"), 1)
                    dve.wait_ge(S("gated2"), i * 8 + (2 * j + 2))
                    nc.vector.tensor_tensor(Y[:, bass.ds(i * 4 + j, 1), :], PROD[:, j % 2, 0:1, :],
                                            PROD[:, j % 2, 1:2, :], ALU.add).then_inc(S("bank_free"), 3)
                    dve.wait_ge(S("bank_free"), num(c, i * 3, 7))
            for k in range(KT):
                dve.wait_ge(S("y_hi"), k + 1)
                nc.vector.tensor_tensor(a_lo[:, k, :], Y[:, k, :], a_hi[:, k, :].bitcast(F32), ALU.subtract)\
                    .then_inc(S("y_lo"), 1)
            b = FIRST["w_out"]
            squares_begin(dve, 6)
            with dve.Fori(0, 2) as i:
                for j in range(4):
                    residual_dve(dve, b + j, i, i * 4 + j, mod_col(5, i * 4 + j))
                    dve.wait_ge(S("bank_free"), num(b + j, i, 5))
                    square_dve(dve, 6, i, j)

        def heads_low(dve, blk):
            dst, src = out_heads(blk)
            dve.wait_ge(S("att_hi"), blk + 1)
            nc.vector.tensor_tensor(dst(a_lo), src, dst(a_hi).bitcast(F32), ALU.subtract).then_inc(S("att_lo"), 1)

        block = ctx.enter_context(nc.Block())

        @block.sync
        def _(sp):
            for k in range(0, KT, 2):
                sp.dma_start(h[:, k:k + 2, :], dram["x"][:, k:k + 2, :]).then_inc(S(f"x_landed{k}"), 16)
            swa_sp(sp)
            ffn_sp(sp, "ffn0")
            gdn_sp(sp)
            ffn_sp(sp, "ffn1")
            ffn_sp(sp, "swi0")
            mix_sp(sp)
            ffn_sp(sp, "swi1")
            for k in range(KT):
                sp.wait_ge(S("final_ready"), k + 1)
                sp.dma_start(out[:, k, :], FINAL[:, k, :]).then_inc(S("stored"), 16)
            sp.wait_ge(S("stored"), 16 * KT)

        @block.gpsimd
        def _(pool):
            for s in range(RING):
                split_lo(pool, s)
            with pool.Fori(0, N_BLOCKS // RING - 1) as i:
                for s in range(RING):
                    split_lo(pool, RING + s, i)
            for s in range(N_BLOCKS % RING):
                split_lo(pool, N_BLOCKS // RING * RING + s)

        @block.scalar
        def _(act):
            act.dma_start(common[:, :], dram["common"]).then_inc(S("common_landed"), 16)
            act.dma_start(params[:, :], dram["params"]).then_inc(S("params_landed"), 16)
            act.dma_start(view(ROPE1_SCRATCH, T).bitcast(I32), dram["positions"]).then_inc(S("positions0"), 16)
            act.dma_start(phase_const[:, 0:640], dram["swa_const"]).then_inc(S("swa_const"), 16)
            act.wait_ge(S("common_landed"), 16)
            act.wait_ge(S("params_landed"), 16)
            split_hi(act, 0)
            split_hi(act, 1)
            split_hi(act, 2)
            norm_act(act, 0)
            rope_act(act, 0, COS1, SIN1)
            swa_act(act)
            act.wait_ge(S("sq_used"), 2)
            silu_row_load(act, 0)
            norm_act(act, 1)
            silu_row_act(act, 0)
            ffn_act(act, "ffn0", 0)
            norm_act(act, 2)
            gdn_act(act)
            act.wait_ge(S("sq_used"), 4)
            silu_row_load(act, 1)
            norm_act(act, 3)
            silu_row_act(act, 1)
            ffn_act(act, "ffn1", 1)
            norm_act(act, 4, lambda k: mod_col(0, k))
            act.dma_start(view(ROPE2_SCRATCH, T).bitcast(I32), dram["positions_2"]).then_inc(S("positions1"), 16)
            act.dma_start(phase_const[:, 0:MIX_W], dram["mix_const"]).then_inc(S("mix_const"), 16)
            ffn_act(act, "swi0", 0)
            norm_act(act, 5, lambda k: mod_col(3, k))
            mix_act(act)
            norm_act(act, 6, lambda k: mod_col(6, k))
            ffn_act(act, "swi1", 0)
            norm_act(act, 7)

        @block.vector
        def _(dve):
            for k in range(4):
                nc.vector.memset(gains[:, k:k + 1], 0.0).then_inc(S("bank_free"), 1)
            for k in range(2):
                nc.vector.memset(gains[:, 4 + k:5 + k], 0.0).then_inc(S("ada_free"), 1)
                nc.vector.memset(gains[:, 6 + k:7 + k], 0.0).then_inc(S("ada_kept"), 1)
            squares_begin(dve, 0)
            for k in range(KT):
                dve.wait_ge(S(f"x_landed{k // 2 * 2}"), 16)
                square_dve(dve, 0, 0, k)
            dve.wait_ge(S("common_landed"), 16)
            dve.wait_ge(S("params_landed"), 16)
            norm_dve(dve, 0, lambda k: par("mixer_norm", k))
            rope_dve(dve, 0, COS1, SIN1, ROPE1_SCRATCH)
            dve.wait_ge(S("swa_const"), 16)
            swa_dve(dve)
            norm_dve(dve, 1, lambda k: par("ffn_norm", k))
            ffn_dve(dve, "ffn0", 0, 2)
            ada_bias_dve(dve, 0)
            norm_dve(dve, 2, lambda k: par("mixer_norm", KT + k))
            gdn_dve(dve)
            norm_dve(dve, 3, lambda k: par("ffn_norm", KT + k))
            ffn_dve(dve, "ffn1", 1, 4)
            ada_bias_dve(dve, 1)
            modulation_dve(dve)
            norm_dve(dve, 4, lambda k: mod_col(0, k, gains), lambda k: mod_col(0, k))
            rope_dve(dve, 1, COS2, SIN2, ROPE2_SCRATCH)
            ffn_dve(dve, "swi0", 0, 5, lambda k: mod_col(2, k))
            norm_dve(dve, 5, lambda k: mod_col(1, k, gains), lambda k: mod_col(3, k))
            mix_dve(dve)
            norm_dve(dve, 6, lambda k: mod_col(2, k, gains), lambda k: mod_col(6, k))
            ffn_dve(dve, "swi1", 0, 7, lambda k: mod_col(8, k))
            final_dve(dve)

        @block.tensor
        def _(pe):
            pe.wait_ge(S("common_landed"), 16)
            norm_pe(pe, 0)
            swa_pe(pe)
            norm_pe(pe, 1)
            ffn_pe(pe, "ffn0", 1)
            norm_pe(pe, 2)
            gdn_pe(pe)
            norm_pe(pe, 3)
            ffn_pe(pe, "ffn1", 3)
            norm_pe(pe, 4)
            ffn_pe(pe, "swi0", 4)
            norm_pe(pe, 5)
            mix_pe(pe)
            norm_pe(pe, 6)
            ffn_pe(pe, "swi1", 6)
            norm_pe(pe, 7)


def blocks(w):
    k, n = w.shape
    return w.reshape(k // P, P, n // P, P).transpose(2, 1, 0, 3).reshape(n // P, P, k)


def ffn_blocks(up, down, tiles):
    full, tail = [], []
    g, u = blocks(up[:, :tiles * P]), blocks(up[:, tiles * P:])
    for at in range(0, tiles, CH):
        m = min(CH, tiles - at)
        full.append(np.stack([g[at:at + m], u[at:at + m]], 1).reshape(2 * m, P, BW))
        (full if m == CH else tail).append(blocks(down[at * P:(at + m) * P]))
    return np.concatenate(full), (np.concatenate(tail) if tail else None)


def columns(*vectors):
    return np.concatenate([np.ascontiguousarray(v).reshape(-1, P).T for v in vectors], 1)


def rows_for_all(v):
    return np.broadcast_to(np.asarray(v).reshape(1, -1), (P, np.asarray(v).size))


def rotation(half, dim):
    m = np.zeros((P, P), np.float32)
    for at in range(0, P, dim):
        for d in range(half):
            m[at + d + half, at + d] = -1.0
            m[at + d, at + d + half] = 1.0
    return m


def frequencies(half, dim, theta):
    d = np.arange(P) % dim
    f = theta ** (-(d % half) / half)
    return np.where(d < 2 * half, f, 0.0).astype(np.float32)[:, None]


def shape_constants():
    r = np.arange(P)
    common = np.concatenate([
        np.eye(P), np.ones((P, P)), np.kron(np.eye(2), np.ones((64, 64))),
        frequencies(ROPE1_HALF, 64, ROPE1_THETA), frequencies(ROPE2_HALF, 32, ROPE2_THETA), np.full((P, 1), EPS),
    ], 1)
    q, k = r[:, None], np.arange(256)[None, :]
    dist = q + P - k
    seen = (dist >= 0) & (dist < P)
    mask = np.where(seen, 0.0, -BIG)
    first = np.where(seen & (k >= P), 0.0, -BIG)
    swa = np.concatenate([rotation(ROPE1_HALF, 64), mask, first], 1)
    same = (r[:, None] // 64) == (r[None, :] // 64)
    before = same & (r[:, None] <= r[None, :])
    levels = []
    for lv in range(6):
        s, c = r[:, None] >> lv, r[None, :] >> lv
        levels.append((s // 2 == c // 2) & (c % 2 == 1) & (s % 2 == 0))
    gdn = np.concatenate([
        before, np.broadcast_to(q < 64, (P, P)), np.broadcast_to(q >= 64, (P, P)),
        np.where(before, 0.0, -BIG)] + levels, 1)
    limit = np.where((q < 64) & (r[None, :] >= 64), -BIG, 0.0)
    large = [max(8, math.ceil(8 * 16.0 ** (m / 8) - 1e-9)) for m in range(8)]
    lows = list(range(1, 8)) + large
    thr = [-1e9] + [-(lows[b] - 1) for b in range(14, -1, -1)] + [lows[b] for b in range(15)] + [1e9]
    of_row = (np.arange(P)[None, :] // 4 % 16)
    query = np.concatenate([of_row == 4 * i + (r[:, None] // 32) for i in range(4)], 1)
    mix = np.concatenate([rotation(ROPE2_HALF, 32), limit, query], 1)
    common = np.concatenate([common, np.tile(np.array(thr), 4)[:, None]], 1)
    rep = np.concatenate([r[:, None] == 16 * s + of_row for s in range(8)], 1)
    f = np.float32
    rep = (rep.astype(f).view(np.uint32) >> 16).astype(np.uint16).view(f)
    return common.astype(f), swa.astype(f), gdn.astype(f), mix.astype(f), rep


def kernel(**inp):
    import concourse.bacc as bacc
    from concourse.bass_utils import run_bass_kernel_spmd as run

    nc, arrays, dram, out = prepare(bacc, inp)
    build(nc, dram, out)
    r = run(nc, [arrays], core_ids=[0])
    got = r.results[0]["out_dram"]
    return np.ascontiguousarray(got.reshape(P, KT, T).transpose(2, 1, 0)).reshape(1, T, D)


def prepare(bacc, inp):
    inp = {k: np.asarray(v) for k, v in inp.items()}
    f = np.float32
    arrays = {}
    arrays["x"] = inp["x"][0].T.reshape(KT, P, T).transpose(1, 0, 2)
    arrays["positions"] = rows_for_all(inp["positions"][0]).astype(np.int32)
    arrays["positions_2"] = rows_for_all(inp["positions_2"][0]).astype(np.int32)
    common, swa, gdn, mix, rep = shape_constants()
    arrays["common"], arrays["swa_const"], arrays["gdn_const"], arrays["mix_const"] = common, swa, gdn, mix
    arrays["rep_const"] = rep

    w = inp["attn_w_in"][0]
    q = w[:, :1024].reshape(D, 2, 2, 4, 64).transpose(0, 1, 3, 2, 4).reshape(D, 1024)
    v = w[:, 1280:].reshape(2, 4, P, 256).transpose(0, 2, 1, 3).reshape(2, P, BW)
    arrays["qkv"] = np.concatenate([blocks(q), blocks(w[:, 1024:1280]), v])
    w = inp["attn_w_out"][0].reshape(4, 2, 2, 64, D).transpose(0, 2, 1, 3, 4).reshape(D, D)
    arrays["attn_out"] = blocks(w)
    for n in range(2):
        arrays[f"ffn{n}"], _ = ffn_blocks(inp["ffn_w_up"][n], inp["ffn_w_down"][n], FFN_TILES)
        k = n + 1
        arrays[f"swi{n}"], arrays[f"swi{n}_tail"] = ffn_blocks(
            inp[f"w_ffn{k}_in_2"][0], inp[f"w_ffn{k}_down_2"][0], SWI_TILES)
    arrays["ada"] = inp["w_ada_2"][0].T.reshape(N_ADA, P, D)
    arrays["c_row"] = rows_for_all(inp["c_2"][0])

    gdn_layout(inp, arrays)
    mix_layout(inp, arrays)

    taps = inp["gdn_conv"][0]
    order = gdn_order()[:, :8].reshape(-1)
    conv = [taps[j].reshape(-1, P)[order] for j in range(4)]
    seg = [15 - s if s < 16 else s + 1 for s in range(31)]
    rel = inp["rel_bias_2"]
    rel_at = np.concatenate([rel[seg], np.zeros((1, 8), f)])
    rel_before = np.concatenate([np.zeros((1, 8), f), rel[seg[:-1]], np.zeros((1, 8), f)])
    packed = {
        "mixer_norm": columns(*inp["mixer_norm"]), "ffn_norm": columns(*inp["ffn_norm"]),
        "ffn_conv": columns(*inp["ffn_conv"].reshape(6, -1)), "ffn_conv_b": columns(*inp["ffn_conv_b"]),
        "g_ffn1": columns(inp["g_ffn1_2"]), "g_mix": columns(inp["g_mix_2"]), "g_ffn2": columns(inp["g_ffn2_2"]),
        "g_final": columns(inp["g_final_2"]), "b_ada": columns(inp["b_ada_2"]),
        "gdn_conv": columns(*conv), "gdn_norm": columns(inp["gdn_norm"]),
        "q_gain": columns(np.tile(inp["attn_q_gain"][0], 2)), "k_gain": columns(np.tile(inp["attn_k_gain"][0], 2)),
        "sinks": rows_for_all(inp["attn_sinks"][0]), "a_log": rows_for_all(inp["gdn_a_log"][0]),
        "dt_bias": rows_for_all(inp["gdn_dt_bias"][0]), "g_cq": columns(inp["g_cq_2"]),
        "g_ckv": columns(inp["g_ckv_2"]), "rel_at": np.tile(rel_at, (4, 1)), "rel_before": np.tile(rel_before, (4, 1)),
    }
    arrays["params"] = np.concatenate([packed[n] for n, _ in PARAM_COLS], 1)

    nc = bacc.Bacc("TRN2", target_bir_lowering=False, num_devices=1)
    dram = {}
    maps = {}
    for name, a in arrays.items():
        a = np.ascontiguousarray(a)
        maps[f"{name}_dram"] = a
        dram[name] = nc.dram_tensor(f"{name}_dram", a.shape, mybir.dt.from_np(a.dtype), kind="ExternalInput").ap()
    out = nc.dram_tensor("out_dram", (P, KT, T), F32, kind="ExternalOutput").ap()
    return nc, maps, dram, out


def gdn_order():
    return np.array([[2 * r, 2 * r + 1, 8 + 2 * r, 9 + 2 * r] + [16 + 4 * r + x for x in range(4)]
                     + [32 + 4 * r + x for x in range(4)] for r in range(4)])


def gdn_layout(inp, arrays):
    w = inp["gdn_w_in"][0]
    main, out = blocks(w[:, :6144]), inp["gdn_w_out"][0]
    order, outs = gdn_order(), []
    for r in range(4):
        outs.append(blocks(out[r * 512:(r + 1) * 512]).reshape(4, 2, P, 512).transpose(0, 2, 1, 3)
                    .reshape(4, P, BW))
    parts = [main[order[0]]]
    for r in range(4):
        parts += [main[order[r + 1][:4]], outs[r], main[order[r + 1][4:]]] if r < 3 else [outs[r]]
    arrays["gdn"] = np.concatenate(parts)
    arrays["gdn_ba"] = w[:, 6144:].reshape(KT, P, 32).transpose(1, 0, 2).reshape(1, P, 256)


def mix_layout(inp, arrays):
    w = inp["w_in_2"][0]
    cuts = np.cumsum([0, 512, 64, 64, 512, 64, 8, 384, 256, 32, 1024, 1024])
    qa, ka, va, qi, ki, wi, cq, ckv, kr, ga, gb = [w[:, a:b] for a, b in zip(cuts[:-1], cuts[1:])]
    vw = np.concatenate([va, wi], 1)
    arrays["mix_v"] = vw.reshape(KT, P, 72).transpose(1, 0, 2).reshape(1, P, 576)
    arrays["mix_in"] = blocks(np.concatenate([qa, ka, ka, qi, ki, ki, cq, ckv, kr, kr, kr, kr], 1))
    uq = inp["w_uq_2"][0].reshape(384, 8, 96)
    uq = np.concatenate([uq[:, :, :64].reshape(384, 512), uq[:, :, 64:].reshape(384, 256)], 1)
    arrays["uq"] = blocks(uq).reshape(3, 2, P, 384).transpose(0, 2, 1, 3).reshape(3, P, 768)
    uk = blocks(inp["w_uk_2"][0]).reshape(1, 4, P, 256).transpose(0, 2, 1, 3).reshape(1, P, BW)
    uv = inp["w_uv_2"][0].reshape(2, P, 512).transpose(1, 0, 2).reshape(1, P, BW)
    arrays["ukv"] = np.concatenate([uk, uv])
    oa, ob = blocks(inp["w_o_a_2"][0]), blocks(inp["w_o_b_2"][0])
    arrays["mix_out"] = np.stack([blocks(ga), blocks(gb), np.concatenate([oa, ob], 2)], 1).reshape(24, P, BW)
    arrays["w_out"] = blocks(inp["w_out_2"][0])
```
